# Optimizing a Trainium2 kernel written in Bass

```python
import jax, jax.numpy as jnp
from jax import lax
import numpy as np

D_MODEL = 2048
BATCH = 1
SEQ = 512
DEPTH = 1
DEC_BATCH = 8
DEC_SEQ = 1
PAST_LEN = 2048
PAGE_SIZE = 128

WINDOWS = (128, 512, 2048)
DILATIONS = (1, 4, 16)
N_GROUPS = 3
A_HEADS = 8
A_HEAD_DIM = 128
A_QKV = N_GROUPS * A_HEADS * A_HEAD_DIM
A_WIDTH = A_HEADS * A_HEAD_DIM
R_HEADS = 8
R_KEY_DIM = 256
R_VAL_DIM = 256
R_QK = R_HEADS * R_KEY_DIM
R_WIDTH = R_HEADS * R_VAL_DIM
R_CHUNK = 128
PLE_DIM = 256
EPS = 1e-6
SPLITS = (A_QKV, A_QKV, A_QKV, A_WIDTH, R_QK, R_QK, R_WIDTH, R_WIDTH, D_MODEL, D_MODEL)
N_IN = 3 * A_QKV + A_WIDTH + 2 * R_QK + 2 * R_WIDTH + 2 * D_MODEL

kernel_name = 'hybrid_dilated_attn_retention_step'

def rms_norm(x, g):
    xf = x.astype(jnp.float32)
    y = xf * lax.rsqrt(jnp.mean(xf * xf, axis=-1, keepdims=True) + EPS)
    return (y * g.astype(jnp.float32)).astype(x.dtype)

def alibi_slopes():
    n = N_GROUPS * A_HEADS
    return jnp.exp2(-8.0 * (jnp.arange(n, dtype=jnp.float32) + 1.0) / n).reshape(N_GROUPS, A_HEADS)

def retention_log_decay():
    return jnp.log1p(-jnp.exp2(-5.0 - jnp.arange(R_HEADS, dtype=jnp.float32)))

def dilated_band(q, k, v, dil, window, slope):
    B, T, H, hd = q.shape
    L = window // dil
    n = T // dil
    n_pad = -(-n // L) * L
    nb = n_pad // L
    Bd = B * dil

    def to_sub(x):
        x = x.reshape(B, n, dil, H, hd).transpose(0, 2, 1, 3, 4).reshape(Bd, n, H, hd)
        x = jnp.pad(x, ((0, 0), (0, n_pad - n), (0, 0), (0, 0)))
        return x.reshape(Bd, nb, L, H, hd)

    def with_prev(x):
        prev = jnp.pad(x[:, :-1], ((0, 0), (1, 0), (0, 0), (0, 0), (0, 0)))
        return jnp.concatenate([prev, x], axis=2)

    qb = to_sub(q)
    kc = with_prev(to_sub(k))
    vc = with_prev(to_sub(v))
    s = jnp.einsum('bnqhd,bnkhd->bnhqk', qb, kc).astype(jnp.float32)
    qi = jnp.arange(L)
    kj = jnp.arange(2 * L)
    dist = qi[:, None] + L - kj[None, :]
    valid = (dist >= 0) & (dist <= L)
    valid = valid[None] & ~((jnp.arange(nb)[:, None, None] == 0) & (kj[None, None, :] < L))
    bias = -slope[:, None, None] * (dist * dil).astype(jnp.float32)[None]
    s = jnp.where(valid[None, :, None], s + bias[None, None], -jnp.inf)
    m = jnp.max(s, axis=-1, keepdims=True)
    e = jnp.exp(s - m)
    den = jnp.sum(e, axis=-1)
    o = jnp.einsum('bnhqk,bnkhd->bnqhd', e, vc.astype(jnp.float32))
    o = o / jnp.swapaxes(den, 2, 3)[..., None]
    lse = jnp.swapaxes(m[..., 0] + jnp.log(den), 2, 3)

    def from_sub(x):
        x = x.reshape((Bd, n_pad) + x.shape[3:])[:, :n]
        x = x.reshape((B, dil, n) + x.shape[2:])
        x = jnp.swapaxes(x, 1, 2)
        return x.reshape((B, T) + x.shape[3:])

    return from_sub(o), from_sub(lse)

def dilated_gather(q, k_all, v_all, past, dil, window, slope):
    S = q.shape[1]
    offs = jnp.arange(window // dil + 1) * dil
    idx = past + jnp.arange(S)[:, None] - offs[None, :]
    valid = idx >= 0
    idx = jnp.maximum(idx, 0)
    kg = k_all[:, idx]
    vg = v_all[:, idx]
    s = jnp.einsum('bshd,bskhd->bshk', q, kg).astype(jnp.float32)
    s = s - slope[:, None] * offs.astype(jnp.float32)[None, :]
    s = jnp.where(valid[None, :, None, :], s, -jnp.inf)
    m = jnp.max(s, axis=-1, keepdims=True)
    e = jnp.exp(s - m)
    den = jnp.sum(e, axis=-1)
    o = jnp.einsum('bshk,bskhd->bshd', e, vg.astype(jnp.float32)) / den[..., None]
    return o, m[..., 0] + jnp.log(den)

def combine_groups(outs, lses):
    o = jnp.stack(outs, axis=0)
    w = jax.nn.softmax(jnp.stack(lses, axis=0), axis=0)
    return jnp.sum(w[..., None] * o, axis=0)

def retention_chunkwise(q, k, v, state0, log_g):
    B, n, H, dk = q.shape
    dv = v.shape[-1]
    L = R_CHUNK if n % R_CHUNK == 0 else n
    nc = n // L

    def chunks(x):
        return x.astype(jnp.float32).reshape(B, nc, L, H, x.shape[-1]).transpose(1, 0, 2, 3, 4)

    qc, kc, vc = chunks(q), chunks(k), chunks(v)
    pos = jnp.arange(L, dtype=jnp.float32)
    rel = pos[:, None] - pos[None, :]
    intra = jnp.where(rel[None] >= 0, jnp.exp(jnp.maximum(rel, 0.0)[None] * log_g[:, None, None]), 0.0)
    q_decay = jnp.exp((pos[:, None] + 1.0) * log_g[None, :])
    k_decay = jnp.exp((L - 1.0 - pos)[:, None] * log_g[None, :])
    chunk_decay = jnp.exp(L * log_g)

    def step(R, xs):
        qi, ki, vi = xs
        scores = jnp.einsum('bihd,bjhd->bhij', qi, ki) * intra[None]
        inner = jnp.einsum('bhij,bjhe->bihe', scores, vi)
        cross = jnp.einsum('bihd,bhde->bihe', qi, R) * q_decay[None, :, :, None]
        R = R * chunk_decay[None, :, None, None] + jnp.einsum('bjhd,bjhe->bhde', ki * k_decay[None, :, :, None], vi)
        return R, inner + cross

    R, out = lax.scan(step, state0.astype(jnp.float32), (qc, kc, vc))
    out = out.transpose(1, 0, 2, 3, 4).reshape(B, n, H, dv)
    return out, R

def layer(h, p, win_caches, ret_state, g_pre, w_in, g_ret, w_a_out, w_r_out, w_o, g_post, w_ple_gate, w_ple_proj):
    B, S, _ = h.shape
    u = rms_norm(h, g_pre)
    z = jnp.einsum('bsd,de->bse', u, w_in)
    split_points = np.cumsum(np.array(SPLITS))[:-1].tolist()
    qa, ka, va, za, qr, kr, vr, zr, ga, gb = jnp.split(z, split_points, axis=-1)
    qa = qa.reshape(B, S, N_GROUPS, A_HEADS, A_HEAD_DIM) * (A_HEAD_DIM ** -0.5)
    ka = ka.reshape(B, S, N_GROUPS, A_HEADS, A_HEAD_DIM)
    va = va.reshape(B, S, N_GROUPS, A_HEADS, A_HEAD_DIM)
    qr = qr.reshape(B, S, R_HEADS, R_KEY_DIM)
    kr = kr.reshape(B, S, R_HEADS, R_KEY_DIM) * (R_KEY_DIM ** -0.5)
    vr = vr.reshape(B, S, R_HEADS, R_VAL_DIM)

    slopes = alibi_slopes()
    outs, lses, new_win = [], [], []
    for g in range(N_GROUPS):
        q_g, k_g, v_g = qa[:, :, g], ka[:, :, g], va[:, :, g]
        if win_caches is None:
            o, l = dilated_band(q_g, k_g, v_g, DILATIONS[g], WINDOWS[g], slopes[g])
            keep = min(WINDOWS[g], S)
            new_win.append(jnp.stack([k_g[:, S - keep:], v_g[:, S - keep:]], axis=2))
        else:
            buf = win_caches[g]
            past = buf.shape[1]
            full = jnp.concatenate([buf, jnp.stack([k_g, v_g], axis=2).astype(buf.dtype)], axis=1)
            o, l = dilated_gather(q_g, full[:, :, 0], full[:, :, 1], past, DILATIONS[g], WINDOWS[g], slopes[g])
            new_win.append(full[:, S:])
        outs.append(o)
        lses.append(l)
    ya = combine_groups(outs, lses).reshape(B, S, A_WIDTH).astype(h.dtype) * jax.nn.silu(za)

    if ret_state is None:
        ret_state = jnp.zeros((B, R_HEADS, R_KEY_DIM, R_VAL_DIM), jnp.float32)
    yr, r_new = retention_chunkwise(qr, kr, vr, ret_state, retention_log_decay())
    yr = yr * lax.rsqrt(jnp.mean(yr * yr, axis=-1, keepdims=True) + EPS)
    yr = (yr.reshape(B, S, R_WIDTH) * g_ret.astype(jnp.float32)).astype(h.dtype) * jax.nn.silu(zr)

    merged = (jax.nn.sigmoid(ga) * jnp.einsum('bse,ed->bsd', ya, w_a_out)
              + jax.nn.sigmoid(gb) * jnp.einsum('bse,ed->bsd', yr, w_r_out))
    y = jnp.einsum('bsd,de->bse', merged, w_o)
    h = h + rms_norm(y, g_post)
    h = h + jax.nn.sigmoid(jnp.einsum('bsd,de->bse', h, w_ple_gate)) * jnp.einsum('bsp,pd->bsd', p, w_ple_proj)
    return h, new_win, r_new

def setup_inputs(seed: int = 0) -> dict:
    key = jax.random.key(seed)
    ks = jax.random.split(key, 20)
    f32 = jnp.float32

    def nrm(k, shape, scale):
        return scale * jax.random.normal(k, shape, f32)

    def win_shape(w):
        return (DEPTH, DEC_BATCH, min(w, PAST_LEN), 2, A_HEADS, A_HEAD_DIM)

    return {
        'x_prompt': nrm(ks[0], (BATCH, SEQ, D_MODEL), 1.0),
        'x_sample': nrm(ks[1], (DEC_BATCH, DEC_SEQ, D_MODEL), 1.0),
        'cache_win0': nrm(ks[2], win_shape(WINDOWS[0]), 1.0),
        'cache_win1': nrm(ks[3], win_shape(WINDOWS[1]), 1.0),
        'cache_win2': nrm(ks[4], win_shape(WINDOWS[2]), 1.0),
        'state_ret': nrm(ks[5], (DEPTH, DEC_BATCH, R_HEADS, R_KEY_DIM, R_VAL_DIM), 0.25),
        'p_prompt': nrm(ks[6], (DEPTH, BATCH, SEQ, PLE_DIM), 1.0),
        'p_sample': nrm(ks[7], (DEPTH, DEC_BATCH, DEC_SEQ, PLE_DIM), 1.0),
        'g_pre': 1.0 + nrm(ks[8], (DEPTH, D_MODEL), 0.02),
        'w_in': nrm(ks[9], (DEPTH, D_MODEL, N_IN), D_MODEL ** -0.5),
        'g_ret': 1.0 + nrm(ks[10], (DEPTH, R_WIDTH), 0.02),
        'w_a_out': nrm(ks[11], (DEPTH, A_WIDTH, D_MODEL), A_WIDTH ** -0.5),
        'w_r_out': nrm(ks[12], (DEPTH, R_WIDTH, D_MODEL), R_WIDTH ** -0.5),
        'w_o': nrm(ks[13], (DEPTH, D_MODEL, D_MODEL), D_MODEL ** -0.5),
        'g_post': 1.0 + nrm(ks[14], (DEPTH, D_MODEL), 0.02),
        'w_ple_gate': nrm(ks[15], (DEPTH, D_MODEL, D_MODEL), D_MODEL ** -0.5),
        'w_ple_proj': nrm(ks[16], (DEPTH, PLE_DIM, D_MODEL), PLE_DIM ** -0.5),
    }

def reference(x_prompt, x_sample, cache_win0, cache_win1, cache_win2, state_ret, p_prompt, p_sample,
              g_pre, w_in, g_ret, w_a_out, w_r_out, w_o, g_post, w_ple_gate, w_ple_proj):
    hp = x_prompt
    hs = x_sample
    wp = [[] for _ in range(N_GROUPS)]
    ws = [[] for _ in range(N_GROUPS)]
    rp, rs = [], []
    for i in range(DEPTH):
        weights = (g_pre[i], w_in[i], g_ret[i], w_a_out[i], w_r_out[i], w_o[i], g_post[i], w_ple_gate[i], w_ple_proj[i])
        hp, nwp, nrp = layer(hp, p_prompt[i], None, None, *weights)
        hs, nws, nrs = layer(hs, p_sample[i], (cache_win0[i], cache_win1[i], cache_win2[i]), state_ret[i], *weights)
        for g in range(N_GROUPS):
            wp[g].append(nwp[g])
            ws[g].append(nws[g])
        rp.append(nrp)
        rs.append(nrs)
    y_prompt = hp
    y_sample = hs
    win0_prompt = jnp.stack(wp[0])
    win1_prompt = jnp.stack(wp[1])
    win2_prompt = jnp.stack(wp[2])
    ret_prompt = jnp.stack(rp)
    win0_sample = jnp.stack(ws[0])
    win1_sample = jnp.stack(ws[1])
    win2_sample = jnp.stack(ws[2])
    ret_sample = jnp.stack(rs)
    return (y_prompt, y_sample, win0_prompt, win1_prompt, win2_prompt, ret_prompt,
            win0_sample, win1_sample, win2_sample, ret_sample)


_drawn_inputs = setup_inputs


def setup_inputs(seed=0):
    import zlib

    import numpy as np

    out = dict(_drawn_inputs(seed))
    spreads = {}
    factors = {}
    for name, (base, spread) in spreads.items():
        noise = np.random.default_rng([zlib.crc32(name.encode()), seed]).standard_normal(out[name].shape)
        drawn = base * np.exp(spread * noise) if base else spread * noise
        out[name] = __import__('jax').numpy.asarray(drawn.astype(out[name].dtype))
    for name, factor in factors.items():
        out[name] = (out[name] * factor).astype(out[name].dtype)
    return out
```

```python
from contextlib import contextmanager, ExitStack

import numpy as np

import concourse.bass as bass
from concourse import mybir
from concourse.alu_op_type import AluOpType as ALU

F32 = mybir.dt.float32
F32R = mybir.dt.float32r
ACT = mybir.ActivationFunctionType
AX = mybir.AxisListType

P = 128
D = 2048
KD = D // P
T = 512
TB = T // P
NS = 8
TC = T + NS
HC = TC // 2
H = 8
G = 3
HD = 128
DIL = (1, 4, 16)
WIN = (128, 512, 2048)
NK = 128
RK = 256
PLE = 256
EPS = 1e-6
QA, KA, VA, ZA = 0, 3072, 6144, 9216
QR, KR, VR, ZR = 10240, 12288, 14336, 16384
GA, GB = 18432, 20480
N_IN = 22528
ZT = GA // P
NYT = H + 2 * H
ROW = 2 * H * HD
BIG = 1e30


def slopes():
    n = G * H
    return 2.0 ** (-8.0 * (np.arange(n) + 1.0) / n)


def log_decay():
    return np.log1p(-(2.0 ** (-5.0 - np.arange(H))))


def score_width(b):
    w0 = P * min(b + 1, 2)
    return w0, w0 + 2 * P * (b + 1)


class Tally:

    def __init__(self, start=0, unit=1):
        self.base, self.unit, self.local, self.i, self.rate = start, unit, 0, None, 0

    def next(self, skip=0):
        self.local += 1 + skip
        n = self.base + self.local
        return self.unit * n if self.i is None else self.unit * (self.i * self.rate + n)

    def enter(self, i, rate, first):
        self.base, self.local, self.rate = self.base + self.local - first * rate, 0, rate
        self.i = i

    def leave(self, n, first, name):
        assert self.local == self.rate, (name, self.local, self.rate)
        self.base, self.local, self.i = self.base + (n + first) * self.rate, 0, None


def build(nc, x_prompt, x_sample, cache0, cache1, cache2, state, p_prompt, p_sample, g_pre, w_in, g_ret,
          w_a, w_r, w_o, g_post, w_gate, w_proj,
          c_ident, c_dist, c_slope, c_decay, c_kdec, c_bias,
          y_prompt, y_sample, win0p, win1p, win2p, ret_p, win0s, win1s, win2s, ret_s):
    stack = ExitStack()
    caches, winp, wins = (cache0, cache1, cache2), (win0p, win1p, win2p), (win0s, win1s, win2s)
    gamma = [float(np.float32(g)) for g in np.exp(log_decay())]

    def dram(name, shape):
        return nc.dram_tensor(name, shape, F32, kind="Internal").ap()

    xt_scr = dram("xt_scr", [KD, P, TC])
    sg_scr = dram("sg_scr", [2, KD, P, TC])
    y_scr = dram("y_scr", [NYT, P, T])
    row_scr = dram("row_scr", [9, 64, HD])
    vrow_scr = dram("vrow_scr", [P, P])

    def sem(name):
        return stack.enter_context(nc.semaphore(name))

    U = stack.enter_context(nc.sbuf_tensor("moving", [P, 2, KD + 2, TC], F32R))
    W = stack.enter_context(nc.sbuf_tensor("weights", [P, 2, 2, KD, P], F32R))
    raw = stack.enter_context(nc.sbuf_tensor("raw_weights", [P, 2, KD, P], F32))
    ident = stack.enter_context(nc.sbuf_tensor("ident", [P, P], F32))
    one = stack.enter_context(nc.sbuf_tensor("one", [P, P], F32))
    mean_rk = stack.enter_context(nc.sbuf_tensor("mean_rk", [P, P], F32))
    mean_d = stack.enter_context(nc.sbuf_tensor("mean_d", [P, P], F32))
    small = stack.enter_context(nc.sbuf_tensor("small", [P, 256], F32))
    zs = stack.enter_context(nc.sbuf_tensor("sampled", [P, ZT * NS], F32))
    POOL_F = (212863 - 107648 - 16384 - 4 * 512 - 1024 - 4608) // 64 * 16 - 16
    pool_f = stack.enter_context(nc.sbuf_tensor("stage_buffers", [P, POOL_F], F32))
    acc = stack.enter_context(nc.psum_tensor("acc", [P, 2, 2, 512], F32))
    aux = stack.enter_context(nc.psum_tensor("aux", [P, 4, 512], F32))

    gpre, gpost, gret = small[:, 0:16], small[:, 16:32], small[:, 32:48]
    nslope, kdec = small[:, 48:72], small[:, 72:104]
    negmax, den, rden = small[:, 104:108], small[:, 108:112], small[:, 112:116]
    selfs, eps = small[:, 116:119], small[:, 120:121]

    def carve():
        at = [0]

        def take(*shape):
            n = int(np.prod(shape))
            a = pool_f[:, at[0]:at[0] + n]
            at[0] += n
            assert at[0] <= POOL_F, (at[0], POOL_F)
            if len(shape) == 1:
                return a
            names = "abcd"[:len(shape)]
            spec = f"p ({' '.join(names)}) -> p {' '.join(names)}"
            return a.rearrange(spec, **dict(zip(names, shape)))
        return take

    t = carve()
    x_nat, xs_nat = t(TB, D), t(D)
    p_nat, ps_nat = t(TB, PLE), t(PLE)
    xT = t(KD, TC)
    t = carve()
    sq, rstd, utmp = t(2, TC), t(TC), t(2, TC)
    t = carve()
    sg_out = t(2, TC)
    t = carve()
    qT, kT, vT, silu_z = t(G, TC), t(G, TC), t(2, TC), t(1, TC)
    k_nat, v_nat = t(G, TB, P), t(G, TB, P)
    sc = [t(score_width(b)[1]) for b in range(TB)]
    PT = t(G, TB, T)
    ya_out = t(T)
    dist = t(256 + 512 + 512)
    t = carve()
    rq, rk, rv, rz = t(2, TC), t(2, TC), t(2, TC), t(2, TC)
    ks, vn = t(TB, RK), t(TB, RK)
    sm = [t(T - P * j) for j in range(TB)]
    rsq, rrs, yt, st = t(2, T), t(T), t(2, T), t(2, RK)
    decay = t(H, T)
    t = carve()
    ysmp = t(NYT, NS)
    s_k, s_q = t(2, G, H * HD), t(2, G, H * HD)
    scol, srow, sbias = t(G, 64), t(G, NK + 1), t(G, NK + 1)
    pcol, pdiag, oself, spv, rows, vrow = t(G, 64), t(G, 64), t(64), t(G, 64), t(9, HD), t(P)
    s_v = s_k
    t = carve()
    t(NYT, NS)
    r_st, r_v = t(2, H, 2, RK), t(2, H, RK)
    ysr, ssq, srs, yg = t(2 * H, NS), t(2 * H, NS), t(64), t(2 * H, NS)
    t = carve()
    t(NYT, NS)
    M, X = t(KD, TC), t(KD, TC)
    sg_in, tmp = t(2, TC), t(TC)
    y_in = X[:, 0:2, :]
    nsq, nrs = sg_in, tmp
    outT = M[:, 0:2, :]
    outS, sgt, onat = M[:, 2, 0:KD * NS], M[:, 3, :], M[:, 4:6, 0:T]
    etmp, osr = M[:, 6, :], M[:, 8:12, :]

    def sems(name, n):
        return [sem(f"{name}{i}") for i in range(n)]
    s_begun = sem("program_begun")
    s_pool_waits = sem("pool_waits")
    s_ident = sem("identity_loaded")
    s_const = sem("consts_loaded")
    s_xload = sems("x_loaded", 6)
    s_wload = sems("weights_loaded", 2)
    s_whi = sem("weights_hi")
    s_wready = sem("weights_ready")
    s_unit = sem("unit_done")
    s_accfree = sems("acc_free", 2)
    s_full = sems("aux_full", 4)
    s_free = sems("aux_free", 4)
    s_xt = sem("xT_ready")
    s_sq = sem("squares_ready")
    s_sqfree = sem("squares_read")
    s_std = sem("std_ready")
    s_u = sem("u_plain_ready")
    s_uhi = sem("moving_hi")
    s_mov = sem("moving_ready")
    s_xtst = sem("xT_stored")
    s_sg = sem("gate_ready")
    s_sgst = sem("gate_stored")
    s_sgfree = sems("gate_buffer_free", 2)
    s_zT = sem("head_tile_ready")
    s_z = sem("silu_z_ready")
    s_knat = sem("k_rows_ready")
    s_vnat = sem("v_rows_ready")
    s_kst = sem("k_rows_stored")
    s_vst = sem("v_rows_stored")
    s_kfree = sems("k_rows_free", 3)
    s_vfree = sems("v_rows_free", 3)
    s_max = sem("max_ready")
    s_exp = sem("exp_ready")
    s_prob = sem("probs_ready")
    s_ya = sem("y_tile_ready")
    s_yast = sem("y_tile_stored")
    s_yafree = sem("y_tile_free")
    s_dist = sem("dist_loaded")
    s_decay = sem("decay_loaded")
    s_ks = sem("scaled_k_ready")
    s_pt = sem("probs_turned")
    s_vn = sem("ret_v_rows_ready")
    s_sm = sem("decayed_scores_ready")
    s_rstd = sem("ret_std_ready")
    s_st = sem("state_ready")
    s_stst = sem("state_stored")
    s_stfree = sem("state_free")
    s_yt = sem("ret_y_ready")
    s_ytst = sem("ret_y_stored")
    s_ytfree = sem("ret_y_free")
    s_rows = sem("sample_rows_ready")
    s_rowst = sem("sample_rows_stored")
    s_newrow = sem("new_cache_rows_stored")
    s_sk = sems("sample_k_loaded", 2)
    s_skfree = sem("sample_k_read")
    s_self = sem("self_scores_ready")
    s_scol = sem("score_columns_ready")
    s_smax = sem("sample_max_ready")
    s_sexp = sem("sample_exp_ready")
    s_sprob = sem("sample_probs_ready")
    s_pcol = sem("prob_columns_ready")
    s_sv = sems("sample_v_loaded", 2)
    s_svfree = sem("sample_v_read")
    s_rst = sems("sample_state_loaded", 2)
    s_rgam = sem("sample_state_scaled")
    s_rnew = sem("sample_state_new")
    s_rnewst = sems("sample_state_stored", 2)
    s_rfree = sem("sample_state_read")
    s_ysr = sem("sample_ret_y_ready")
    s_ssq = sem("sample_squares_ready")
    s_sstd = sem("sample_std_ready")
    s_ysmp = sem("sample_y_ready")
    s_sbias = sem("sample_bias_loaded")
    s_yin = sems("y_in_loaded", 2)
    s_yinfree = sem("y_in_read")
    s_sgin = sems("gate_in_loaded", 2)
    s_xin = sem("x_in_loaded")
    s_m = sem("merged_ready")
    s_h = sem("h_ready")
    s_sgt = sem("ple_gate_ready")
    s_out = sem("out_tile_ready")
    s_onat = sem("out_rows_ready")
    s_ost = sem("out_rows_stored")
    s_ofree = sems("out_rows_free", 2)
    s_os = sem("sample_out_ready")
    s_osrow = sem("sample_out_rows_ready")
    s_osst = sem("sample_out_stored")
    s_copy = sem("cache_rows_copied")

    BY16 = {id(s) for s in [s_const, s_dist, s_decay, s_xtst, s_yast, s_stst, s_ytst, s_rowst, s_xin,
                            s_sbias, s_sgst, s_kst, s_vst, s_ost, *s_xload, *s_wload, *s_sk, *s_sv, *s_rst,
                            *s_rnewst, *s_yin, *s_sgin]}

    class Waits:

        def __init__(self, e, ahead=False):
            self.e, self.t, self.ahead, self.starts = e, {}, ahead, {}

        def tally(self, s):
            if id(s) not in self.t:
                self.t[id(s)] = (Tally(self.starts.get(id(s), 0), 16 if id(s) in BY16 else 1), s)
            return self.t[id(s)][0]

        def due(self, s, skip=0):
            v = self.tally(s).next(skip)
            return self.e.to_reg(v) if self.ahead and not isinstance(v, int) else v

        def address(self, v, top):
            return self.e.snap(self.e.to_reg(v), min_val=0, max_val=top)

        def skip(self, s, n=1):
            self.tally(s).local += n

        @contextmanager
        def loop(self, n, rates, first=0):
            for s, _ in rates:
                self.tally(s)
            with self.e.Fori(first, first + n) as i:
                for s, r in rates:
                    self.tally(s).enter(i, r, first)
                yield i
                for s, r in rates:
                    self.tally(s).leave(n, first, s)

    def cols(i, n=P):
        return bass.ds(i, n)

    def halves(a):
        return a.rearrange("p (s c) -> p s c", s=2)

    def w_cols(w, col):
        return w.rearrange("(k p) c -> p k c", p=P)[:, :, bass.ds(col, P)]

    UNITS_ATT, UNITS_RET, UNITS_GATE = 10, 8, 4

    def att_cols(h):
        return [base + g * 1024 + h * P for base in (QA, KA, VA) for g in range(G)] + [ZA + h * P]

    def ret_cols(h):
        return [base + h * RK + j * P for base in (QR, KR, VR, ZR) for j in range(2)]

    def gate_cols(i):
        return [base + i * 2 * P + j * P for j in range(2) for base in (GA, GB)]

    def keep_rows(e, g, b, c):
        rows_kept = WIN[g] - 1
        chunk = {0: 1, 1: 4, 2: 16}[g]
        n = rows_kept * ROW // chunk
        src = caches[g][0].rearrange("b r k h d -> (b r k h d)")
        dst = wins[g][0].rearrange("b r k h d -> (b r k h d)")
        at = b * (WIN[g] * ROW) + c * n
        inner = n // P
        e.dma_start(dst[bass.ds(at, n)].rearrange("(p m n) -> p m n", p=16, n=inner),
                    src[bass.ds(at + ROW, n)].rearrange("(p m n) -> p m n", p=16, n=inner)).then_inc(s_copy, 16)
    N_COPIES = NS * (16 + 4 + 1)

    PT_BATCHES = {0: [(0, 3, 0, 1)], 1: [(0, 2, 0, 2), (2, 3, 0, 2)],
                  2: [(0, 1, 1, 3), (1, 2, 0, 3), (2, 3, 0, 3)],
                  3: [(0, 1, 2, 4), (1, 2, 0, 4), (2, 3, 0, 4)]}
    BATCHES = [(b, *q) for b in range(TB) for q in PT_BATCHES[b]]

    def prob_col(b, g, kb):
        w0, w = score_width(b)
        if g == 0:
            return (kb - max(b - 1, 0)) * P
        return w0 + (g - 1) * P * (b + 1) + kb * P

    block = stack.enter_context(nc.Block())

    @block.sync
    def _(sp):
        count = Waits(sp, ahead=True)
        for tb in range(TB):
            sp.dma_start(x_nat[:, tb, :], x_prompt[0, tb * P:(tb + 1) * P, :]).then_inc(s_xload[tb], 16)
            if tb == 0:
                sp.dma_start(ident[:], c_ident).then_inc(s_ident, 16)
        sp.dma_start(xs_nat[0:NS, :], x_sample[:, 0, :]).then_inc(s_xload[4], 16)
        sp.dma_start(p_nat, p_prompt[0, 0].rearrange("(t p) c -> p t c", p=P)).then_inc(s_xload[5], 16)
        sp.dma_start(ps_nat[0:NS, :], p_sample[0, :, 0, :]).then_inc(s_xload[5], 16)

        def load(slot, w, col, k=KD):
            v, col = count.due(s_wready), count.address(col, w.shape[1] - P)
            sp.wait_ge(s_begun, 1)
            sp.wait_ge(s_wready, v)
            sp.dma_start(raw[:, slot, 0:k, :], w_cols(w, col)).then_inc(s_wload[slot], 16)

        w0 = w_in[0]
        with count.loop(H, [(s_wready, UNITS_GATE)]) as i:
            for j, c in enumerate(gate_cols(i)):
                load(j % 2, w0, c)
                if j < 2:
                    keep_rows(sp, 1, i, j)
                if j == 2:
                    keep_rows(sp, 0, i, 0)
        sp.wait_ge(s_xtst, 16 * KD)
        sp.dma_start(dist, c_dist).then_inc(s_dist, 16)
        with count.loop(H, [(s_wready, UNITS_ATT)]) as h:
            for j, c in enumerate(att_cols(h)):
                load(j % 2, w0, c)
                keep_rows(sp, 2, h, j)
        with count.loop(H, [(s_wready, UNITS_RET)]) as h:
            for j, c in enumerate(ret_cols(h)):
                load(j % 2, w0, c)
                if j < 6:
                    keep_rows(sp, 2, h, 10 + j)
                else:
                    keep_rows(sp, 1, h, j - 4)
        with count.loop(KD // 2, [(s_wready, 2)]) as i:
            for j in range(2):
                load(j, w_a[0], i * 2 * P + j * P, H)
        with count.loop(KD // 2, [(s_wready, 2)]) as i:
            for j in range(2):
                load(j, w_r[0], i * 2 * P + j * P)
        with count.loop(KD // 2, [(s_wready, 2)]) as i:
            for j in range(2):
                load(j, w_o[0], i * 2 * P + j * P)
        with count.loop(KD, [(s_wready, 2)]) as i:
            load(0, w_proj[0], i * P, 2)
            load(1, w_gate[0], i * P)
        sp.wait_ge(s_copy, 16 * N_COPIES)

    @block.tensor
    def _(pe):
        count = Waits(pe)
        count.starts[id(s_wready)] = 2
        halfcols = [(0, HC), (HC, TC)]

        def unit(par, k_tiles=KD, first_tile=0, hooks=None):
            pe.wait_ge(s_wready, count.due(s_wready))
            pe.wait_ge(s_accfree[par], count.due(s_accfree[par]))
            passes = [(0, 0), (0, 1), (1, 0)]
            for k in range(k_tiles):
                for f in (hooks or {}).get(k, ()):
                    f()
                for n, (wp, up) in enumerate(passes):
                    for half, (a, b) in enumerate(halfcols):
                        mm = pe.matmul(acc[:, par, half, 0:HC], W[:, par, wp, k, :], U[:, up, first_tile + k, a:b],
                                       start=(k == 0 and n == 0), stop=(k == k_tiles - 1 and n == 2))
            mm.then_inc(s_unit, 1)

        pe.wait_ge(s_ident, 16)
        fill = 0
        for tb in range(TB):
            pe.wait_ge(s_xload[tb], count.due(s_xload[tb]))
            for n0 in range(0, KD, 4):
                pe.wait_ge(s_free[fill % 4], count.due(s_free[fill % 4]))
                for n in range(4):
                    mm = pe.transpose(aux[:, fill % 4, n * P:(n + 1) * P],
                                      x_nat[:, tb, (n0 + n) * P:(n0 + n + 1) * P], ident[:])
                mm.then_inc(s_full[fill % 4], 1)
                fill += 1
        pe.wait_ge(s_xload[4], count.due(s_xload[4]))
        pe.wait_ge(s_free[0], count.due(s_free[0]))
        for n in range(KD):
            mm = pe.transpose(aux[:, 0, n * NS:(n + 1) * NS], xs_nat[0:NS, n * P:(n + 1) * P], ident[0:NS, 0:NS])
        mm.then_inc(s_full[0], 1)
        pe.wait_ge(s_xload[5], count.due(s_xload[5], skip=1))
        for j in range(2):
            pe.wait_ge(s_free[1 + j], count.due(s_free[1 + j]))
            for tb in range(TB):
                mm = pe.transpose(aux[:, 1 + j, tb * P:(tb + 1) * P], p_nat[:, tb, j * P:(j + 1) * P], ident[:])
            mm.then_inc(s_full[1 + j], 1)
        pe.wait_ge(s_free[3], count.due(s_free[3]))
        for j in range(2):
            mm = pe.transpose(aux[:, 3, j * NS:(j + 1) * NS], ps_nat[0:NS, j * P:(j + 1) * P], ident[0:NS, 0:NS])
        mm.then_inc(s_full[3], 1)

        def norm_sums():
            pe.wait_ge(s_free[0], count.due(s_free[0]))
            pe.wait_ge(s_free[1], count.due(s_free[1]))
            for n in range(KD):
                pe.wait_ge(s_sq, count.due(s_sq))
                pe.matmul(aux[:, 0, 0:HC], mean_d[:], sq_now[:, n % 2, 0:HC], start=(n == 0), stop=(n == KD - 1))
                mm = pe.matmul(aux[:, 1, 0:HC], mean_d[:], sq_now[:, n % 2, HC:TC], start=(n == 0), stop=(n == KD - 1))
                mm.then_inc(s_sqfree if n < KD - 1 else s_full[0], 1)

        sq_now = sq
        norm_sums()
        pe.wait_ge(s_mov, count.due(s_mov, skip=KD - 1))

        with count.loop(H, [(s_wready, 4), (s_accfree[0], 2), (s_accfree[1], 2)]) as i:
            for j in range(UNITS_GATE):
                unit(j % 2)

        def head_rows(src, nth_skip, bank, ntb=TB):
            pe.wait_ge(s_zT, count.due(s_zT, nth_skip))
            pe.wait_ge(s_free[bank], count.due(s_free[bank]))
            for tb in range(ntb):
                mm = pe.transpose(aux[:, bank, tb * P:(tb + 1) * P], src[:, tb * P:(tb + 1) * P], ident[:])
            mm.then_inc(s_full[bank], 1)

        def scores(b):
            w0, w = score_width(b)
            wg = P * (b + 1)
            q = slice(b * P, (b + 1) * P)
            for g, (a, n) in enumerate([(max(b - 1, 0) * P, w0), (0, wg), (0, wg)]):
                pe.wait_ge(s_free[g], count.due(s_free[g]))
                pe.matmul(aux[:, g, 0:n], qT[:, g, q], kT[:, g, a:a + n], start=True, stop=True).then_inc(s_full[g], 1)

        def prob_turn(m):
            b, g0, g1, k0, k1 = BATCHES[m]
            if m == 0 or BATCHES[m - 1][0] != b:
                pe.wait_ge(s_prob, count.due(s_prob))
            pe.wait_ge(s_free[m % 3], count.due(s_free[m % 3]))
            at = 0
            for g in range(g0, g1):
                for kb in range(k0, k1):
                    c = prob_col(b, g, kb)
                    mm = pe.transpose(aux[:, m % 3, at:at + P], sc[b][:, c:c + P], ident[:])
                    at += P
            mm.then_inc(s_full[m % 3], 1)

        def values():
            pe.wait_ge(s_vnat, count.due(s_vnat, skip=2))
            pe.wait_ge(s_pt, count.due(s_pt, skip=len(BATCHES) - 1))
            pe.wait_ge(s_free[3], count.due(s_free[3]))
            parts = [(1, kb) for kb in range(TB)] + [(2, kb) for kb in range(TB)] + [(0, kb) for kb in range(TB)]
            for n, (g, kb) in enumerate(parts):
                a, z = kb * P, (min(kb + 2, TB) * P if g == 0 else T)
                mm = pe.matmul(aux[:, 3, a:z], v_nat[:, g, kb, :], PT[:, g, kb, a:z], start=(n == 0),
                               stop=(n == len(parts) - 1))
            mm.then_inc(s_full[3], 1)

        with count.loop(H, [(s_wready, 10), (s_accfree[0], 5), (s_accfree[1], 5), (s_zT, 9), (s_free[0], 7),
                        (s_free[1], 7), (s_free[2], 7), (s_free[3], 7), (s_prob, 4), (s_vnat, 3), (s_pt, 9)]) as h:
            hooks = {
                4: {8: [lambda: head_rows(kT[:, 0, :], 3, 3)]},
                5: {8: [lambda: head_rows(kT[:, 1, :], 0, 3)]},
                6: {2: [lambda: head_rows(kT[:, 2, :], 0, 3)], 4: [lambda: scores(0)], 8: [lambda: scores(1)],
                    12: [lambda: scores(2)]},
                7: {0: [lambda: scores(3)], 6: [lambda: head_rows(vT[:, 0, :], 0, 3)]},
                8: {2: [lambda: head_rows(vT[:, 1, :], 0, 3)], 6: [lambda: prob_turn(0)], 9: [lambda: prob_turn(1)],
                    12: [lambda: prob_turn(2)]},
                9: {0: [lambda: prob_turn(3)], 2: [lambda: head_rows(vT[:, 0, :], 0, 3)],
                    4: [lambda: prob_turn(4)], 6: [lambda: prob_turn(5)], 8: [lambda: prob_turn(6)],
                    10: [lambda: prob_turn(7)], 12: [lambda: prob_turn(8)], 15: [values]},
            }
            for j in range(UNITS_ATT):
                unit(j % 2, hooks=hooks.get(j))

        def ret_rows(src, j, nth_skip, bank):
            pe.wait_ge(s_zT, count.due(s_zT, nth_skip))
            pe.wait_ge(s_free[bank], count.due(s_free[bank]))
            for tb in range(TB):
                mm = pe.transpose(aux[:, bank, tb * P:(tb + 1) * P], src[:, j, tb * P:(tb + 1) * P], ident[:])
            mm.then_inc(s_full[bank], 1)

        def ret_scores(jb):
            bank = jb % 2
            pe.wait_ge(s_free[bank], count.due(s_free[bank]))
            for j in range(2):
                mm = pe.matmul(aux[:, bank, 0:T - jb * P], rk[:, j, jb * P:(jb + 1) * P], rq[:, j, jb * P:T],
                               start=(j == 0), stop=(j == 1))
            mm.then_inc(s_full[bank], 1)

        def ret_values(e):
            if e == 0:
                pe.wait_ge(s_sm, count.due(s_sm, skip=3))
                pe.wait_ge(s_vn, count.due(s_vn, skip=1))
            pe.wait_ge(s_free[2 + e], count.due(s_free[2 + e]))
            for jb in range(TB):
                mm = pe.matmul(aux[:, 2 + e, jb * P:T], vn[:, jb, e * P:(e + 1) * P], sm[jb], start=(jb == 0),
                               stop=(jb == TB - 1))
            mm.then_inc(s_full[2 + e], 1)

        def ret_state():
            pe.wait_ge(s_ks, count.due(s_ks, skip=1))
            pe.wait_ge(s_free[0], count.due(s_free[0]))
            for j in range(2):
                for jb in range(TB):
                    mm = pe.matmul(aux[:, 0, j * RK:(j + 1) * RK], ks[:, jb, j * P:(j + 1) * P], vn[:, jb, :],
                                   start=(jb == 0), stop=(jb == TB - 1))
            mm.then_inc(s_full[0], 1)

        def ret_norm():
            pe.wait_ge(s_sq, count.due(s_sq, skip=1))
            pe.wait_ge(s_free[1], count.due(s_free[1]))
            for e in range(2):
                mm = pe.matmul(aux[:, 1, :], mean_rk[:], rsq[:, e, :], start=(e == 0), stop=(e == 1))
            mm.then_inc(s_full[1], 1)

        with count.loop(H, [(s_wready, 8), (s_accfree[0], 4), (s_accfree[1], 4), (s_zT, 6), (s_free[0], 5),
                        (s_free[1], 5), (s_free[2], 1), (s_free[3], 1), (s_sm, 4), (s_vn, 2), (s_ks, 2),
                        (s_sq, 2)]) as h:
            hooks = {
                4: {4: [lambda: ret_rows(rk, 0, 2, 0)], 8: [lambda: ret_rows(rk, 1, 0, 1)]},
                5: {1: [lambda: ret_scores(0)], 5: [lambda: ret_scores(1)], 9: [lambda: ret_scores(2)],
                    13: [lambda: ret_scores(3)]},
                6: {2: [lambda: ret_rows(rv, 0, 0, 0)], 6: [lambda: ret_rows(rv, 1, 0, 1)]},
                7: {1: [lambda: ret_values(0)], 5: [lambda: ret_values(1)], 9: [ret_state], 13: [ret_norm]},
            }
            for j in range(UNITS_RET):
                unit(j % 2, hooks=hooks.get(j))

        def tiles64(first):
            return zs[:, first * NS:(first + H) * NS]

        for n in range(9):
            bank = n // 4
            if n % 4 == 0:
                pe.wait_ge(s_free[bank], count.due(s_free[bank]))
            mm = pe.transpose(aux[0:64, bank, (n % 4) * P:(n % 4 + 1) * P], tiles64(n * H), ident[:])
            if n % 4 == 3 or n == 8:
                mm.then_inc(s_full[bank], 1)
        pe.wait_ge(s_free[3], count.due(s_free[3]))
        pe.transpose(aux[:, 3, 0:P], zs[:, VR // P * NS:(VR // P + 16) * NS], ident[:]).then_inc(s_full[3], 1)
        pe.wait_ge(s_self, count.due(s_self))
        pe.wait_ge(s_free[3], count.due(s_free[3]))
        for g in range(G):
            mm = pe.matmul(aux[0:64, 3, g:g + 1], pcol[:, g, :], one[:, 0:1], start=True, stop=True)
        mm.then_inc(s_full[3], 1)
        pe.wait_ge(s_scol, count.due(s_scol))
        pe.wait_ge(s_free[0], count.due(s_free[0]))
        for g in range(G):
            mm = pe.transpose(aux[0:64, 0, g * P:(g + 1) * P], scol[:, g, :], ident[:])
        mm.then_inc(s_full[0], 1)
        pe.wait_ge(s_sprob, count.due(s_sprob))
        pe.wait_ge(s_free[1], count.due(s_free[1]))
        for g in range(G):
            mm = pe.transpose(aux[:, 1, g * 64:(g + 1) * 64], srow[0:64, g, 0:NK], ident[0:64, 0:64])
        mm.then_inc(s_full[1], 1)
        pe.wait_ge(s_free[2], count.due(s_free[2]))
        for g in range(G):
            mm = pe.matmul(aux[:, 2, g * 64:(g + 1) * 64], one[0:64, :], pdiag[0:64, g, :], start=True, stop=True)
        mm.then_inc(s_full[2], 1)
        pe.wait_ge(s_pcol, count.due(s_pcol))
        pe.wait_ge(s_free[3], count.due(s_free[3]))
        for b in range(NS):
            pe.wait_ge(s_sv[b % 2], 48 * (b // 2 + 1))
            for h in range(H):
                for g in range(G):
                    mm = pe.matmul(aux[:, 3, h * NS + b:h * NS + b + 1], s_v[:, b % 2, g, h * HD:(h + 1) * HD],
                                   pcol[:, g, h * NS + b:h * NS + b + 1], start=(g == 0), stop=(g == G - 1))
            mm.then_inc(s_svfree if b < NS - 1 else s_full[3], 1)

        for b in range(NS):
            pe.wait_ge(s_rnew, count.due(s_rnew))
            bank = b % 2
            pe.wait_ge(s_free[bank], count.due(s_free[bank]))
            for h in range(H):
                for e in range(2):
                    for j in range(2):
                        at = (QR // P + 2 * h + j) * NS + b
                        mm = pe.matmul(aux[:, bank, 2 * h + e:2 * h + e + 1], r_st[:, b % 2, h, j, e * P:(e + 1) * P],
                                       zs[:, at:at + 1], start=(j == 0), stop=(j == 1))
            mm.then_inc(s_full[bank], 1)
        pe.wait_ge(s_ssq, count.due(s_ssq))
        pe.wait_ge(s_free[2], count.due(s_free[2]))
        for e in range(2):
            mm = pe.matmul(aux[:, 2, 0:64], mean_rk[:], ssq[:, :, :].rearrange("p (h e) b -> p e h b", e=2)[:, e],
                           start=(e == 0), stop=(e == 1))
        mm.then_inc(s_full[2], 1)

        rates = [(s_wready, 2), (s_accfree[0], 1), (s_accfree[1], 1)]
        pe.wait_ge(s_mov, count.due(s_mov, skip=H - 1))
        with count.loop(KD // 2, rates) as i:
            for j in range(2):
                unit(j, H)
        pe.wait_ge(s_mov, count.due(s_mov, skip=KD - 1))
        with count.loop(KD // 2, rates) as i:
            for j in range(2):
                unit(j)
        pe.wait_ge(s_mov, count.due(s_mov, skip=KD - 1))
        with count.loop(KD // 2, rates) as i:
            for j in range(2):
                unit(j)
        sq_now = nsq
        norm_sums()
        pe.wait_ge(s_mov, count.due(s_mov, skip=KD - 1))

        def out_turn(slot):
            pe.wait_ge(s_out, count.due(s_out))
            pe.wait_ge(s_free[slot], count.due(s_free[slot]))
            for tb in range(TB):
                mm = pe.transpose(aux[:, slot, tb * P:(tb + 1) * P], outT[:, slot, tb * P:(tb + 1) * P], ident[:])
            mm.then_inc(s_full[slot], 1)

        def ple(first):
            for n in range(2):
                unit(0, 2, KD)
                unit(1, hooks=None if first and n == 0 else {8: [lambda: out_turn(1 - n)]})

        ple(True)
        with count.loop(KD // 2 - 1, [(s_wready, 4), (s_accfree[0], 2), (s_accfree[1], 2), (s_out, 2), (s_free[0], 1),
                                  (s_free[1], 1)], first=1) as i:
            ple(False)
        out_turn(1)
        pe.wait_ge(s_os, count.due(s_os))
        for n in range(KD):
            if n % 4 == 0:
                pe.wait_ge(s_free[n // 4], count.due(s_free[n // 4]))
            mm = pe.transpose(aux[0:NS, n // 4, (n % 4) * P:(n % 4 + 1) * P], outS[:, n * NS:(n + 1) * NS], ident[:])
            if n % 4 == 3:
                mm.then_inc(s_full[n // 4], 1)

    @block.scalar
    def _(act):
        count = Waits(act)

        def hi(par):
            act.wait_ge(s_wload[par], count.due(s_wload[par]))
            act.activation(W[:, par, 0], raw[:, par], ACT.Copy).then_inc(s_whi, 1)

        act.sem_inc(s_accfree[0], 1)
        act.sem_inc(s_accfree[1], 1)
        for b in range(4):
            act.sem_inc(s_free[b], 1)

        for tb in range(TB):
            for q in range(4):
                if q % 2 == 0:
                    act.wait_ge(s_full[q], count.due(s_full[q]))
                    act.activation(xT[:, 4 * q:4 * q + 4, tb * P:(tb + 1) * P],
                                   aux[:, q, :].rearrange("p (n c) -> p n c", n=4), ACT.Copy).then_inc(s_free[q], 1)
                else:
                    count.skip(s_full[q])
        act.wait_ge(s_full[0], count.due(s_full[0]))
        act.activation(xT[:, :, T:TC], aux[:, 0, 0:P].rearrange("p (n c) -> p n c", n=KD), ACT.Copy).then_inc(s_free[0], 1)
        for j in range(2):
            act.wait_ge(s_full[1 + j], count.due(s_full[1 + j]))
            act.activation(U[:, 0, KD + j, 0:T], aux[:, 1 + j, :], ACT.Copy).then_inc(s_uhi, 1)
        act.wait_ge(s_full[3], count.due(s_full[3]))
        act.activation(U[:, 0, KD:KD + 2, T:TC], aux[:, 3, 0:2 * NS].rearrange("p (n c) -> p n c", n=2),
                       ACT.Copy).then_inc(s_uhi, 1)
        act.drain().then_inc(s_xt, 1)
        hi(0)
        hi(1)

        def squares(src, dst):
            for n in range(KD):
                if n >= 2:
                    act.wait_ge(s_sqfree, count.due(s_sqfree))
                act.activation(dst[:, n % 2, :], src[:, n, :], ACT.Square).then_inc(s_sq, 1)
            count.skip(s_sqfree, 1)

        def std(dst):
            act.wait_ge(s_full[0], count.due(s_full[0]))
            act.activation(dst[:, 0:HC], aux[:, 0, 0:HC], ACT.Sqrt, bias=eps[:, 0:1]).then_inc(s_free[0], 1)
            act.activation(dst[:, HC:TC], aux[:, 1, 0:HC], ACT.Sqrt, bias=eps[:, 0:1]).then_inc(s_free[1], 1)
            act.drain().then_inc(s_std, 1)

        act.wait_ge(s_xt, count.due(s_xt, skip=1))
        squares(xT, sq)
        std(rstd)
        for n in range(KD):
            act.wait_ge(s_u, count.due(s_u))
            act.activation(U[:, 0, n, :], utmp[:, n % 2, :], ACT.Copy).then_inc(s_uhi, 1)

        with count.loop(H, [(s_unit, 4), (s_wload[0], 2), (s_wload[1], 2), (s_sgfree[0], 2), (s_sgfree[1], 2)]) as i:
            for j in range(UNITS_GATE):
                par = j % 2
                act.wait_ge(s_unit, count.due(s_unit))
                act.wait_ge(s_sgfree[par], count.due(s_sgfree[par]))
                act.activation(halves(sg_out[:, par, :]), acc[:, par, :, 0:HC], ACT.Sigmoid).then_inc(s_accfree[par], 1)
                act.drain().then_inc(s_sg, 1)
                hi(par)
        act.wait_ge(s_sgfree[0], count.due(s_sgfree[0]))
        act.wait_ge(s_sgfree[1], count.due(s_sgfree[1]))

        def head_tile(par, dst, tile, ready, func=ACT.Copy, scale=1.0):
            act.wait_ge(s_unit, count.due(s_unit))
            act.activation(halves(dst), acc[:, par, :, 0:HC], func, scale=scale).then_inc(ready, 1)
            act.activation(zs[:, bass.ds(tile * NS, NS)], acc[:, par, 1, HC - NS:HC], func,
                           scale=scale).then_inc(s_accfree[par], 1)

        def exps(b):
            act.wait_ge(s_max, count.due(s_max))
            act.activation(sc[b], sc[b], ACT.Exp, bias=negmax[:, b:b + 1], accum_out=den[:, b:b + 1]).then_inc(s_exp, 1)

        def prob_copy(m):
            b, g0, g1, k0, k1 = BATCHES[m]
            act.wait_ge(s_full[m % 3], count.due(s_full[m % 3]))
            ng, nk = g1 - g0, k1 - k0
            src = aux[:, m % 3, 0:ng * nk * P].rearrange("p (g k c) -> p g k c", g=ng, k=nk)
            act.activation(PT[:, g0:g1, k0:k1, b * P:(b + 1) * P], src, ACT.Copy).then_inc(s_free[m % 3], 1)
            act.drain().then_inc(s_pt, 1)

        with count.loop(H, [(s_unit, 10), (s_wload[0], 5), (s_wload[1], 5), (s_max, 4), (s_full[0], 7), (s_full[1], 7),
                        (s_full[2], 7), (s_full[3], 7)]) as h:
            for j in range(UNITS_ATT):
                par = j % 2
                if j == 6:
                    for b in range(3):
                        exps(b)
                if j == 7:
                    exps(3)
                    for g in range(G):
                        count.skip(s_full[g], 4)
                if j == 8:
                    for m in range(3):
                        prob_copy(m)
                if j == 9:
                    for m in range(3, 9):
                        prob_copy(m)
                    count.skip(s_full[3], 7)
                g = j % 3
                if j < 3:
                    head_tile(par, qT[:, g, :], QA // P + g * H + h, s_zT, scale=HD ** -0.5)
                elif j < 6:
                    head_tile(par, kT[:, g, :], KA // P + g * H + h, s_zT)
                elif j < 9:
                    head_tile(par, vT[:, g % 2, :], VA // P + g * H + h, s_zT)
                else:
                    head_tile(par, silu_z[:, 0, :], ZA // P + h, s_z, ACT.Silu)
                hi(par)

        with count.loop(H, [(s_unit, 8), (s_wload[0], 4), (s_wload[1], 4), (s_full[0], 5), (s_full[1], 5),
                        (s_full[2], 1), (s_full[3], 1)]) as h:
            for j in range(UNITS_RET):
                par = j % 2
                if j == 7:
                    for e in range(2):
                        act.wait_ge(s_full[2 + e], count.due(s_full[2 + e]))
                        act.activation(rsq[:, e, :], aux[:, 2 + e, :], ACT.Square).then_inc(s_sq, 1)
                    count.skip(s_full[0], 5)
                    act.wait_ge(s_full[1], count.due(s_full[1], skip=4))
                    act.activation(rrs, aux[:, 1, :], ACT.Sqrt, bias=eps[:, 0:1]).then_inc(s_free[1], 1)
                    act.drain().then_inc(s_rstd, 1)
                dst = (rq, rk, rv, rz)[j // 2][:, par, :]
                tile = (QR, KR, VR, ZR)[j // 2] // P + 2 * h + par
                if j < 6:
                    head_tile(par, dst, tile, s_zT, scale=RK ** -0.5 if j // 2 == 1 else 1.0)
                else:
                    head_tile(par, dst, tile, s_z, ACT.Silu)
                hi(par)

        count.skip(s_full[0], 1)
        count.skip(s_full[1], 1)
        count.skip(s_full[2], 1)
        count.skip(s_full[3], 2)
        count.skip(s_full[0], 1)
        act.wait_ge(s_smax, count.due(s_smax))
        act.activation(srow[0:64], srow[0:64], ACT.Exp, bias=negmax[0:64, 0:1], accum_out=den[0:64, 0:1]).then_inc(s_sexp, 1)
        count.skip(s_full[1], 1)
        count.skip(s_full[2], 1)
        count.skip(s_full[3], 1)
        for b in range(NS):
            act.wait_ge(s_rst[b % 2], 32 * (b // 2 + 1))
            for h in range(H):
                a = act.activation(r_st[:, b % 2, h], r_st[:, b % 2, h], ACT.Copy, scale=gamma[h])
            a.then_inc(s_rgam, 1)
        count.skip(s_full[0], 4)
        count.skip(s_full[1], 4)
        act.wait_ge(s_full[2], count.due(s_full[2]))
        act.activation(srs, aux[:, 2, 0:64], ACT.Sqrt, bias=eps[:, 0:1]).then_inc(s_free[2], 1)
        act.drain().then_inc(s_sstd, 1)

        def y_hi(first, n, slot):
            act.wait_ge(s_yin[slot], count.due(s_yin[slot]))
            act.activation(U[:, 0, n, 0:T], y_in[:, slot, 0:T], ACT.Copy)
            act.activation(U[:, 0, n, T:TC], ysmp[:, first + n, :], ACT.Copy).then_inc(s_uhi, 1)

        act.wait_ge(s_ysmp, count.due(s_ysmp))
        for n in range(H):
            y_hi(0, n, n % 2)
        with count.loop(KD // 2, [(s_unit, 2), (s_wload[0], 1), (s_wload[1], 1)]) as i:
            for j in range(2):
                act.wait_ge(s_unit, count.due(s_unit))
                hi(j)
        for n in range(KD):
            y_hi(H, n, n % 2)
        with count.loop(KD // 2, [(s_unit, 2), (s_wload[0], 1), (s_wload[1], 1)]) as i:
            for j in range(2):
                act.wait_ge(s_unit, count.due(s_unit))
                hi(j)
        act.wait_ge(s_m, count.due(s_m, skip=KD - 1))
        for n in range(KD):
            act.activation(U[:, 0, n, :], M[:, n, :], ACT.Copy).then_inc(s_uhi, 1)
        mflat = M.rearrange("p n c -> p (n c)")
        with count.loop(KD // 2, [(s_unit, 2), (s_wload[0], 1), (s_wload[1], 1)]) as i:
            for j in range(2):
                act.wait_ge(s_unit, count.due(s_unit))
                act.activation(halves(mflat[:, bass.ds((2 * i + j) * TC, TC)]), acc[:, j, :, 0:HC],
                               ACT.Copy).then_inc(s_accfree[j], 1)
                hi(j)
        act.drain()
        squares(M, nsq)
        std(nrs)
        for n in range(KD):
            act.wait_ge(s_h, count.due(s_h))
            act.activation(U[:, 0, n, :], X[:, n, :], ACT.Copy).then_inc(s_uhi, 1)

        def ple_out(slot):
            act.wait_ge(s_full[slot], count.due(s_full[slot]))
            act.wait_ge(s_ofree[slot], count.due(s_ofree[slot]))
            act.activation(onat[:, slot, :], aux[:, slot, :], ACT.Copy).then_inc(s_free[slot], 1)
            act.drain().then_inc(s_onat, 1)

        def ple(first, last):
            for n in range(2):
                act.wait_ge(s_unit, count.due(s_unit))
                if not (last and n == 1):
                    hi(0)
                if not (first and n == 0):
                    ple_out(1 - n)
                act.wait_ge(s_unit, count.due(s_unit))
                act.activation(halves(sgt), acc[:, 1, :, 0:HC], ACT.Sigmoid).then_inc(s_accfree[1], 1)
                act.drain().then_inc(s_sgt, 1)
                if not (last and n == 1):
                    hi(1)

        ple(True, False)
        with count.loop(KD // 2 - 2, [(s_unit, 4), (s_wload[0], 2), (s_wload[1], 2), (s_full[0], 1), (s_full[1], 1),
                                  (s_ofree[0], 1), (s_ofree[1], 1)], first=1) as i:
            ple(False, False)
        ple(False, True)
        ple_out(1)
        for q in range(4):
            act.wait_ge(s_full[q], count.due(s_full[q]))
            a = act.activation(osr[0:NS, q, 0:T], aux[0:NS, q, :], ACT.Copy)
        a.then_inc(s_osrow, 1)

    @block.vector
    def _(dve):
        count = Waits(dve)

        def lo(par):
            dve.wait_ge(s_whi, count.due(s_whi))
            dve.tensor_tensor(W[:, par, 1], raw[:, par], W[:, par, 0].bitcast(F32), ALU.subtract).then_inc(s_wready, 1)

        dve.sem_inc(s_wready, 2)
        dve.memset(mean_rk[:], 1.0 / RK)
        dve.memset(one[:], 1.0)
        dve.memset(eps, EPS)
        dve.memset(mean_d[:], 1.0 / D)
        for tb in range(TB):
            for q in range(4):
                if q % 2 == 1:
                    dve.wait_ge(s_full[q], count.due(s_full[q]))
                    dve.tensor_copy(xT[:, 4 * q:4 * q + 4, tb * P:(tb + 1) * P],
                                    aux[:, q, :].rearrange("p (n c) -> p n c", n=4)).then_inc(s_free[q], 1)
                else:
                    count.skip(s_full[q])
        count.skip(s_full[0], 1)
        dve.drain()
        for j in range(2):
            count.skip(s_full[1 + j], 1)
            dve.wait_ge(s_uhi, count.due(s_uhi))
            dve.tensor_tensor(U[:, 1, KD + j, 0:T], aux[:, 1 + j, :], U[:, 0, KD + j, 0:T].bitcast(F32),
                              ALU.subtract).then_inc(s_free[1 + j], 1)
        count.skip(s_full[3], 1)
        dve.wait_ge(s_uhi, count.due(s_uhi))
        dve.tensor_tensor(U[:, 1, KD:KD + 2, T:TC], aux[:, 3, 0:2 * NS].rearrange("p (n c) -> p n c", n=2),
                          U[:, 0, KD:KD + 2, T:TC].bitcast(F32), ALU.subtract).then_inc(s_free[3], 1)
        dve.drain().then_inc(s_xt, 1)
        lo(0)
        lo(1)
        dve.wait_ge(s_std, count.due(s_std))
        count.skip(s_full[0], 1)
        dve.reciprocal(rstd, rstd)
        dve.drain()
        dve.wait_ge(s_const, 5 * 16)
        for n in range(KD):
            dve.scalar_tensor_tensor(out=utmp[:, n % 2, :], in0=xT[:, n, :], scalar=gpre[:, n:n + 1], in1=rstd,
                                     op0=ALU.mult, op1=ALU.mult).then_inc(s_u, 1)
            dve.wait_ge(s_uhi, count.due(s_uhi))
            dve.wait_ge(s_u, count.due(s_u))
            dve.tensor_tensor(U[:, 1, n, :], utmp[:, n % 2, :], U[:, 0, n, :].bitcast(F32),
                              ALU.subtract).then_inc(s_mov, 1)

        with count.loop(H, [(s_whi, 4)]) as i:
            for j in range(UNITS_GATE):
                lo(j % 2)
        count.skip(s_unit, 4 * H)

        def rows_copy(dst, ready, free):
            dve.wait_ge(s_full[3], count.due(s_full[3]))
            dve.wait_ge(free, count.due(free))
            dve.tensor_copy(dst, aux[:, 3, :].rearrange("p (t c) -> p t c", t=TB)).then_inc(s_free[3], 1)
            dve.drain().then_inc(ready, 1)

        def masked(b, h):
            w0, w = score_width(b)
            wg = P * (b + 1)
            parts = [(0, w0, 256 - w0), (w0, wg, 256 + T - wg), (w0 + wg, wg, 256 + 2 * T - wg)]
            for g, (at, n, tab) in enumerate(parts):
                dve.wait_ge(s_full[g], count.due(s_full[g]))
                dve.scalar_tensor_tensor(out=sc[b][:, at:at + n], in0=dist[:, tab:tab + n],
                                         scalar=nslope[:, bass.ds(h + g * H, 1)], in1=aux[:, g, 0:n],
                                         op0=ALU.mult, op1=ALU.add).then_inc(s_free[g], 1)
            dve.drain()
            dve.reduce_max(negmax[:, b:b + 1], sc[b], AX.X)
            dve.drain()
            dve.tensor_scalar(negmax[:, b:b + 1], negmax[:, b:b + 1], -1.0, None, ALU.mult).then_inc(s_max, 1)

        def normed(b):
            dve.wait_ge(s_exp, count.due(s_exp))
            dve.reciprocal(rden[:, b:b + 1], den[:, b:b + 1])
            dve.drain()
            dve.tensor_scalar(sc[b], sc[b], rden[:, b:b + 1], None, ALU.mult).then_inc(s_prob, 1)

        dve.wait_ge(s_dist, count.due(s_dist))
        with count.loop(H, [(s_whi, 10), (s_full[0], 7), (s_full[1], 7), (s_full[2], 7), (s_full[3], 7), (s_exp, 4),
                        (s_kfree[0], 1), (s_kfree[1], 1), (s_kfree[2], 1), (s_vfree[0], 1), (s_vfree[1], 1), (s_vfree[2], 1),
                        (s_z, 1), (s_yafree, 1)]) as h:
            for j in range(UNITS_ATT):
                if j in (4, 5, 6):
                    rows_copy(k_nat[:, j - 4], s_knat, s_kfree[j - 4])
                if j == 6:
                    masked(0, h)
                    masked(1, h)
                    normed(0)
                    masked(2, h)
                    normed(1)
                if j == 7:
                    masked(3, h)
                    for g in range(G):
                        count.skip(s_full[g], 3)
                    normed(2)
                    rows_copy(v_nat[:, 0], s_vnat, s_vfree[0])
                    normed(3)
                if j == 8:
                    rows_copy(v_nat[:, 1], s_vnat, s_vfree[1])
                if j == 9:
                    rows_copy(v_nat[:, 2], s_vnat, s_vfree[2])
                lo(j % 2)
            dve.wait_ge(s_full[3], count.due(s_full[3]))
            dve.wait_ge(s_z, count.due(s_z))
            dve.wait_ge(s_yafree, count.due(s_yafree))
            dve.tensor_tensor(ya_out, aux[:, 3, :], silu_z[:, 0, 0:T], ALU.mult).then_inc(s_free[3], 1)
            dve.drain().then_inc(s_ya, 1)
        count.skip(s_unit, 10 * H)

        for g in range(G):
            dve.wait_ge(s_kfree[g], count.due(s_kfree[g]))
            dve.wait_ge(s_vfree[g], count.due(s_vfree[g]))
        dve.wait_ge(s_yafree, count.due(s_yafree))
        dve.wait_ge(s_decay, count.due(s_decay))
        decayf = decay.rearrange("p h c -> p (h c)")
        with count.loop(H, [(s_whi, 8), (s_full[0], 5), (s_full[1], 5), (s_full[2], 1), (s_full[3], 1), (s_z, 2),
                        (s_rstd, 1), (s_stfree, 1), (s_ytfree, 1)]) as h:
            for j in range(UNITS_RET):
                if j == 4:
                    for d in range(2):
                        dve.wait_ge(s_full[d], count.due(s_full[d]))
                        for tb in range(TB):
                            a = dve.tensor_scalar(ks[:, tb, d * P:(d + 1) * P], aux[:, d, tb * P:(tb + 1) * P],
                                                  kdec[:, bass.ds(h * TB + tb, 1)], None, ALU.mult)
                        a.then_inc(s_free[d], 1)
                        dve.drain().then_inc(s_ks, 1)
                if j == 5:
                    for jb in range(TB):
                        dve.wait_ge(s_full[jb % 2], count.due(s_full[jb % 2]))
                        dve.tensor_tensor(sm[jb], aux[:, jb % 2, 0:T - jb * P], decayf[:, bass.ds(h * T, T - jb * P)],
                                          ALU.mult).then_inc(s_free[jb % 2], 1)
                        dve.drain().then_inc(s_sm, 1)
                if j == 6:
                    for e in range(2):
                        dve.wait_ge(s_full[e], count.due(s_full[e]))
                        dve.tensor_copy(vn[:, :, e * P:(e + 1) * P],
                                        aux[:, e, :].rearrange("p (t c) -> p t c", t=TB)).then_inc(s_free[e], 1)
                        dve.drain().then_inc(s_vn, 1)
                if j == 7:
                    dve.wait_ge(s_full[0], count.due(s_full[0]))
                    dve.wait_ge(s_stfree, count.due(s_stfree))
                    dve.tensor_copy(st, aux[:, 0, :].rearrange("p (j c) -> p j c", j=2)).then_inc(s_free[0], 1)
                    dve.drain().then_inc(s_st, 1)
                lo(j % 2)
            dve.wait_ge(s_full[1], count.due(s_full[1]))
            dve.wait_ge(s_rstd, count.due(s_rstd))
            dve.wait_ge(s_z, count.due(s_z, skip=1))
            dve.wait_ge(s_ytfree, count.due(s_ytfree))
            dve.reciprocal(rrs, rrs)
            dve.drain()
            for e in range(2):
                dve.wait_ge(s_full[2 + e], count.due(s_full[2 + e]))
                dve.scalar_tensor_tensor(out=yt[:, e, :], in0=aux[:, 2 + e, :], scalar=gret[:, bass.ds(2 * h + e, 1)],
                                         in1=rrs, op0=ALU.mult, op1=ALU.mult).then_inc(s_free[2 + e], 1)
            dve.drain()
            for e in range(2):
                dve.tensor_tensor(yt[:, e, :], yt[:, e, :], rz[:, e, 0:T], ALU.mult).then_inc(s_yt, 1)
        count.skip(s_unit, 8 * H)

        dve.wait_ge(s_stfree, count.due(s_stfree))
        dve.wait_ge(s_ytfree, count.due(s_ytfree))
        for bank, n in ((0, 4), (1, 4), (2, 1)):
            dve.wait_ge(s_full[bank], count.due(s_full[bank]))
            dve.tensor_copy(rows[0:64, bank * 4:bank * 4 + n, :],
                            aux[0:64, bank, 0:n * P].rearrange("p (n c) -> p n c", n=n)).then_inc(s_free[bank], 1)
        dve.wait_ge(s_full[3], count.due(s_full[3]))
        dve.tensor_copy(vrow, aux[:, 3, 0:P]).then_inc(s_free[3], 1)
        dve.drain().then_inc(s_rows, 1)
        zg = zs[:].rearrange("p (t b) -> p t b", b=NS)
        dve.tensor_tensor(pcol.rearrange("p g c -> p (g c)"), zs[:, 0:G * 64],
                          zs[:, KA // P * NS:KA // P * NS + G * 64], ALU.mult).then_inc(s_self, 1)
        dve.wait_ge(s_full[3], count.due(s_full[3]))
        dve.tensor_copy(selfs[0:64, :], aux[0:64, 3, 0:G]).then_inc(s_free[3], 1)
        dve.drain()
        for b in range(NS):
            q = b % 2
            dve.wait_ge(s_sk[q], 64 * (b // 2 + 1))
            dve.tensor_tensor(s_k[:, q], s_k[:, q], s_q[:, q], ALU.mult)
            dve.drain()
            dve.tensor_reduce(scol.rearrange("p g (h b) -> p g h b", b=NS)[:, :, :, b], s_k[:, q].rearrange("p g (h d) -> p g h d", h=H),
                              AX.X, ALU.add).then_inc(s_skfree if b < NS - 1 else s_scol, 1)
        dve.wait_ge(s_full[0], count.due(s_full[0]))
        dve.wait_ge(s_sbias, count.due(s_sbias))
        dve.tensor_tensor(srow[0:64, :, 0:NK], aux[0:64, 0, 0:G * P].rearrange("p (g c) -> p g c", g=G),
                          sbias[0:64, :, 0:NK], ALU.add).then_inc(s_free[0], 1)
        dve.tensor_copy(srow[0:64, :, NK:NK + 1], selfs[0:64, :].rearrange("p (g o) -> p g o", o=1))
        dve.drain()
        dve.reduce_max(negmax[0:64, 0:1], srow[0:64].rearrange("p g c -> p (g c)"), AX.X)
        dve.drain()
        dve.tensor_scalar(negmax[0:64, 0:1], negmax[0:64, 0:1], -1.0, None, ALU.mult).then_inc(s_smax, 1)
        dve.wait_ge(s_sexp, count.due(s_sexp))
        dve.reciprocal(rden[0:64, 0:1], den[0:64, 0:1])
        dve.drain()
        dve.tensor_scalar(srow[0:64], srow[0:64], rden[0:64, 0:1], None, ALU.mult)
        dve.drain()
        for g in range(G):
            dve.tensor_scalar(pdiag[0:64, g, :], ident[0:64, 0:64], srow[0:64, g, NK:NK + 1], None, ALU.mult)
        dve.drain().then_inc(s_sprob, 1)
        dve.wait_ge(s_full[1], count.due(s_full[1]))
        dve.tensor_copy(pcol, aux[:, 1, 0:G * 64].rearrange("p (g c) -> p g c", g=G)).then_inc(s_free[1], 1)
        dve.drain().then_inc(s_pcol, 1)
        dve.wait_ge(s_full[2], count.due(s_full[2]))
        dve.tensor_tensor(spv.rearrange("p g c -> p (g c)"), aux[:, 2, 0:G * 64],
                          zs[:, VA // P * NS:VA // P * NS + G * 64], ALU.mult).then_inc(s_free[2], 1)
        dve.drain()
        dve.tensor_tensor(oself, spv[:, 0, :], spv[:, 1, :], ALU.add)
        dve.drain()
        dve.tensor_tensor(oself, oself, spv[:, 2, :], ALU.add)
        dve.drain()
        dve.wait_ge(s_full[3], count.due(s_full[3]))
        dve.tensor_tensor(oself, aux[:, 3, 0:64], oself, ALU.add).then_inc(s_free[3], 1)
        dve.drain()
        dve.tensor_tensor(ysmp[:, 0:H, :].rearrange("p h b -> p (h b)"), oself,
                          zs[:, ZA // P * NS:ZA // P * NS + 64], ALU.mult)

        dve.drain().then_inc(s_skfree, 1)
        for b in range(NS):
            q = b % 2
            dve.wait_ge(s_rgam, count.due(s_rgam))
            for h in range(H):
                for j in range(2):
                    at = (KR // P + 2 * h + j) * NS + b
                    dve.scalar_tensor_tensor(out=r_st[:, q, h, j, :], in0=r_v[:, q, h, :], scalar=zs[:, at:at + 1],
                                             in1=r_st[:, q, h, j, :], op0=ALU.mult, op1=ALU.add)
            dve.drain().then_inc(s_rnew, 1)
            dve.wait_ge(s_full[q], count.due(s_full[q]))
            dve.tensor_copy(ysr[:, :, b:b + 1], aux[:, q, 0:16].rearrange("p (t o) -> p t o", o=1)).then_inc(s_free[q], 1)
            dve.drain().then_inc(s_ysr, 1)
        dve.tensor_tensor(ssq, ysr, ysr, ALU.mult).then_inc(s_ssq, 1)
        dve.wait_ge(s_full[2], count.due(s_full[2]))
        dve.wait_ge(s_sstd, count.due(s_sstd))
        dve.reciprocal(srs, srs)
        for tile in range(2 * H):
            dve.tensor_scalar(yg[:, tile, :], zg[:, ZR // P + tile, :], gret[:, tile:tile + 1], None, ALU.mult)
        dve.drain()
        dve.tensor_tensor(yg, yg, ysr, ALU.mult)
        dve.drain()
        for e in range(2):
            dve.tensor_tensor(ysmp[:, H:NYT, :].rearrange("p (h e) b -> p e h b", e=2)[:, e],
                              yg.rearrange("p (h e) b -> p e h b", e=2)[:, e],
                              srs.rearrange("p (h b) -> p h b", b=NS), ALU.mult)
        dve.drain().then_inc(s_ysmp, 1)

        def y_lo(first, n, slot):
            dve.wait_ge(s_uhi, count.due(s_uhi))
            dve.tensor_tensor(U[:, 1, n, 0:T], y_in[:, slot, 0:T], U[:, 0, n, 0:T].bitcast(F32),
                              ALU.subtract).then_inc(s_yinfree, 1)
            dve.tensor_tensor(U[:, 1, n, T:TC], ysmp[:, first + n, :], U[:, 0, n, T:TC].bitcast(F32),
                              ALU.subtract).then_inc(s_mov, 1)

        mflat = M.rearrange("p n c -> p (n c)")
        proj_rates = [(s_unit, 2), (s_whi, 2), (s_sgin[0], 1), (s_sgin[1], 1)]
        for n in range(H):
            y_lo(0, n, n % 2)
        with count.loop(KD // 2, proj_rates) as i:
            for j in range(2):
                dve.wait_ge(s_unit, count.due(s_unit))
                dve.wait_ge(s_sgin[j], count.due(s_sgin[j]))
                dve.tensor_tensor(halves(mflat[:, bass.ds((2 * i + j) * TC, TC)]), acc[:, j, :, 0:HC],
                                  halves(sg_in[:, j, :]), ALU.mult).then_inc(s_accfree[j], 1)
                lo(j)
        for n in range(KD):
            y_lo(H, n, n % 2)
        with count.loop(KD // 2, proj_rates) as i:
            for j in range(2):
                dve.wait_ge(s_unit, count.due(s_unit))
                dve.wait_ge(s_sgin[j], count.due(s_sgin[j]))
                dve.tensor_tensor(halves(tmp), acc[:, j, :, 0:HC], halves(sg_in[:, j, :]),
                                  ALU.mult).then_inc(s_accfree[j], 1)
                dve.drain()
                mt = mflat[:, bass.ds((2 * i + j) * TC, TC)]
                dve.tensor_tensor(mt, mt, tmp, ALU.add).then_inc(s_m, 1)
                lo(j)
                dve.drain()
        dve.drain()
        for n in range(KD):
            dve.wait_ge(s_uhi, count.due(s_uhi))
            dve.tensor_tensor(U[:, 1, n, :], M[:, n, :], U[:, 0, n, :].bitcast(F32), ALU.subtract).then_inc(s_mov, 1)
        with count.loop(KD // 2, [(s_whi, 2)]) as i:
            for j in range(2):
                lo(j)
        count.skip(s_unit, KD)
        dve.wait_ge(s_std, count.due(s_std))
        count.skip(s_full[0], 1)
        dve.reciprocal(nrs, nrs)
        dve.drain()
        dve.wait_ge(s_xin, count.due(s_xin, skip=KD - 1))
        for n in range(KD):
            dve.scalar_tensor_tensor(out=M[:, n, :], in0=M[:, n, :], scalar=gpost[:, n:n + 1], in1=nrs,
                                     op0=ALU.mult, op1=ALU.mult)
            dve.drain()
            dve.tensor_tensor(X[:, n, :], X[:, n, :], M[:, n, :], ALU.add).then_inc(s_h, 1)
            dve.wait_ge(s_uhi, count.due(s_uhi))
            dve.tensor_tensor(U[:, 1, n, :], X[:, n, :], U[:, 0, n, :].bitcast(F32), ALU.subtract).then_inc(s_mov, 1)

        xflat = X.rearrange("p n c -> p (n c)")
        lo_in_ple = [0]

        def ple(i, last):
            for n in range(2):
                dve.wait_ge(s_unit, count.due(s_unit))
                if not (last and n == 1):
                    lo(0)
                dve.wait_ge(s_unit, count.due(s_unit))
                dve.wait_ge(s_sgt, count.due(s_sgt))
                dve.tensor_tensor(halves(etmp), acc[:, 0, :, 0:HC], halves(sgt), ALU.mult).then_inc(s_accfree[0], 1)
                dve.drain()
                at = (2 * i + n) * TC
                dve.tensor_tensor(outT[:, n, :], etmp, xflat[:, bass.ds(at, TC)], ALU.add).then_inc(s_out, 1)
                dve.drain()
                dve.tensor_copy(outS[:, bass.ds((2 * i + n) * NS, NS)], outT[:, n, T:TC])
                dve.drain()
                if not (last and n == 1):
                    lo(1)

        with count.loop(KD // 2 - 1, [(s_unit, 4), (s_whi, 4), (s_sgt, 2)]) as i:
            ple(i, False)
        ple(KD // 2 - 1, True)
        dve.drain().then_inc(s_os, 1)

    @block.gpsimd
    def _(pool):
        count = Waits(pool)
        pool.sem_inc(s_begun, 1)
        for q in [*s_sgfree, *s_kfree, *s_vfree, s_yafree, s_stfree, s_ytfree, *s_ofree]:
            pool.sem_inc(q, 1)

        def store(dst, src, stored, free=None):
            pool.dma_start(dst, src).then_inc(stored, 16)
            pool.wait_ge(stored, count.due(stored))
            if free is not None:
                pool.sem_inc(free, 1)
        with nc.allow_non_contiguous_dma("small per-feature vectors"):
            pool.dma_start(small[:, 0:16], g_pre[0].rearrange("(n p) -> p n", p=P)).then_inc(s_const, 16)
            pool.dma_start(small[:, 16:32], g_post[0].rearrange("(n p) -> p n", p=P)).then_inc(s_const, 16)
            pool.dma_start(small[:, 32:48], g_ret[0].rearrange("(n p) -> p n", p=P)).then_inc(s_const, 16)
        pool.dma_start(small[:, 48:72], c_slope).then_inc(s_const, 16)
        pool.dma_start(small[:, 72:104], c_kdec).then_inc(s_const, 16)
        pool.wait_ge(s_xt, count.due(s_xt, skip=1))
        for n in range(KD):
            pool.dma_start(xt_scr[n], xT[:, n, :]).then_inc(s_xtst, 16)
        with count.loop(H, [(s_sg, 4), (s_sgst, 4)]) as i:
            for j in range(UNITS_GATE):
                pool.wait_ge(s_sg, count.due(s_sg))
                store(sg_scr[j % 2, bass.ds(2 * i + j // 2, 1)].rearrange("o p c -> (o p) c"),
                      sg_out[:, j % 2, :], s_sgst, s_sgfree[j % 2])
        with count.loop(H, [(s_knat, 3), (s_vnat, 3), (s_ya, 1), (s_kst, 3), (s_vst, 3), (s_yast, 1)]) as h:
            for kv, (src, ready, stored, free) in enumerate(((k_nat, s_knat, s_kst, s_kfree), (v_nat, s_vnat, s_vst, s_vfree))):
                for g in range(G):
                    pool.wait_ge(ready, count.due(ready))
                    pool.sem_inc(s_pool_waits, 1)
                    keep = min(WIN[g], T)
                    dst = winp[g][0, 0].rearrange("(t p) k h d -> p t k (h d)", p=P)[:, :, kv, bass.ds(h * HD, HD)]
                    store(dst, src[:, g, TB - keep // P:TB, :], stored, free[g])
            pool.wait_ge(s_ya, count.due(s_ya))
            store(y_scr[bass.ds(h, 1)].rearrange("o p c -> (o p) c"), ya_out, s_yast, s_yafree)
        pool.dma_start(decay.rearrange("p h c -> p (h c)"), c_decay).then_inc(s_decay, 16)
        with count.loop(H, [(s_st, 1), (s_yt, 2), (s_stst, 1), (s_ytst, 2)]) as h:
            pool.wait_ge(s_st, count.due(s_st))
            store(ret_p[0, 0, bass.ds(h, 1)].rearrange("o (j p) e -> p (o j) e", p=P), st, s_stst, s_stfree)
            for e in range(2):
                pool.wait_ge(s_yt, count.due(s_yt))
                store(y_scr[bass.ds(H + 2 * h + e, 1)].rearrange("o p c -> (o p) c"), yt[:, e, :], s_ytst,
                      s_ytfree if e == 1 else None)

        pool.wait_ge(s_rows, 1)
        pool.dma_start(row_scr.rearrange("n p c -> p n c"), rows[0:64]).then_inc(s_rowst, 16)
        pool.dma_start(vrow_scr, vrow).then_inc(s_rowst, 16)
        pool.dma_start(sbias[0:64], c_bias.rearrange("p (g c) -> p g c", g=G)).then_inc(s_sbias, 16)
        pool.wait_ge(s_rowst, 32)
        for kv in range(2):
            for g in range(G):
                pool.dma_start(wins[g][0, :, WIN[g] - 1, kv],
                               row_scr[(1 + kv) * G + g].rearrange("(h b) d -> b h d", b=NS)).then_inc(s_newrow, 16)

        def cached(b, kv, dst, done):
            for g in range(G):
                src = caches[g][0, b, :, kv].rearrange("(m o) h d -> m o (h d)", o=DIL[g])[:, 0, :]
                pool.dma_start(dst[:, b % 2, g, :], src).then_inc(done[b % 2], 16)
        for b in range(NS):
            if b >= 2:
                pool.wait_ge(s_skfree, b - 1)
            cached(b, 0, s_k, s_sk)
            q_src = row_scr[0:G].rearrange("g (h b) d -> b (g h) d", b=NS)[b:b + 1]
            pool.dma_start(s_q[:, b % 2].rearrange("p g (h d) -> p (g h) d", h=H), q_src.broadcast_to([P, G * H, HD])).then_inc(s_sk[b % 2], 16)
        pool.wait_ge(s_scol, 1)
        for b in range(NS):
            if b >= 2:
                pool.wait_ge(s_svfree, b - 1)
            cached(b, 1, s_v, s_sv)
        pool.wait_ge(s_skfree, NS)
        for b in range(NS):
            q = b % 2
            if b >= 2:
                pool.wait_ge(s_rnewst[q], 16 * (b // 2))
                pool.wait_ge(s_ysr, b - 1)
            pool.dma_start(r_st[:, q].rearrange("p h j e -> p (h j) e"),
                           state[0, b].rearrange("h (j p) e -> p (h j) e", p=P)).then_inc(s_rst[q], 16)
            v_src = vrow_scr.rearrange("(t b) c -> b t c", b=NS)[b:b + 1]
            pool.dma_start(r_v[:, q].rearrange("p h (e c) -> p (h e) c", e=2), v_src.broadcast_to([P, 2 * H, P])).then_inc(s_rst[q], 16)
            pool.wait_ge(s_rnew, b + 1)
            pool.dma_start(ret_s[0, b].rearrange("h (j p) e -> p (h j) e", p=P),
                           r_st[:, q].rearrange("p h j e -> p (h j) e")).then_inc(s_rnewst[q], 16)

        pool.wait_ge(s_ysmp, 1)
        for q in range(2):
            pool.wait_ge(s_rnewst[q], 16 * (NS // 2))
            count.starts[id(s_accfree[q])] = (H * UNITS_GATE + H * UNITS_ATT + H * UNITS_RET) // 2
        pool.wait_ge(s_xtst, 16 * KD)

        def y_loads(first, count, before):
            for n in range(count):
                if before + n >= 2:
                    pool.wait_ge(s_yinfree, before + n - 1)
                pool.dma_start(y_in[:, n % 2, 0:T], y_scr[first + n]).then_inc(s_yin[n % 2], 16)

        def gate_loads(which):
            with count.loop(KD // 2, [(s_accfree[0], 1), (s_accfree[1], 1)]) as i:
                for j in range(2):
                    pool.wait_ge(s_accfree[j], count.due(s_accfree[j]))
                    pool.dma_start(sg_in[:, j, :], sg_scr[which, bass.ds(2 * i + j, 1)].rearrange("o p c -> (o p) c")
                                   ).then_inc(s_sgin[j], 16)

        y_loads(0, H, 0)
        gate_loads(0)
        y_loads(H, 2 * H, H)
        gate_loads(1)
        pool.wait_ge(s_yinfree, NYT)
        for n in range(KD):
            pool.dma_start(X[:, n, :], xt_scr[n]).then_inc(s_xin, 16)
        with count.loop(KD // 2, [(s_onat, 2), (s_ost, 2)]) as i:
            for n in range(2):
                pool.wait_ge(s_onat, count.due(s_onat))
                dst = y_prompt[0].rearrange("(t p) c -> p t c", p=P)[:, :, bass.ds((2 * i + n) * P, P)]
                store(dst, onat[:, n, :].rearrange("p (t c) -> p t c", t=TB), s_ost, s_ofree[n])
        pool.wait_ge(s_osrow, 1)
        pool.dma_start(y_sample.rearrange("b o (q c) -> (b o) q c", q=4), osr[0:NS, :, 0:T]).then_inc(s_osst, 16)
        pool.wait_ge(s_newrow, 16 * 2 * G)
        pool.wait_ge(s_osst, 16)

    stack.close()


def constants():
    ident = np.eye(P, dtype=np.float32)
    q, x = np.arange(P)[:, None], np.arange(T)[None, :]
    d0 = q + P - x[:, :2 * P]
    d0 = np.where((d0 >= 0) & (d0 <= WIN[0]), d0, BIG)
    d12 = q + T - P - x
    tabs = [d0] + [np.where((d12 >= 0) & (d12 % dil == 0) & (d12 <= win), d12, BIG)
                   for dil, win in zip(DIL[1:], WIN[1:])]
    dist = np.concatenate(tabs, axis=1).astype(np.float32)
    slope = np.tile(-slopes()[None, :], (P, 1)).astype(np.float32)
    lg = log_decay()
    rel = x - q
    decay = np.concatenate([np.where(rel >= 0, np.exp(np.maximum(rel, 0) * lg[h]), 0.0) for h in range(H)], axis=1)
    j = np.arange(TB)[None, :] * P + np.arange(P)[:, None]
    kdec = np.concatenate([np.exp((T - 1 - j) * lg[h]) for h in range(H)], axis=1)
    bias = np.zeros((64, G, NK + 1))
    sl = slopes().reshape(G, H)
    for g in range(G):
        far = (NK - np.arange(NK + 1)) * DIL[g]
        bias[:, g] = -sl[g][np.arange(64) // NS][:, None] * far[None, :]
    return {"c_ident": ident, "c_dist": dist, "c_slope": slope, "c_decay": decay.astype(np.float32),
            "c_kdec": kdec.astype(np.float32), "c_bias": bias.reshape(64, -1).astype(np.float32)}


_INS = ["x_prompt", "x_sample", "cache_win0", "cache_win1", "cache_win2", "state_ret", "p_prompt", "p_sample",
        "g_pre", "w_in", "g_ret", "w_a_out", "w_r_out", "w_o", "g_post", "w_ple_gate", "w_ple_proj"]
_OUTS = [(1, T, D), (NS, 1, D), (1, 1, 128, 2, H, HD), (1, 1, T, 2, H, HD), (1, 1, T, 2, H, HD),
         (1, 1, H, RK, RK), (1, NS, 128, 2, H, HD), (1, NS, 512, 2, H, HD), (1, NS, 2048, 2, H, HD),
         (1, NS, H, RK, RK)]


def declare(nc, inputs):
    arrays, args = {}, []
    for name, a in [(n, inputs[n]) for n in _INS] + list(constants().items()):
        a = np.ascontiguousarray(a)
        arrays[f"in_{name}"] = a
        args.append(nc.dram_tensor(f"in_{name}", a.shape, mybir.dt.from_np(a.dtype), kind="ExternalInput").ap())
    for i, shape in enumerate(_OUTS):
        args.append(nc.dram_tensor(f"out_{i}", shape, F32, kind="ExternalOutput").ap())
    build(nc, *args)
    return arrays


def kernel(**inputs):
    import concourse.bacc as bacc
    from concourse.bass_utils import run_bass_kernel_spmd

    nc = bacc.Bacc("TRN2", target_bir_lowering=False, num_devices=1)
    arrays = declare(nc, inputs)
    r = run_bass_kernel_spmd(nc, [arrays], core_ids=[0])
    return tuple(r.results[0][f"out_{i}"] for i in range(len(_OUTS)))
```

```python
from contextlib import contextmanager, ExitStack

import numpy as np

import concourse.bass as bass
from concourse import mybir
from concourse.alu_op_type import AluOpType as ALU

F32 = mybir.dt.float32
F32R = mybir.dt.float32r
ACT = mybir.ActivationFunctionType
AX = mybir.AxisListType

P = 128
D = 2048
KD = D // P
T = 512
TB = T // P
NS = 8
TC = T + NS
HC = TC // 2
H = 8
G = 3
HD = 128
DIL = (1, 4, 16)
WIN = (128, 512, 2048)
NK = 128
RK = 256
PLE = 256
EPS = 1e-6
QA, KA, VA, ZA = 0, 3072, 6144, 9216
QR, KR, VR, ZR = 10240, 12288, 14336, 16384
GA, GB = 18432, 20480
N_IN = 22528
ZT = GA // P
NYT = H + 2 * H
ROW = 2 * H * HD
BIG = 1e30


def slopes():
    n = G * H
    return 2.0 ** (-8.0 * (np.arange(n) + 1.0) / n)


def log_decay():
    return np.log1p(-(2.0 ** (-5.0 - np.arange(H))))


def score_width(b):
    w0 = P * min(b + 1, 2)
    return w0, w0 + 2 * P * (b + 1)


class Tally:

    def __init__(self, start=0, unit=1):
        self.base, self.unit, self.local, self.i, self.rate = start, unit, 0, None, 0

    def next(self, skip=0):
        self.local += 1 + skip
        n = self.base + self.local
        return self.unit * n if self.i is None else self.unit * (self.i * self.rate + n)

    def enter(self, i, rate, first):
        self.base, self.local, self.rate = self.base + self.local - first * rate, 0, rate
        self.i = i

    def leave(self, n, first, name):
        assert self.local == self.rate, (name, self.local, self.rate)
        self.base, self.local, self.i = self.base + (n + first) * self.rate, 0, None


def build(nc, x_prompt, x_sample, cache0, cache1, cache2, state, p_prompt, p_sample, g_pre, w_in, g_ret,
          w_a, w_r, w_o, g_post, w_gate, w_proj,
          c_ident, c_dist, c_slope, c_decay, c_kdec, c_bias,
          y_prompt, y_sample, win0p, win1p, win2p, ret_p, win0s, win1s, win2s, ret_s):
    stack = ExitStack()
    caches, winp, wins = (cache0, cache1, cache2), (win0p, win1p, win2p), (win0s, win1s, win2s)
    gamma = [float(np.float32(g)) for g in np.exp(log_decay())]

    def dram(name, shape):
        return nc.dram_tensor(name, shape, F32, kind="Internal").ap()

    xt_scr = dram("xt_scr", [KD, P, TC])
    sg_scr = dram("sg_scr", [2, KD, P, TC])
    y_scr = dram("y_scr", [NYT, P, T])
    pp_scr = dram("pp_scr", [KD, P, TC])
    row_scr = dram("row_scr", [9, 64, HD])
    vrow_scr = dram("vrow_scr", [P, P])

    def sem(name):
        return stack.enter_context(nc.semaphore(name))

    U = stack.enter_context(nc.sbuf_tensor("moving", [P, 2, KD + 2, TC], F32R))
    W = stack.enter_context(nc.sbuf_tensor("weights", [P, 2, 2, KD, P], F32R))
    raw = stack.enter_context(nc.sbuf_tensor("raw_weights", [P, 2, KD, P], F32))
    ident = stack.enter_context(nc.sbuf_tensor("ident", [P, P], F32))
    one = stack.enter_context(nc.sbuf_tensor("one", [P, P], F32))
    mean_rk = stack.enter_context(nc.sbuf_tensor("mean_rk", [P, P], F32))
    mean_d = stack.enter_context(nc.sbuf_tensor("mean_d", [P, P], F32))
    small = stack.enter_context(nc.sbuf_tensor("small", [P, 256], F32))
    zs = stack.enter_context(nc.sbuf_tensor("sampled", [P, ZT * NS], F32))
    POOL_F = (212863 - 107648 - 16384 - 4 * 512 - 1024 - 4608) // 64 * 16 - 16
    pool_f = stack.enter_context(nc.sbuf_tensor("stage_buffers", [P, POOL_F], F32))
    acc = stack.enter_context(nc.psum_tensor("acc", [P, 2, 2, 512], F32))
    aux = stack.enter_context(nc.psum_tensor("aux", [P, 4, 512], F32))

    gpre, gpost, gret = small[:, 0:16], small[:, 16:32], small[:, 32:48]
    nslope, kdec = small[:, 48:72], small[:, 72:104]
    negmax, den, rden = small[:, 104:108], small[:, 108:112], small[:, 112:116]
    selfs, eps = small[:, 116:119], small[:, 120:121]

    def carve():
        at = [0]

        def take(*shape):
            n = int(np.prod(shape))
            a = pool_f[:, at[0]:at[0] + n]
            at[0] += n
            assert at[0] <= POOL_F, (at[0], POOL_F)
            if len(shape) == 1:
                return a
            names = "abcd"[:len(shape)]
            spec = f"p ({' '.join(names)}) -> p {' '.join(names)}"
            return a.rearrange(spec, **dict(zip(names, shape)))
        return take

    t = carve()
    x_nat, xs_nat = t(TB, D), t(D)
    p_nat, ps_nat = t(TB, PLE), t(PLE)
    xT = t(KD, TC)
    t = carve()
    sq, rstd, utmp, pp_out = t(2, TC), t(TC), t(2, TC), t(2, TC)
    t = carve()
    qT, kT, vT, silu_z = t(G, TC), t(G, TC), t(2, TC), t(1, TC)
    k_nat, v_nat = t(G, TB, P), t(G, TB, P)
    sc = [t(score_width(b)[1]) for b in range(TB)]
    PT = t(G, TB, T)
    ya_out = t(T)
    dist = t(256 + 512 + 512)
    t = carve()
    rq, rk, rv, rz = t(2, TC), t(2, TC), t(2, TC), t(2, TC)
    ks, vn = t(TB, RK), t(TB, RK)
    sm = [t(T - P * j) for j in range(TB)]
    rsq, rrs, yt, st = t(2, T), t(T), t(2, T), t(2, RK)
    decay = t(H, T)
    t = carve()
    HH = H // 2
    ysmp = t(NYT, NS)
    sg_out = t(2, TC)
    r_st, r_v = t(2, HH, 2, RK), t(2, HH, RK)
    ysr, ssq, srs, yg = t(2 * H, NS), t(2 * H, NS), t(64), t(2 * H, NS)
    scol, qk, pcol, oself, spv = t(G, H), t(G, H), t(G, H), t(H), t(G, H)
    t = carve()
    t(NYT, NS)
    t(KD, TC)
    s_k, s_q, s_v = t(G, H * HD), t(G, H * HD), t(G, H * HD)
    srow, sbias = t(G, NK + 1), t(G, NK + 1)
    rows = s_v.rearrange("p g c -> p (g c)")[:, 0:9 * HD].rearrange("p (n c) -> p n c", n=9)
    vrow = s_v.rearrange("p g c -> p (g c)")[:, 9 * HD:10 * HD]
    pdiag = small[0:H, 128:128 + G * H].rearrange("p (g h) -> p g h", g=G)
    t = carve()
    t(NYT, NS)
    M, X = t(KD, TC), t(KD, TC)
    sg_in, tmp = t(2, TC), t(TC)
    y_in = X
    sqb, sqsum, nrs = sg_in, tmp, sg_in[:, 0, :]
    outT = M[:, 0:2, :]
    outS, sgt, onat = M[:, 2, 0:KD * NS], M[:, 3, :], M[:, 4:6, 0:T]
    etmp, osr, pp_in = M[:, 6, :], M[:, 8:12, :], M[:, 12:14, :]

    def sems(name, n):
        return [sem(f"{name}{i}") for i in range(n)]
    s_begun = sem("program_begun")
    s_pool_waits = sem("pool_waits")
    s_ident = sem("identity_loaded")
    s_const = sem("consts_loaded")
    s_xload = sems("x_loaded", 6)
    s_wload = sems("weights_loaded", 2)
    s_whi = sem("weights_hi")
    s_wready = sem("weights_ready")
    s_unit = sem("unit_done")
    s_accfree = sems("acc_free", 2)
    s_full = sems("aux_full", 4)
    s_free = sems("aux_free", 4)
    s_xt = sem("xT_ready")
    s_sq = sem("squares_ready")
    s_sqfree = sem("squares_read")
    s_std = sem("std_ready")
    s_u = sem("u_plain_ready")
    s_uhi = sem("moving_hi")
    s_mov = sem("moving_ready")
    s_xtst = sem("xT_stored")
    s_pp = sem("projected_input_ready")
    s_ppst = sem("projected_input_stored")
    s_ppfree = sems("projected_input_free", 2)
    s_ppin = sems("projected_input_loaded", 2)
    s_ppread = sem("projected_input_read")
    s_sg = sem("gate_ready")
    s_sgst = sem("gate_stored")
    s_sgfree = sems("gate_buffer_free", 2)
    s_zT = sem("head_tile_ready")
    s_z = sem("silu_z_ready")
    s_knat = sem("k_rows_ready")
    s_vnat = sem("v_rows_ready")
    s_kst = sem("k_rows_stored")
    s_vst = sem("v_rows_stored")
    s_kfree = sems("k_rows_free", 3)
    s_vfree = sems("v_rows_free", 3)
    s_max = sem("max_ready")
    s_exp = sem("exp_ready")
    s_prob = sem("probs_ready")
    s_ya = sem("y_tile_ready")
    s_yast = sem("y_tile_stored")
    s_yafree = sem("y_tile_free")
    s_dist = sem("dist_loaded")
    s_decay = sem("decay_loaded")
    s_ks = sem("scaled_k_ready")
    s_pt = sem("probs_turned")
    s_vn = sem("ret_v_rows_ready")
    s_sm = sem("decayed_scores_ready")
    s_rstd = sem("ret_std_ready")
    s_st = sem("state_ready")
    s_stst = sem("state_stored")
    s_stfree = sem("state_free")
    s_yt = sem("ret_y_ready")
    s_ytst = sem("ret_y_stored")
    s_ytfree = sem("ret_y_free")
    s_rows = sem("sample_rows_ready")
    s_rowst = sem("sample_rows_stored")
    s_newrow = sem("new_cache_rows_stored")
    s_sk = sem("sample_k_and_q_loaded")
    s_skfree = sem("sample_k_and_q_read")
    s_scol = sem("score_columns_ready")
    s_smax = sem("sample_max_ready")
    s_sexp = sem("sample_exp_ready")
    s_sprob = sem("sample_probs_ready")
    s_pcol = sem("prob_columns_ready")
    s_sv = sem("sample_v_loaded")
    s_svfree = sem("sample_v_read")
    s_rst = sems("sample_state_loaded", 2)
    s_rgam = sem("sample_state_scaled")
    s_rhalf = sem("half_states_read")
    s_rnew = sem("sample_state_new")
    s_rnewst = sems("sample_state_stored", 2)
    s_ssq = sem("sample_squares_ready")
    s_sstd = sem("sample_std_ready")
    s_ysmp = sem("sample_y_ready")
    s_sbias = sem("sample_bias_loaded")
    s_yin = [sem(f"y_in_{n}_loaded") for n in ("attention", "ret_8_to_15", "ret_0_to_7")]
    s_yinfree = sem("y_in_read")
    s_sgin = sems("gate_in_loaded", 2)
    s_xin = sem("x_in_loaded")
    s_m = sem("merged_ready")
    s_sqadd = sem("squares_added")
    s_sqsum = sem("square_sums_ready")
    s_mr = sem("normed_y_ready")
    s_h = sem("h_ready")
    s_sgt = sem("ple_gate_ready")
    s_out = sem("out_tile_ready")
    s_onat = sem("out_rows_ready")
    s_ost = sem("out_rows_stored")
    s_ofree = sems("out_rows_free", 2)
    s_os = sem("sample_out_ready")
    s_osrow = sem("sample_out_rows_ready")
    s_osst = sem("sample_out_stored")
    s_copy = sem("cache_rows_copied")

    BY16 = {id(s) for s in [s_const, s_dist, s_decay, s_xtst, s_yast, s_stst, s_ytst, s_rowst, s_xin,
                            s_sbias, s_sgst, s_kst, s_vst, s_ost, s_ppst, *s_ppin, *s_xload, *s_wload, s_sk, s_sv, *s_rst,
                            *s_rnewst, *s_yin, *s_sgin]}

    class Waits:

        def __init__(self, e, ahead=False):
            self.e, self.t, self.ahead, self.starts = e, {}, ahead, {}

        def tally(self, s):
            if id(s) not in self.t:
                self.t[id(s)] = (Tally(self.starts.get(id(s), 0), 16 if id(s) in BY16 else 1), s)
            return self.t[id(s)][0]

        def due(self, s, skip=0):
            v = self.tally(s).next(skip)
            return self.e.to_reg(v) if self.ahead and not isinstance(v, int) else v

        def address(self, v, top):
            return self.e.snap(self.e.to_reg(v), min_val=0, max_val=top)

        def skip(self, s, n=1):
            self.tally(s).local += n

        @contextmanager
        def loop(self, n, rates, first=0):
            for s, _ in rates:
                self.tally(s)
            with self.e.Fori(first, first + n) as i:
                for s, r in rates:
                    self.tally(s).enter(i, r, first)
                yield i
                for s, r in rates:
                    self.tally(s).leave(n, first, s)

    def cols(i, n=P):
        return bass.ds(i, n)

    def halves(a):
        return a.rearrange("p (s c) -> p s c", s=2)

    def w_cols(w, col):
        return w.rearrange("(k p) c -> p k c", p=P)[:, :, bass.ds(col, P)]

    UNITS_ATT, UNITS_RET, UNITS_GATE = 10, 8, 4

    def att_cols(h):
        return [base + g * 1024 + h * P for base in (QA, KA, VA) for g in range(G)] + [ZA + h * P]

    def ret_cols(h):
        return [base + h * RK + j * P for base in (QR, KR, VR, ZR) for j in range(2)]

    def gate_cols(i):
        return [base + i * 2 * P + j * P for j in range(2) for base in (GA, GB)]

    def keep_rows(e, g, b, c):
        rows_kept = WIN[g] - 1
        chunk = {0: 1, 1: 4, 2: 16}[g]
        n = rows_kept * ROW // chunk
        src = caches[g][0].rearrange("b r k h d -> (b r k h d)")
        dst = wins[g][0].rearrange("b r k h d -> (b r k h d)")
        at = b * (WIN[g] * ROW) + c * n
        inner = n // P
        e.dma_start(dst[bass.ds(at, n)].rearrange("(p m n) -> p m n", p=16, n=inner),
                    src[bass.ds(at + ROW, n)].rearrange("(p m n) -> p m n", p=16, n=inner)).then_inc(s_copy, 16)
    N_COPIES = NS * (16 + 4 + 1)

    PT_BATCHES = {0: [(0, 3, 0, 1)], 1: [(0, 2, 0, 2), (2, 3, 0, 2)],
                  2: [(0, 1, 1, 3), (1, 2, 0, 3), (2, 3, 0, 3)],
                  3: [(0, 1, 2, 4), (1, 2, 0, 4), (2, 3, 0, 4)]}
    BATCHES = [(b, *q) for b in range(TB) for q in PT_BATCHES[b]]

    def prob_col(b, g, kb):
        w0, w = score_width(b)
        if g == 0:
            return (kb - max(b - 1, 0)) * P
        return w0 + (g - 1) * P * (b + 1) + kb * P

    block = stack.enter_context(nc.Block())

    @block.sync
    def _(sp):
        count = Waits(sp, ahead=True)
        for tb in range(TB):
            sp.dma_start(x_nat[:, tb, :], x_prompt[0, tb * P:(tb + 1) * P, :]).then_inc(s_xload[tb], 16)
            if tb == 0:
                sp.dma_start(ident[:], c_ident).then_inc(s_ident, 16)
        sp.dma_start(xs_nat[0:NS, :], x_sample[:, 0, :]).then_inc(s_xload[4], 16)
        sp.dma_start(p_nat, p_prompt[0, 0].rearrange("(t p) c -> p t c", p=P)).then_inc(s_xload[5], 16)
        sp.dma_start(ps_nat[0:NS, :], p_sample[0, :, 0, :]).then_inc(s_xload[5], 16)

        def load(slot, w, col, k=KD):
            v, col = count.due(s_wready), count.address(col, w.shape[1] - P)
            sp.wait_ge(s_begun, 1)
            sp.wait_ge(s_wready, v)
            sp.dma_start(raw[:, slot, 0:k, :], w_cols(w, col)).then_inc(s_wload[slot], 16)

        w0 = w_in[0]
        for u in range(2):
            sp.wait_ge(s_wready, count.due(s_wready))
            for k in range(2):
                sp.dma_start(raw[:, u].rearrange("p (n k) c -> p k n c", k=2)[:, k],
                             w_proj[0][k * P:(k + 1) * P, u * 8 * P:(u + 1) * 8 * P].rearrange("p (n c) -> p n c", c=P)
                             ).then_inc(s_wload[u], 16)
        with count.loop(H, [(s_wready, UNITS_ATT)]) as h:
            for j, c in enumerate(att_cols(h)):
                load(j % 2, w0, c)
                keep_rows(sp, 2, h, j)
        with count.loop(H, [(s_wready, UNITS_RET)]) as h:
            for j, c in enumerate(ret_cols(h)):
                load(j % 2, w0, c)
                if j < 6:
                    keep_rows(sp, 2, h, 10 + j)
                else:
                    keep_rows(sp, 1, h, j - 4)
        with count.loop(H, [(s_wready, UNITS_GATE)]) as i:
            for j, c in enumerate(gate_cols(i)):
                load(j % 2, w0, c)
        sp.wait_ge(s_skfree, 1 + NS)
        for n in range(H):
            sp.dma_start(y_in[:, n, 0:T], y_scr[n]).then_inc(s_yin[0], 16)
        with count.loop(KD // 2, [(s_wready, 2)]) as i:
            for j in range(2):
                load(j, w_a[0], i * 2 * P + j * P, H)
        with count.loop(KD // 2, [(s_wready, 2)]) as i:
            for j in range(2):
                load(j, w_r[0], i * 2 * P + j * P)
                if j == 0:
                    keep_rows(sp, 1, i, 0)
        with count.loop(KD // 2, [(s_wready, 2)]) as i:
            for j in range(2):
                load(j, w_o[0], i * 2 * P + j * P)
                if j == 0:
                    keep_rows(sp, 1, i, 1)
        with count.loop(KD // 2, [(s_wready, 2)]) as i:
            for j in range(2):
                load(j, w_gate[0], i * 2 * P + j * P)
                if j == 0:
                    keep_rows(sp, 0, i, 0)
        sp.wait_ge(s_copy, 16 * N_COPIES)

    @block.tensor
    def _(pe):
        count = Waits(pe)
        count.starts[id(s_wready)] = 2
        halfcols = [(0, HC), (HC, TC)]

        def unit(par, ks=range(KD), hooks=None, tiles_due=None):
            pe.wait_ge(s_wready, count.due(s_wready))
            pe.wait_ge(s_accfree[par], count.due(s_accfree[par]))
            passes = [(0, 0), (0, 1), (1, 0)]
            for k in ks:
                for f in (hooks or {}).get(k, ()):
                    f()
                if tiles_due and k in tiles_due:
                    pe.wait_ge(s_mov, count.due(s_mov, skip=tiles_due[k] - 1))
                for n, (wp, up) in enumerate(passes):
                    for half, (a, b) in enumerate(halfcols):
                        mm = pe.matmul(acc[:, par, half, 0:HC], W[:, par, wp, k, :], U[:, up, k, a:b],
                                       start=(k == ks[0] and n == 0), stop=(k == ks[-1] and n == 2))
            mm.then_inc(s_unit, 1)

        pe.wait_ge(s_ident, 16)
        fill = 0
        for tb in range(TB):
            pe.wait_ge(s_xload[tb], count.due(s_xload[tb]))
            for n0 in range(0, KD, 4):
                pe.wait_ge(s_free[fill % 4], count.due(s_free[fill % 4]))
                for n in range(4):
                    mm = pe.transpose(aux[:, fill % 4, n * P:(n + 1) * P],
                                      x_nat[:, tb, (n0 + n) * P:(n0 + n + 1) * P], ident[:])
                mm.then_inc(s_full[fill % 4], 1)
                fill += 1
        pe.wait_ge(s_xload[4], count.due(s_xload[4]))
        pe.wait_ge(s_free[0], count.due(s_free[0]))
        for n in range(KD):
            mm = pe.transpose(aux[:, 0, n * NS:(n + 1) * NS], xs_nat[0:NS, n * P:(n + 1) * P], ident[0:NS, 0:NS])
        mm.then_inc(s_full[0], 1)
        pe.wait_ge(s_xload[5], count.due(s_xload[5], skip=1))
        for j in range(2):
            pe.wait_ge(s_free[1 + j], count.due(s_free[1 + j]))
            for tb in range(TB):
                mm = pe.transpose(aux[:, 1 + j, tb * P:(tb + 1) * P], p_nat[:, tb, j * P:(j + 1) * P], ident[:])
            mm.then_inc(s_full[1 + j], 1)
        pe.wait_ge(s_free[3], count.due(s_free[3]))
        for j in range(2):
            mm = pe.transpose(aux[:, 3, j * NS:(j + 1) * NS], ps_nat[0:NS, j * P:(j + 1) * P], ident[0:NS, 0:NS])
        mm.then_inc(s_full[3], 1)

        def norm_sums(sq_now):
            pe.wait_ge(s_free[0], count.due(s_free[0]))
            pe.wait_ge(s_free[1], count.due(s_free[1]))
            for n in range(KD):
                pe.wait_ge(s_sq, count.due(s_sq))
                pe.matmul(aux[:, 0, 0:HC], mean_d[:], sq_now[:, n % 2, 0:HC], start=(n == 0), stop=(n == KD - 1))
                mm = pe.matmul(aux[:, 1, 0:HC], mean_d[:], sq_now[:, n % 2, HC:TC], start=(n == 0), stop=(n == KD - 1))
                mm.then_inc(s_sqfree if n < KD - 1 else s_full[0], 1)

        norm_sums(sq)
        for n in range(KD):
            if n % 8 == 0:
                pe.wait_ge(s_wready, count.due(s_wready))
            pe.wait_ge(s_accfree[n % 2], count.due(s_accfree[n % 2]))
            for k in range(2):
                for m, (wp, up) in enumerate([(0, 0), (0, 1), (1, 0)]):
                    for half, (a, b) in enumerate(halfcols):
                        mm = pe.matmul(acc[:, n % 2, half, 0:HC], W[:, n // 8, wp, 2 * (n % 8) + k, :],
                                       U[:, up, KD + k, a:b], start=(k == 0 and m == 0), stop=(k == 1 and m == 2))
            mm.then_inc(s_unit, 1)
        pe.wait_ge(s_mov, count.due(s_mov, skip=KD - 1))

        def head_rows(src, nth_skip, bank, ntb=TB):
            pe.wait_ge(s_zT, count.due(s_zT, nth_skip))
            pe.wait_ge(s_free[bank], count.due(s_free[bank]))
            for tb in range(ntb):
                mm = pe.transpose(aux[:, bank, tb * P:(tb + 1) * P], src[:, tb * P:(tb + 1) * P], ident[:])
            mm.then_inc(s_full[bank], 1)

        def scores(b):
            w0, w = score_width(b)
            wg = P * (b + 1)
            q = slice(b * P, (b + 1) * P)
            for g, (a, n) in enumerate([(max(b - 1, 0) * P, w0), (0, wg), (0, wg)]):
                pe.wait_ge(s_free[g], count.due(s_free[g]))
                pe.matmul(aux[:, g, 0:n], qT[:, g, q], kT[:, g, a:a + n], start=True, stop=True).then_inc(s_full[g], 1)

        def prob_turn(m):
            b, g0, g1, k0, k1 = BATCHES[m]
            if m == 0 or BATCHES[m - 1][0] != b:
                pe.wait_ge(s_prob, count.due(s_prob))
            pe.wait_ge(s_free[m % 3], count.due(s_free[m % 3]))
            at = 0
            for g in range(g0, g1):
                for kb in range(k0, k1):
                    c = prob_col(b, g, kb)
                    mm = pe.transpose(aux[:, m % 3, at:at + P], sc[b][:, c:c + P], ident[:])
                    at += P
            mm.then_inc(s_full[m % 3], 1)

        def values():
            pe.wait_ge(s_vnat, count.due(s_vnat, skip=2))
            pe.wait_ge(s_pt, count.due(s_pt, skip=len(BATCHES) - 1))
            pe.wait_ge(s_free[3], count.due(s_free[3]))
            parts = [(1, kb) for kb in range(TB)] + [(2, kb) for kb in range(TB)] + [(0, kb) for kb in range(TB)]
            for n, (g, kb) in enumerate(parts):
                a, z = kb * P, (min(kb + 2, TB) * P if g == 0 else T)
                mm = pe.matmul(aux[:, 3, a:z], v_nat[:, g, kb, :], PT[:, g, kb, a:z], start=(n == 0),
                               stop=(n == len(parts) - 1))
            mm.then_inc(s_full[3], 1)

        with count.loop(H, [(s_wready, 10), (s_accfree[0], 5), (s_accfree[1], 5), (s_zT, 9), (s_free[0], 7),
                        (s_free[1], 7), (s_free[2], 7), (s_free[3], 7), (s_prob, 4), (s_vnat, 3), (s_pt, 9)]) as h:
            hooks = {
                4: {8: [lambda: head_rows(kT[:, 0, :], 3, 3)]},
                5: {8: [lambda: head_rows(kT[:, 1, :], 0, 3)]},
                6: {2: [lambda: head_rows(kT[:, 2, :], 0, 3)], 4: [lambda: scores(0)], 8: [lambda: scores(1)],
                    12: [lambda: scores(2)]},
                7: {0: [lambda: scores(3)], 6: [lambda: head_rows(vT[:, 0, :], 0, 3)]},
                8: {2: [lambda: head_rows(vT[:, 1, :], 0, 3)], 6: [lambda: prob_turn(0)], 9: [lambda: prob_turn(1)],
                    12: [lambda: prob_turn(2)]},
                9: {0: [lambda: prob_turn(3)], 2: [lambda: head_rows(vT[:, 0, :], 0, 3)],
                    4: [lambda: prob_turn(4)], 6: [lambda: prob_turn(5)], 8: [lambda: prob_turn(6)],
                    10: [lambda: prob_turn(7)], 12: [lambda: prob_turn(8)], 15: [values]},
            }
            for j in range(UNITS_ATT):
                unit(j % 2, hooks=hooks.get(j))

        def ret_rows(src, j, nth_skip, bank):
            pe.wait_ge(s_zT, count.due(s_zT, nth_skip))
            pe.wait_ge(s_free[bank], count.due(s_free[bank]))
            for tb in range(TB):
                mm = pe.transpose(aux[:, bank, tb * P:(tb + 1) * P], src[:, j, tb * P:(tb + 1) * P], ident[:])
            mm.then_inc(s_full[bank], 1)

        def ret_scores(jb):
            bank = jb % 2
            pe.wait_ge(s_free[bank], count.due(s_free[bank]))
            for j in range(2):
                mm = pe.matmul(aux[:, bank, 0:T - jb * P], rk[:, j, jb * P:(jb + 1) * P], rq[:, j, jb * P:T],
                               start=(j == 0), stop=(j == 1))
            mm.then_inc(s_full[bank], 1)

        def ret_values(e):
            if e == 0:
                pe.wait_ge(s_sm, count.due(s_sm, skip=3))
                pe.wait_ge(s_vn, count.due(s_vn, skip=1))
            pe.wait_ge(s_free[2 + e], count.due(s_free[2 + e]))
            for jb in range(TB):
                mm = pe.matmul(aux[:, 2 + e, jb * P:T], vn[:, jb, e * P:(e + 1) * P], sm[jb], start=(jb == 0),
                               stop=(jb == TB - 1))
            mm.then_inc(s_full[2 + e], 1)

        def ret_state():
            pe.wait_ge(s_ks, count.due(s_ks, skip=1))
            pe.wait_ge(s_free[0], count.due(s_free[0]))
            for j in range(2):
                for jb in range(TB):
                    mm = pe.matmul(aux[:, 0, j * RK:(j + 1) * RK], ks[:, jb, j * P:(j + 1) * P], vn[:, jb, :],
                                   start=(jb == 0), stop=(jb == TB - 1))
            mm.then_inc(s_full[0], 1)

        def ret_norm():
            pe.wait_ge(s_sq, count.due(s_sq, skip=1))
            pe.wait_ge(s_free[1], count.due(s_free[1]))
            for e in range(2):
                mm = pe.matmul(aux[:, 1, :], mean_rk[:], rsq[:, e, :], start=(e == 0), stop=(e == 1))
            mm.then_inc(s_full[1], 1)

        with count.loop(H, [(s_wready, 8), (s_accfree[0], 4), (s_accfree[1], 4), (s_zT, 6), (s_free[0], 5),
                        (s_free[1], 5), (s_free[2], 1), (s_free[3], 1), (s_sm, 4), (s_vn, 2), (s_ks, 2),
                        (s_sq, 2)]) as h:
            hooks = {
                4: {4: [lambda: ret_rows(rk, 0, 2, 0)], 8: [lambda: ret_rows(rk, 1, 0, 1)]},
                5: {1: [lambda: ret_scores(0)], 5: [lambda: ret_scores(1)], 9: [lambda: ret_scores(2)],
                    13: [lambda: ret_scores(3)]},
                6: {2: [lambda: ret_rows(rv, 0, 0, 0)], 6: [lambda: ret_rows(rv, 1, 0, 1)]},
                7: {1: [lambda: ret_values(0)], 5: [lambda: ret_values(1)], 9: [ret_state], 13: [ret_norm]},
            }
            for j in range(UNITS_RET):
                unit(j % 2, hooks=hooks.get(j))

        for n in range(9):
            bank = n // 4
            if n % 4 == 0:
                pe.wait_ge(s_free[bank], count.due(s_free[bank]))
            mm = pe.transpose(aux[0:64, bank, (n % 4) * P:(n % 4 + 1) * P], zs[:, n * H * NS:(n + 1) * H * NS], ident[:])
            if n % 4 == 3 or n == 8:
                mm.then_inc(s_full[bank], 1)
        pe.wait_ge(s_free[3], count.due(s_free[3]))
        pe.transpose(aux[:, 3, 0:P], zs[:, VR // P * NS:(VR // P + 16) * NS], ident[:]).then_inc(s_full[3], 1)

        def sample_scores():
            pe.wait_ge(s_scol, count.due(s_scol))
            pe.wait_ge(s_free[0], count.due(s_free[0]))
            for g in range(G):
                at = g * (NK + 1)
                pe.transpose(aux[0:H, 0, at:at + NK], scol[:, g, :], ident[:])
                mm = pe.matmul(aux[0:H, 0, at + NK:at + NK + 1], qk[:, g, :], one[:, 0:1], start=True, stop=True)
            mm.then_inc(s_full[0], 1)

        def sample_probs():
            pe.wait_ge(s_sprob, count.due(s_sprob))
            pe.wait_ge(s_free[1], count.due(s_free[1]))
            for g in range(G):
                pe.matmul(aux[:, 1, (G + g) * H:(G + g + 1) * H], one[0:H, :], pdiag[:, g, :], start=True, stop=True)
                mm = pe.transpose(aux[:, 1, g * H:(g + 1) * H], srow[0:H, g, 0:NK], ident[0:H, 0:H])
            mm.then_inc(s_full[1], 1)

        def sample_values():
            pe.wait_ge(s_pcol, count.due(s_pcol))
            pe.wait_ge(s_sv, count.due(s_sv, skip=G - 1))
            pe.wait_ge(s_free[2], count.due(s_free[2]))
            for h in range(H):
                for g in range(G):
                    mm = pe.matmul(aux[:, 2, h:h + 1], s_v[:, g, h * HD:(h + 1) * HD], pcol[:, g, h:h + 1],
                                   start=(g == 0), stop=(g == G - 1))
            mm.then_inc(s_full[2], 1)

        def sample_states(half, i):
            pe.wait_ge(s_rnew, count.due(s_rnew))
            pe.wait_ge(s_free[3], count.due(s_free[3]))
            for h in range(HH):
                for e in range(2):
                    for j in range(2):
                        at = (QR // P + 2 * (half * HH + h) + j) * NS
                        mm = pe.matmul(aux[:, 3, 2 * h + e:2 * h + e + 1], r_st[:, half, h, j, e * P:(e + 1) * P],
                                       zs[:, bass.ds(at + i, 1)], start=(j == 0), stop=(j == 1))
            mm.then_inc(s_full[3], 1)

        with count.loop(H, [(s_wready, 4), (s_accfree[0], 2), (s_accfree[1], 2), (s_scol, 1), (s_sprob, 1),
                            (s_pcol, 1), (s_sv, G), (s_rnew, 2), (s_free[0], 1), (s_free[1], 1), (s_free[2], 1),
                            (s_free[3], 2)]) as i:
            hooks = {
                2: {2: [sample_scores], 12: [sample_probs]},
                3: {4: [lambda: sample_states(0, i)], 10: [sample_values], 15: [lambda: sample_states(1, i)]},
            }
            for j in range(UNITS_GATE):
                unit(j % 2, hooks=hooks.get(j))

        rates = [(s_wready, 2), (s_accfree[0], 1), (s_accfree[1], 1)]

        def sample_norm():
            pe.wait_ge(s_ssq, count.due(s_ssq))
            pe.wait_ge(s_free[2], count.due(s_free[2]))
            for e in range(2):
                mm = pe.matmul(aux[:, 2, 0:64], mean_rk[:], ssq[:, :, :].rearrange("p (h e) b -> p e h b", e=2)[:, e],
                               start=(e == 0), stop=(e == 1))
            mm.then_inc(s_full[2], 1)

        att_ks = list(range(H))
        unit(0, att_ks, tiles_due={k: 1 for k in att_ks})
        unit(1, att_ks, hooks={0: [sample_norm]})
        with count.loop(KD // 2 - 1, rates, first=1) as i:
            for j in range(2):
                unit(j, att_ks)
        ret_ks = list(range(8, KD)) + list(range(8))
        unit(0, ret_ks, tiles_due={8: 8, **{k: 1 for k in range(8)}})
        unit(1, ret_ks)
        with count.loop(KD // 2 - 1, rates, first=1) as i:
            for j in range(2):
                unit(j, ret_ks)
        unit(0, tiles_due={k: 1 for k in range(KD)})
        unit(1)
        with count.loop(KD // 2 - 1, rates, first=1) as i:
            for j in range(2):
                unit(j)
        pe.wait_ge(s_sqsum, 1)
        pe.wait_ge(s_free[0], count.due(s_free[0]))
        pe.wait_ge(s_free[1], count.due(s_free[1]))
        pe.matmul(aux[:, 0, 0:HC], mean_d[:], sqsum[:, 0:HC], start=True, stop=True)
        pe.matmul(aux[:, 1, 0:HC], mean_d[:], sqsum[:, HC:TC], start=True, stop=True).then_inc(s_full[0], 1)

        def out_turn(slot):
            pe.wait_ge(s_out, count.due(s_out))
            pe.wait_ge(s_free[slot], count.due(s_free[slot]))
            for tb in range(TB):
                mm = pe.transpose(aux[:, slot, tb * P:(tb + 1) * P], outT[:, slot, tb * P:(tb + 1) * P], ident[:])
            mm.then_inc(s_full[slot], 1)

        unit(0, tiles_due={k: 1 for k in range(KD)})
        unit(1, hooks={8: [lambda: out_turn(0)]})
        with count.loop(KD // 2 - 1, [*rates, (s_out, 2), (s_free[0], 1), (s_free[1], 1)], first=1) as i:
            for j in range(2):
                unit(j, hooks={8: [lambda: out_turn(1 - j)]})
        out_turn(1)
        pe.wait_ge(s_os, count.due(s_os))
        for n in range(KD):
            if n % 4 == 0:
                pe.wait_ge(s_free[n // 4], count.due(s_free[n // 4]))
            mm = pe.transpose(aux[0:NS, n // 4, (n % 4) * P:(n % 4 + 1) * P], outS[:, n * NS:(n + 1) * NS], ident[:])
            if n % 4 == 3:
                mm.then_inc(s_full[n // 4], 1)

    @block.scalar
    def _(act):
        count = Waits(act)

        def hi(par, k=KD, loads=1):
            act.wait_ge(s_wload[par], count.due(s_wload[par], skip=loads - 1))
            act.activation(W[:, par, 0, 0:k], raw[:, par, 0:k], ACT.Copy).then_inc(s_whi, 1)

        act.sem_inc(s_accfree[0], 1)
        act.sem_inc(s_accfree[1], 1)
        for b in range(4):
            act.sem_inc(s_free[b], 1)

        for tb in range(TB):
            for q in range(4):
                if q % 2 == 0:
                    act.wait_ge(s_full[q], count.due(s_full[q]))
                    act.activation(xT[:, 4 * q:4 * q + 4, tb * P:(tb + 1) * P],
                                   aux[:, q, :].rearrange("p (n c) -> p n c", n=4), ACT.Copy).then_inc(s_free[q], 1)
                else:
                    count.skip(s_full[q])
        act.wait_ge(s_full[0], count.due(s_full[0]))
        act.activation(xT[:, :, T:TC], aux[:, 0, 0:P].rearrange("p (n c) -> p n c", n=KD), ACT.Copy).then_inc(s_free[0], 1)
        for j in range(2):
            act.wait_ge(s_full[1 + j], count.due(s_full[1 + j]))
            act.activation(U[:, 0, KD + j, 0:T], aux[:, 1 + j, :], ACT.Copy).then_inc(s_uhi, 1)
        act.wait_ge(s_full[3], count.due(s_full[3]))
        act.activation(U[:, 0, KD:KD + 2, T:TC], aux[:, 3, 0:2 * NS].rearrange("p (n c) -> p n c", n=2),
                       ACT.Copy).then_inc(s_uhi, 1)
        act.drain().then_inc(s_xt, 1)
        hi(0, loads=2)
        hi(1, loads=2)

        def squares(src, dst):
            for n in range(KD):
                if n >= 2:
                    act.wait_ge(s_sqfree, count.due(s_sqfree))
                act.activation(dst[:, n % 2, :], src[:, n, :], ACT.Square).then_inc(s_sq, 1)
            count.skip(s_sqfree, 1)

        def std(dst):
            act.wait_ge(s_full[0], count.due(s_full[0]))
            act.activation(dst[:, 0:HC], aux[:, 0, 0:HC], ACT.Sqrt, bias=eps[:, 0:1]).then_inc(s_free[0], 1)
            act.activation(dst[:, HC:TC], aux[:, 1, 0:HC], ACT.Sqrt, bias=eps[:, 0:1]).then_inc(s_free[1], 1)
            act.drain().then_inc(s_std, 1)

        act.wait_ge(s_xt, count.due(s_xt, skip=1))
        squares(xT, sq)
        std(rstd)
        for n in range(KD):
            act.wait_ge(s_u, count.due(s_u))
            act.activation(U[:, 0, n, :], utmp[:, n % 2, :], ACT.Copy).then_inc(s_uhi, 1)
            act.wait_ge(s_unit, count.due(s_unit))
            act.wait_ge(s_ppfree[n % 2], count.due(s_ppfree[n % 2]))
            act.activation(halves(pp_out[:, n % 2, :]), acc[:, n % 2, :, 0:HC], ACT.Copy).then_inc(s_accfree[n % 2], 1)
            act.drain().then_inc(s_pp, 1)
            if n % 8 == 7:
                hi(n // 8)
        act.wait_ge(s_xtst, 16 * KD)
        for q in range(2):
            act.wait_ge(s_ppfree[q], count.due(s_ppfree[q]))

        def head_tile(par, dst, tile, ready, func=ACT.Copy, scale=1.0):
            act.wait_ge(s_unit, count.due(s_unit))
            act.activation(halves(dst), acc[:, par, :, 0:HC], func, scale=scale).then_inc(ready, 1)
            act.activation(zs[:, bass.ds(tile * NS, NS)], acc[:, par, 1, HC - NS:HC], func,
                           scale=scale).then_inc(s_accfree[par], 1)

        def exps(b):
            act.wait_ge(s_max, count.due(s_max))
            act.activation(sc[b], sc[b], ACT.Exp, bias=negmax[:, b:b + 1], accum_out=den[:, b:b + 1]).then_inc(s_exp, 1)

        def prob_copy(m):
            b, g0, g1, k0, k1 = BATCHES[m]
            act.wait_ge(s_full[m % 3], count.due(s_full[m % 3]))
            ng, nk = g1 - g0, k1 - k0
            src = aux[:, m % 3, 0:ng * nk * P].rearrange("p (g k c) -> p g k c", g=ng, k=nk)
            act.activation(PT[:, g0:g1, k0:k1, b * P:(b + 1) * P], src, ACT.Copy).then_inc(s_free[m % 3], 1)
            act.drain().then_inc(s_pt, 1)

        with count.loop(H, [(s_unit, 10), (s_wload[0], 5), (s_wload[1], 5), (s_max, 4), (s_full[0], 7), (s_full[1], 7),
                        (s_full[2], 7), (s_full[3], 7)]) as h:
            for j in range(UNITS_ATT):
                par = j % 2
                if j == 6:
                    for b in range(3):
                        exps(b)
                if j == 7:
                    exps(3)
                    for g in range(G):
                        count.skip(s_full[g], 4)
                if j == 8:
                    for m in range(3):
                        prob_copy(m)
                if j == 9:
                    for m in range(3, 9):
                        prob_copy(m)
                    count.skip(s_full[3], 7)
                g = j % 3
                if j < 3:
                    head_tile(par, qT[:, g, :], QA // P + g * H + h, s_zT, scale=HD ** -0.5)
                elif j < 6:
                    head_tile(par, kT[:, g, :], KA // P + g * H + h, s_zT)
                elif j < 9:
                    head_tile(par, vT[:, g % 2, :], VA // P + g * H + h, s_zT)
                else:
                    head_tile(par, silu_z[:, 0, :], ZA // P + h, s_z, ACT.Silu)
                hi(par)

        with count.loop(H, [(s_unit, 8), (s_wload[0], 4), (s_wload[1], 4), (s_full[0], 5), (s_full[1], 5),
                        (s_full[2], 1), (s_full[3], 1)]) as h:
            for j in range(UNITS_RET):
                par = j % 2
                if j == 7:
                    for e in range(2):
                        act.wait_ge(s_full[2 + e], count.due(s_full[2 + e]))
                        act.activation(rsq[:, e, :], aux[:, 2 + e, :], ACT.Square).then_inc(s_sq, 1)
                    count.skip(s_full[0], 5)
                    act.wait_ge(s_full[1], count.due(s_full[1], skip=4))
                    act.activation(rrs, aux[:, 1, :], ACT.Sqrt, bias=eps[:, 0:1]).then_inc(s_free[1], 1)
                    act.drain().then_inc(s_rstd, 1)
                dst = (rq, rk, rv, rz)[j // 2][:, par, :]
                tile = (QR, KR, VR, ZR)[j // 2] // P + 2 * h + par
                if j < 6:
                    head_tile(par, dst, tile, s_zT, scale=RK ** -0.5 if j // 2 == 1 else 1.0)
                else:
                    head_tile(par, dst, tile, s_z, ACT.Silu)
                hi(par)

        act.wait_ge(s_stfree, H + 1)
        act.wait_ge(s_ytfree, H + 1)
        count.skip(s_full[0], 1)
        count.skip(s_full[1], 1)
        count.skip(s_full[2], 1)
        count.skip(s_full[3], 1)

        def scaled_states(half):
            act.wait_ge(s_rst[half], count.due(s_rst[half], skip=1))
            for h in range(HH):
                a = act.activation(r_st[:, half, h], r_st[:, half, h], ACT.Copy, scale=gamma[half * HH + h])
            a.then_inc(s_rgam, 1)

        with count.loop(H, [(s_unit, 4), (s_wload[0], 2), (s_wload[1], 2), (s_sgfree[0], 2), (s_sgfree[1], 2),
                            (s_smax, 1), (s_rst[0], 2), (s_rst[1], 2)]) as i:
            for j in range(UNITS_GATE):
                par = j % 2
                if j == 2:
                    scaled_states(0)
                    act.wait_ge(s_smax, count.due(s_smax))
                    act.activation(srow[0:H], srow[0:H], ACT.Exp, bias=negmax[0:H, 0:1],
                                   accum_out=den[0:H, 0:1]).then_inc(s_sexp, 1)
                if j == 3:
                    scaled_states(1)
                act.wait_ge(s_unit, count.due(s_unit))
                act.wait_ge(s_sgfree[par], count.due(s_sgfree[par]))
                act.activation(halves(sg_out[:, par, :]), acc[:, par, :, 0:HC], ACT.Sigmoid).then_inc(s_accfree[par], 1)
                act.drain().then_inc(s_sg, 1)
                hi(par)

        def y_tile(n):
            act.activation(U[:, 0, bass.ds(n, 1), 0:T], y_in[:, bass.ds(n, 1), 0:T], ACT.Copy).then_inc(s_uhi, 1)

        def sampled_tiles(first, at, n):
            act.activation(U[:, 0, at:at + n, T:TC], ysmp[:, first:first + n, :], ACT.Copy).then_inc(s_uhi, 1)

        proj_rates = [(s_unit, 2), (s_wload[0], 1), (s_wload[1], 1)]
        act.wait_ge(s_ysmp, count.due(s_ysmp))
        sampled_tiles(0, 0, H)
        act.wait_ge(s_yin[0], 16 * H)
        for n in range(H):
            y_tile(n)
        for j in range(2):
            act.wait_ge(s_unit, count.due(s_unit))
            hi(j, H)
        count.skip(s_full[0], H)
        count.skip(s_full[1], H)
        act.wait_ge(s_full[2], count.due(s_full[2], skip=H))
        act.activation(srs, aux[:, 2, 0:64], ACT.Sqrt, bias=eps[:, 0:1]).then_inc(s_free[2], 1)
        count.skip(s_full[3], 2 * H)
        act.drain().then_inc(s_sstd, 1)
        act.wait_ge(s_yin[1], 16 * 8)
        y_tile(8)
        with count.loop(KD // 2 - 2, proj_rates, first=1) as i:
            y_tile(8 + i)
            for j in range(2):
                act.wait_ge(s_unit, count.due(s_unit))
                hi(j, H)
        act.wait_ge(s_ysmp, count.due(s_ysmp))
        sampled_tiles(H + 8, 8, 8)
        y_tile(KD - 1)
        for j in range(2):
            act.wait_ge(s_unit, count.due(s_unit))
            hi(j)
        sampled_tiles(H, 0, 8)
        act.wait_ge(s_yin[2], 16 * 8)
        for n in range(8):
            y_tile(n)
        with count.loop(KD // 2, proj_rates) as i:
            for j in range(2):
                act.wait_ge(s_unit, count.due(s_unit))
                hi(j)
        for n in range(KD):
            act.wait_ge(s_m, count.due(s_m))
            act.activation(U[:, 0, n, :], M[:, n, :], ACT.Copy).then_inc(s_uhi, 1)
        mflat = M.rearrange("p n c -> p (n c)")
        with count.loop(KD // 2, [*proj_rates, (s_sqadd, 2)]) as i:
            for j in range(2):
                act.wait_ge(s_unit, count.due(s_unit))
                act.activation(halves(mflat[:, bass.ds((2 * i + j) * TC, TC)]), acc[:, j, :, 0:HC], ACT.Copy)
                act.wait_ge(s_sqadd, count.due(s_sqadd))
                act.activation(halves(sqb[:, j, :]), acc[:, j, :, 0:HC], ACT.Square).then_inc(s_accfree[j], 1)
                act.drain().then_inc(s_sq, 1)
                hi(j)
        std(nrs)
        for n in range(KD):
            act.wait_ge(s_h, count.due(s_h))
            act.activation(U[:, 0, n, :], X[:, n, :], ACT.Copy).then_inc(s_uhi, 1)

        def ple_out(slot):
            act.wait_ge(s_full[slot], count.due(s_full[slot]))
            act.wait_ge(s_ofree[slot], count.due(s_ofree[slot]))
            act.activation(onat[:, slot, :], aux[:, slot, :], ACT.Copy).then_inc(s_free[slot], 1)
            act.drain().then_inc(s_onat, 1)

        def ple(first, last):
            for j in range(2):
                if not (first and j == 0):
                    ple_out(1 - j)
                act.wait_ge(s_unit, count.due(s_unit))
                act.activation(halves(sgt), acc[:, j, :, 0:HC], ACT.Sigmoid).then_inc(s_accfree[j], 1)
                act.drain().then_inc(s_sgt, 1)
                if not last:
                    hi(j)

        ple(True, False)
        with count.loop(KD // 2 - 2, [*proj_rates, (s_full[0], 1), (s_full[1], 1), (s_ofree[0], 1), (s_ofree[1], 1)],
                        first=1) as i:
            ple(False, False)
        ple(False, True)
        ple_out(1)
        for q in range(4):
            act.wait_ge(s_full[q], count.due(s_full[q]))
            a = act.activation(osr[0:NS, q, 0:T], aux[0:NS, q, :], ACT.Copy)
        a.then_inc(s_osrow, 1)

    @block.vector
    def _(dve):
        count = Waits(dve)

        def lo(par, k=KD):
            dve.wait_ge(s_whi, count.due(s_whi))
            dve.tensor_tensor(W[:, par, 1, 0:k], raw[:, par, 0:k], W[:, par, 0, 0:k].bitcast(F32),
                              ALU.subtract).then_inc(s_wready, 1)

        dve.sem_inc(s_wready, 2)
        dve.sem_inc(s_skfree, 1)
        dve.sem_inc(s_svfree, 1)
        dve.sem_inc(s_rhalf, 2)
        dve.sem_inc(s_sqadd, 2)
        dve.memset(mean_rk[:], 1.0 / RK)
        dve.memset(one[:], 1.0)
        dve.memset(eps, EPS)
        dve.memset(mean_d[:], 1.0 / D)
        for tb in range(TB):
            for q in range(4):
                if q % 2 == 1:
                    dve.wait_ge(s_full[q], count.due(s_full[q]))
                    dve.tensor_copy(xT[:, 4 * q:4 * q + 4, tb * P:(tb + 1) * P],
                                    aux[:, q, :].rearrange("p (n c) -> p n c", n=4)).then_inc(s_free[q], 1)
                else:
                    count.skip(s_full[q])
        count.skip(s_full[0], 1)
        dve.drain()
        for j in range(2):
            count.skip(s_full[1 + j], 1)
            dve.wait_ge(s_uhi, count.due(s_uhi))
            dve.tensor_tensor(U[:, 1, KD + j, 0:T], aux[:, 1 + j, :], U[:, 0, KD + j, 0:T].bitcast(F32),
                              ALU.subtract).then_inc(s_free[1 + j], 1)
        count.skip(s_full[3], 1)
        dve.wait_ge(s_uhi, count.due(s_uhi))
        dve.tensor_tensor(U[:, 1, KD:KD + 2, T:TC], aux[:, 3, 0:2 * NS].rearrange("p (n c) -> p n c", n=2),
                          U[:, 0, KD:KD + 2, T:TC].bitcast(F32), ALU.subtract).then_inc(s_free[3], 1)
        dve.drain().then_inc(s_xt, 1)
        lo(0)
        lo(1)
        dve.wait_ge(s_std, count.due(s_std))
        count.skip(s_full[0], 1)
        dve.reciprocal(rstd, rstd)
        dve.drain()
        dve.wait_ge(s_const, 5 * 16)
        for n in range(KD):
            dve.scalar_tensor_tensor(out=utmp[:, n % 2, :], in0=xT[:, n, :], scalar=gpre[:, n:n + 1], in1=rstd,
                                     op0=ALU.mult, op1=ALU.mult).then_inc(s_u, 1)
            dve.wait_ge(s_uhi, count.due(s_uhi))
            dve.wait_ge(s_u, count.due(s_u))
            dve.tensor_tensor(U[:, 1, n, :], utmp[:, n % 2, :], U[:, 0, n, :].bitcast(F32),
                              ALU.subtract).then_inc(s_mov, 1)
            if n == 10:
                lo(0)
        lo(1)
        count.skip(s_unit, KD)

        def rows_copy(dst, ready, free):
            dve.wait_ge(s_full[3], count.due(s_full[3]))
            dve.wait_ge(free, count.due(free))
            dve.tensor_copy(dst, aux[:, 3, :].rearrange("p (t c) -> p t c", t=TB)).then_inc(s_free[3], 1)
            dve.drain().then_inc(ready, 1)

        def masked(b, h):
            w0, w = score_width(b)
            wg = P * (b + 1)
            parts = [(0, w0, 256 - w0), (w0, wg, 256 + T - wg), (w0 + wg, wg, 256 + 2 * T - wg)]
            for g, (at, n, tab) in enumerate(parts):
                dve.wait_ge(s_full[g], count.due(s_full[g]))
                dve.scalar_tensor_tensor(out=sc[b][:, at:at + n], in0=dist[:, tab:tab + n],
                                         scalar=nslope[:, bass.ds(h + g * H, 1)], in1=aux[:, g, 0:n],
                                         op0=ALU.mult, op1=ALU.add).then_inc(s_free[g], 1)
            dve.drain()
            dve.reduce_max(negmax[:, b:b + 1], sc[b], AX.X)
            dve.drain()
            dve.tensor_scalar(negmax[:, b:b + 1], negmax[:, b:b + 1], -1.0, None, ALU.mult).then_inc(s_max, 1)

        def normed(b):
            dve.wait_ge(s_exp, count.due(s_exp))
            dve.reciprocal(rden[:, b:b + 1], den[:, b:b + 1])
            dve.drain()
            dve.tensor_scalar(sc[b], sc[b], rden[:, b:b + 1], None, ALU.mult).then_inc(s_prob, 1)

        dve.wait_ge(s_dist, count.due(s_dist))
        with count.loop(H, [(s_whi, 10), (s_full[0], 7), (s_full[1], 7), (s_full[2], 7), (s_full[3], 7), (s_exp, 4),
                        (s_kfree[0], 1), (s_kfree[1], 1), (s_kfree[2], 1), (s_vfree[0], 1), (s_vfree[1], 1), (s_vfree[2], 1),
                        (s_z, 1), (s_yafree, 1)]) as h:
            for j in range(UNITS_ATT):
                if j in (4, 5, 6):
                    rows_copy(k_nat[:, j - 4], s_knat, s_kfree[j - 4])
                if j == 6:
                    masked(0, h)
                    masked(1, h)
                    normed(0)
                    masked(2, h)
                    normed(1)
                if j == 7:
                    masked(3, h)
                    for g in range(G):
                        count.skip(s_full[g], 3)
                    normed(2)
                    rows_copy(v_nat[:, 0], s_vnat, s_vfree[0])
                    normed(3)
                if j == 8:
                    rows_copy(v_nat[:, 1], s_vnat, s_vfree[1])
                if j == 9:
                    rows_copy(v_nat[:, 2], s_vnat, s_vfree[2])
                lo(j % 2)
            dve.wait_ge(s_full[3], count.due(s_full[3]))
            dve.wait_ge(s_z, count.due(s_z))
            dve.wait_ge(s_yafree, count.due(s_yafree))
            dve.tensor_tensor(ya_out, aux[:, 3, :], silu_z[:, 0, 0:T], ALU.mult).then_inc(s_free[3], 1)
            dve.drain().then_inc(s_ya, 1)
        count.skip(s_unit, 10 * H)

        for g in range(G):
            dve.wait_ge(s_kfree[g], count.due(s_kfree[g]))
            dve.wait_ge(s_vfree[g], count.due(s_vfree[g]))
        dve.wait_ge(s_yafree, count.due(s_yafree))
        dve.wait_ge(s_decay, count.due(s_decay))
        decayf = decay.rearrange("p h c -> p (h c)")
        with count.loop(H, [(s_whi, 8), (s_full[0], 5), (s_full[1], 5), (s_full[2], 1), (s_full[3], 1), (s_z, 2),
                        (s_rstd, 1), (s_stfree, 1), (s_ytfree, 1)]) as h:
            for j in range(UNITS_RET):
                if j == 4:
                    for d in range(2):
                        dve.wait_ge(s_full[d], count.due(s_full[d]))
                        for tb in range(TB):
                            a = dve.tensor_scalar(ks[:, tb, d * P:(d + 1) * P], aux[:, d, tb * P:(tb + 1) * P],
                                                  kdec[:, bass.ds(h * TB + tb, 1)], None, ALU.mult)
                        a.then_inc(s_free[d], 1)
                        dve.drain().then_inc(s_ks, 1)
                if j == 5:
                    for jb in range(TB):
                        dve.wait_ge(s_full[jb % 2], count.due(s_full[jb % 2]))
                        dve.tensor_tensor(sm[jb], aux[:, jb % 2, 0:T - jb * P], decayf[:, bass.ds(h * T, T - jb * P)],
                                          ALU.mult).then_inc(s_free[jb % 2], 1)
                        dve.drain().then_inc(s_sm, 1)
                if j == 6:
                    for e in range(2):
                        dve.wait_ge(s_full[e], count.due(s_full[e]))
                        dve.tensor_copy(vn[:, :, e * P:(e + 1) * P],
                                        aux[:, e, :].rearrange("p (t c) -> p t c", t=TB)).then_inc(s_free[e], 1)
                        dve.drain().then_inc(s_vn, 1)
                if j == 7:
                    dve.wait_ge(s_full[0], count.due(s_full[0]))
                    dve.wait_ge(s_stfree, count.due(s_stfree))
                    dve.tensor_copy(st, aux[:, 0, :].rearrange("p (j c) -> p j c", j=2)).then_inc(s_free[0], 1)
                    dve.drain().then_inc(s_st, 1)
                lo(j % 2)
            dve.wait_ge(s_full[1], count.due(s_full[1]))
            dve.wait_ge(s_rstd, count.due(s_rstd))
            dve.wait_ge(s_z, count.due(s_z, skip=1))
            dve.wait_ge(s_ytfree, count.due(s_ytfree))
            dve.reciprocal(rrs, rrs)
            dve.drain()
            for e in range(2):
                dve.wait_ge(s_full[2 + e], count.due(s_full[2 + e]))
                dve.scalar_tensor_tensor(out=yt[:, e, :], in0=aux[:, 2 + e, :], scalar=gret[:, bass.ds(2 * h + e, 1)],
                                         in1=rrs, op0=ALU.mult, op1=ALU.mult).then_inc(s_free[2 + e], 1)
            dve.drain()
            for e in range(2):
                dve.tensor_tensor(yt[:, e, :], yt[:, e, :], rz[:, e, 0:T], ALU.mult).then_inc(s_yt, 1)
        count.skip(s_unit, 8 * H)

        dve.wait_ge(s_stfree, count.due(s_stfree))
        dve.wait_ge(s_ytfree, count.due(s_ytfree))
        for bank, n in ((0, 4), (1, 4), (2, 1)):
            dve.wait_ge(s_full[bank], count.due(s_full[bank]))
            dve.tensor_copy(rows[0:64, bank * 4:bank * 4 + n, :],
                            aux[0:64, bank, 0:n * P].rearrange("p (n c) -> p n c", n=n)).then_inc(s_free[bank], 1)
        dve.wait_ge(s_full[3], count.due(s_full[3]))
        dve.tensor_copy(vrow, aux[:, 3, 0:P]).then_inc(s_free[3], 1)
        dve.drain().then_inc(s_rows, 1)
        zg = zs[:].rearrange("p (t b) -> p t b", b=NS)

        def flat(a):
            return a.rearrange("p g c -> p (g c)")

        def token(first, n, i):
            return zg[:, first:first + n, bass.ds(i, 1)]

        def column(a):
            return a.rearrange("p (t o) -> p t o", o=1)

        def sample_keys(i):
            dve.wait_ge(s_sk, count.due(s_sk, skip=G))
            dve.tensor_tensor(s_k, s_k, s_q, ALU.mult)
            dve.tensor_tensor(column(flat(qk)), token(0, G * H, i), token(KA // P, G * H, i), ALU.mult)
            dve.drain()
            dve.tensor_reduce(scol, s_k.rearrange("p g (h d) -> p g h d", h=H), AX.X, ALU.add).then_inc(s_skfree, 1)
            dve.drain().then_inc(s_scol, 1)

        def sample_softmax():
            dve.wait_ge(s_full[0], count.due(s_full[0]))
            dve.tensor_tensor(flat(srow)[0:H], aux[0:H, 0, 0:G * (NK + 1)], flat(sbias)[0:H], ALU.add).then_inc(s_free[0], 1)
            dve.drain()
            dve.reduce_max(negmax[0:H, 0:1], flat(srow)[0:H], AX.X)
            dve.drain()
            dve.tensor_scalar(negmax[0:H, 0:1], negmax[0:H, 0:1], -1.0, None, ALU.mult).then_inc(s_smax, 1)

        def sample_normed():
            dve.wait_ge(s_sexp, count.due(s_sexp))
            dve.reciprocal(rden[0:H, 0:1], den[0:H, 0:1])
            dve.drain()
            dve.tensor_scalar(srow[0:H], srow[0:H], rden[0:H, 0:1], None, ALU.mult)
            dve.drain()
            for g in range(G):
                dve.tensor_scalar(pdiag[:, g, :], ident[0:H, 0:H], srow[0:H, g, NK:NK + 1], None, ALU.mult)
            dve.drain().then_inc(s_sprob, 1)

        def sample_columns(i):
            dve.wait_ge(s_full[1], count.due(s_full[1]))
            dve.tensor_copy(flat(pcol), aux[:, 1, 0:G * H])
            dve.tensor_tensor(column(flat(spv)), column(aux[:, 1, G * H:2 * G * H]), token(VA // P, G * H, i),
                              ALU.mult).then_inc(s_free[1], 1)
            dve.drain().then_inc(s_pcol, 1)
            dve.tensor_tensor(oself, spv[:, 0, :], spv[:, 1, :], ALU.add)
            dve.drain()
            dve.tensor_tensor(oself, oself, spv[:, 2, :], ALU.add)

        def sample_output(i):
            dve.wait_ge(s_full[2], count.due(s_full[2]))
            dve.tensor_tensor(oself, aux[:, 2, 0:H], oself, ALU.add).then_inc(s_free[2], 1)
            dve.drain()
            dve.tensor_tensor(ysmp[:, 0:H, bass.ds(i, 1)], column(oself), token(ZA // P, H, i), ALU.mult).then_inc(s_svfree, 1)

        def sample_states(half, i):
            dve.wait_ge(s_rgam, count.due(s_rgam))
            for h in range(HH):
                for j in range(2):
                    at = (KR // P + 2 * (half * HH + h) + j) * NS
                    dve.scalar_tensor_tensor(out=r_st[:, half, h, j, :], in0=r_v[:, half, h, :],
                                             scalar=zs[:, bass.ds(at + i, 1)],
                                             in1=r_st[:, half, h, j, :], op0=ALU.mult, op1=ALU.add)
            dve.drain().then_inc(s_rnew, 1)

        def sample_ret_y(half, i):
            dve.wait_ge(s_full[3], count.due(s_full[3]))
            dve.tensor_copy(ysr[:, half * H:(half + 1) * H, bass.ds(i, 1)], column(aux[:, 3, 0:H])).then_inc(s_free[3], 1)
            dve.drain().then_inc(s_rhalf, 1)

        with count.loop(H, [(s_whi, 4), (s_sk, G + 1), (s_full[0], 1), (s_full[1], 1), (s_full[2], 1), (s_full[3], 2),
                            (s_sexp, 1), (s_rgam, 2)]) as i:
            for j in range(UNITS_GATE):
                if j == 1:
                    sample_keys(i)
                if j == 2:
                    sample_softmax()
                    sample_states(0, i)
                    sample_normed()
                    sample_columns(i)
                if j == 3:
                    sample_states(1, i)
                    sample_ret_y(0, i)
                    sample_output(i)
                    sample_ret_y(1, i)
                lo(j % 2)
        dve.drain().then_inc(s_ysmp, 1)
        count.skip(s_unit, 4 * H)

        def y_tile(n):
            dve.wait_ge(s_uhi, count.due(s_uhi))
            dve.tensor_tensor(U[:, 1, bass.ds(n, 1), 0:T], y_in[:, bass.ds(n, 1), 0:T],
                              U[:, 0, bass.ds(n, 1), 0:T].bitcast(F32), ALU.subtract).then_inc(s_mov, 1)

        def sampled_tiles(first, at, n):
            dve.wait_ge(s_uhi, count.due(s_uhi))
            dve.tensor_tensor(U[:, 1, at:at + n, T:TC], ysmp[:, first:first + n, :],
                              U[:, 0, at:at + n, T:TC].bitcast(F32), ALU.subtract)

        mflat = M.rearrange("p n c -> p (n c)")
        proj_rates = [(s_unit, 2), (s_whi, 2), (s_sgin[0], 1), (s_sgin[1], 1)]

        def att_unit(i, j, k):
            dve.wait_ge(s_unit, count.due(s_unit))
            dve.wait_ge(s_sgin[j], count.due(s_sgin[j]))
            dve.tensor_tensor(halves(mflat[:, bass.ds((2 * i + j) * TC, TC)]), acc[:, j, :, 0:HC],
                              halves(sg_in[:, j, :]), ALU.mult).then_inc(s_accfree[j], 1)
            lo(j, k)

        sampled_tiles(0, 0, H)
        for n in range(H):
            y_tile(n)
        dve.drain().then_inc(s_yinfree, 1)
        dve.tensor_tensor(ssq, ysr, ysr, ALU.mult).then_inc(s_ssq, 1)
        for j in range(2):
            att_unit(0, j, H)
        dve.wait_ge(s_full[2], count.due(s_full[2]))
        dve.wait_ge(s_sstd, count.due(s_sstd))
        dve.reciprocal(srs, srs)
        for tile in range(2 * H):
            dve.tensor_scalar(yg[:, tile, :], zg[:, ZR // P + tile, :], gret[:, tile:tile + 1], None, ALU.mult)
        dve.drain()
        dve.tensor_tensor(yg, yg, ysr, ALU.mult)
        dve.drain()
        for e in range(2):
            dve.tensor_tensor(ysmp[:, H:NYT, :].rearrange("p (h e) b -> p e h b", e=2)[:, e],
                              yg.rearrange("p (h e) b -> p e h b", e=2)[:, e],
                              srs.rearrange("p (h b) -> p h b", b=NS), ALU.mult)
        dve.drain().then_inc(s_ysmp, 1)
        y_tile(8)
        with count.loop(KD // 2 - 2, [*proj_rates, (s_uhi, 1)], first=1) as i:
            y_tile(8 + i)
            for j in range(2):
                att_unit(i, j, H)
        sampled_tiles(H + 8, 8, 8)
        y_tile(KD - 1)
        for j in range(2):
            att_unit(KD // 2 - 1, j, KD)
        sampled_tiles(H, 0, 8)
        for n in range(8):
            y_tile(n)
        dve.drain().then_inc(s_yinfree, 1)
        with count.loop(KD // 2, proj_rates) as i:
            for j in range(2):
                dve.wait_ge(s_unit, count.due(s_unit))
                dve.wait_ge(s_sgin[j], count.due(s_sgin[j]))
                dve.tensor_tensor(halves(tmp), acc[:, j, :, 0:HC], halves(sg_in[:, j, :]),
                                  ALU.mult).then_inc(s_accfree[j], 1)
                dve.drain()
                mt = mflat[:, bass.ds((2 * i + j) * TC, TC)]
                dve.tensor_tensor(mt, mt, tmp, ALU.add).then_inc(s_m, 1)
                lo(j)
                dve.drain()
        for n in range(KD):
            dve.wait_ge(s_uhi, count.due(s_uhi))
            dve.tensor_tensor(U[:, 1, n, :], M[:, n, :], U[:, 0, n, :].bitcast(F32), ALU.subtract).then_inc(s_mov, 1)
        dve.memset(sqsum, 0.0)
        count.skip(s_sq, KD + 2 * H)
        with count.loop(KD // 2, [(s_whi, 2), (s_sq, 2)]) as i:
            for j in range(2):
                dve.drain()
                dve.wait_ge(s_sq, count.due(s_sq))
                dve.tensor_tensor(sqsum, sqsum, sqb[:, j, :], ALU.add).then_inc(s_sqadd, 1)
                lo(j)
        dve.drain().then_inc(s_sqsum, 1)
        count.skip(s_unit, KD)
        dve.wait_ge(s_std, count.due(s_std))
        count.skip(s_full[0], 1)
        dve.reciprocal(nrs, nrs)
        dve.drain()
        for n in range(KD + 3):
            if n < KD:
                dve.scalar_tensor_tensor(out=M[:, n, :], in0=M[:, n, :], scalar=gpost[:, n:n + 1], in1=nrs,
                                         op0=ALU.mult, op1=ALU.mult).then_inc(s_mr, 1)
            if n >= 3:
                dve.wait_ge(s_uhi, count.due(s_uhi))
                dve.tensor_tensor(U[:, 1, n - 3, :], X[:, n - 3, :], U[:, 0, n - 3, :].bitcast(F32),
                                  ALU.subtract).then_inc(s_mov, 1)

        xflat = X.rearrange("p n c -> p (n c)")

        def ple(i, last):
            for j in range(2):
                dve.wait_ge(s_sgt, count.due(s_sgt))
                dve.wait_ge(s_ppin[j], count.due(s_ppin[j]))
                dve.tensor_tensor(etmp, sgt, pp_in[:, j, :], ALU.mult).then_inc(s_ppread, 1)
                dve.drain()
                dve.tensor_tensor(outT[:, j, :], etmp, xflat[:, bass.ds((2 * i + j) * TC, TC)], ALU.add).then_inc(s_out, 1)
                dve.drain()
                dve.tensor_copy(outS[:, bass.ds((2 * i + j) * NS, NS)], outT[:, j, T:TC])
                if not last:
                    lo(j)

        with count.loop(KD // 2 - 1, [(s_whi, 2), (s_sgt, 2), (s_ppin[0], 1), (s_ppin[1], 1)]) as i:
            ple(i, False)
        ple(KD // 2 - 1, True)
        dve.drain().then_inc(s_os, 1)

    @block.gpsimd
    def _(pool):
        count = Waits(pool)
        pool.sem_inc(s_begun, 1)
        for q in [*s_ppfree, *s_sgfree, *s_kfree, *s_vfree, s_yafree, s_stfree, s_ytfree, *s_ofree]:
            pool.sem_inc(q, 1)

        def store(dst, src, stored, free=None):
            pool.dma_start(dst, src).then_inc(stored, 16)
            pool.wait_ge(stored, count.due(stored))
            if free is not None:
                pool.sem_inc(free, 1)
        with nc.allow_non_contiguous_dma("small per-feature vectors"):
            pool.dma_start(small[:, 0:16], g_pre[0].rearrange("(n p) -> p n", p=P)).then_inc(s_const, 16)
            pool.dma_start(small[:, 16:32], g_post[0].rearrange("(n p) -> p n", p=P)).then_inc(s_const, 16)
            pool.dma_start(small[:, 32:48], g_ret[0].rearrange("(n p) -> p n", p=P)).then_inc(s_const, 16)
        pool.dma_start(small[:, 48:72], c_slope).then_inc(s_const, 16)
        pool.dma_start(small[:, 72:104], c_kdec).then_inc(s_const, 16)
        pool.wait_ge(s_xt, count.due(s_xt, skip=1))
        for n in range(KD):
            pool.dma_start(xt_scr[n], xT[:, n, :]).then_inc(s_xtst, 16)
        for n in range(KD):
            pool.wait_ge(s_pp, count.due(s_pp))
            store(pp_scr[n], pp_out[:, n % 2, :], s_ppst, s_ppfree[n % 2])
        pool.wait_ge(s_xtst, 16 * KD)
        pool.dma_start(dist, c_dist).then_inc(s_dist, 16)
        with count.loop(H, [(s_knat, 3), (s_vnat, 3), (s_ya, 1), (s_kst, 3), (s_vst, 3), (s_yast, 1)]) as h:
            for kv, (src, ready, stored, free) in enumerate(((k_nat, s_knat, s_kst, s_kfree), (v_nat, s_vnat, s_vst, s_vfree))):
                for g in range(G):
                    pool.wait_ge(ready, count.due(ready))
                    pool.sem_inc(s_pool_waits, 1)
                    keep = min(WIN[g], T)
                    dst = winp[g][0, 0].rearrange("(t p) k h d -> p t k (h d)", p=P)[:, :, kv, bass.ds(h * HD, HD)]
                    store(dst, src[:, g, TB - keep // P:TB, :], stored, free[g])
            pool.wait_ge(s_ya, count.due(s_ya))
            store(y_scr[bass.ds(h, 1)].rearrange("o p c -> (o p) c"), ya_out, s_yast, s_yafree)
        pool.dma_start(decay.rearrange("p h c -> p (h c)"), c_decay).then_inc(s_decay, 16)
        with count.loop(H, [(s_st, 1), (s_yt, 2), (s_stst, 1), (s_ytst, 2)]) as h:
            pool.wait_ge(s_st, count.due(s_st))
            store(ret_p[0, 0, bass.ds(h, 1)].rearrange("o (j p) e -> p (o j) e", p=P), st, s_stst, s_stfree)
            for e in range(2):
                pool.wait_ge(s_yt, count.due(s_yt))
                store(y_scr[bass.ds(H + 2 * h + e, 1)].rearrange("o p c -> (o p) c"), yt[:, e, :], s_ytst,
                      s_ytfree if e == 1 else None)

        pool.dma_start(sbias[0:H], c_bias.rearrange("p (g c) -> p g c", g=G)).then_inc(s_sbias, 16)
        pool.wait_ge(s_rows, 1)
        pool.dma_start(row_scr.rearrange("n p c -> p n c"), rows[0:64]).then_inc(s_rowst, 16)
        pool.dma_start(vrow_scr, vrow).then_inc(s_rowst, 16)
        pool.wait_ge(s_rowst, 32)
        for kv in range(2):
            for g in range(G):
                pool.dma_start(wins[g][0, :, WIN[g] - 1, kv],
                               row_scr[(1 + kv) * G + g].rearrange("(h b) d -> b h d", b=NS)).then_inc(s_newrow, 16)

        def cached(i, kv, dst, done):
            for g in range(G):
                src = caches[g][0, bass.ds(i, 1), :, kv].rearrange("b (m o) h d -> m (b o) (h d)", o=DIL[g])[:, 0, :]
                pool.dma_start(dst[:, g, :], src).then_inc(done, 16)

        def gate_store(i, j):
            pool.wait_ge(s_sg, count.due(s_sg))
            pool.sem_inc(s_pool_waits, 1)
            store(sg_scr[j % 2, bass.ds(2 * i + j // 2, 1)].rearrange("o p c -> (o p) c"),
                  sg_out[:, j % 2, :], s_sgst, s_sgfree[j % 2])

        def states_in(i, half):
            pool.wait_ge(s_rhalf, count.due(s_rhalf))
            pool.sem_inc(s_pool_waits, 1)
            pool.dma_start(r_st[:, half].rearrange("p h j e -> p (h j) e"),
                           state[0, bass.ds(i, 1), half * HH:(half + 1) * HH].rearrange("b h (j p) e -> p (b h j) e", p=P)
                           ).then_inc(s_rst[half], 16)
            v_src = vrow_scr.rearrange("(t b) c -> b t c", b=NS)[bass.ds(i, 1), half * H:(half + 1) * H]
            pool.dma_start(r_v[:, half].rearrange("p h (e c) -> p (h e) c", e=2),
                           v_src.broadcast_to([P, H, P])).then_inc(s_rst[half], 16)

        def states_out(i, half):
            pool.wait_ge(s_rnew, count.due(s_rnew))
            pool.sem_inc(s_pool_waits, 1)
            pool.dma_start(ret_s[0, bass.ds(i, 1), half * HH:(half + 1) * HH].rearrange("b h (j p) e -> p (b h j) e", p=P),
                           r_st[:, half].rearrange("p h j e -> p (h j) e")).then_inc(s_rnewst[half], 16)

        with count.loop(H, [(s_skfree, 1), (s_svfree, 1), (s_rhalf, 2), (s_rnew, 2), (s_rnewst[0], 1), (s_rnewst[1], 1),
                            (s_sg, 4), (s_sgst, 4)]) as i:
            pool.wait_ge(s_skfree, count.due(s_skfree))
            pool.sem_inc(s_pool_waits, 1)
            cached(i, 0, s_k, s_sk)
            q_src = row_scr[0:G].rearrange("g (h b) d -> b (g h) d", b=NS)[bass.ds(i, 1)]
            pool.dma_start(s_q.rearrange("p g (h d) -> p (g h) d", h=H), q_src.broadcast_to([P, G * H, HD])).then_inc(s_sk, 16)
            states_in(i, 0)
            gate_store(i, 0)
            pool.wait_ge(s_svfree, count.due(s_svfree))
            pool.sem_inc(s_pool_waits, 1)
            cached(i, 1, s_v, s_sv)
            states_in(i, 1)
            gate_store(i, 1)
            states_out(i, 0)
            gate_store(i, 2)
            states_out(i, 1)
            gate_store(i, 3)
            for q in range(2):
                pool.wait_ge(s_rnewst[q], count.due(s_rnewst[q]))

        for q in range(2):
            count.starts[id(s_accfree[q])] = KD // 2 + (H * UNITS_GATE + H * UNITS_ATT + H * UNITS_RET) // 2

        def gate_loads(which, n, first):
            with count.loop(n, [(s_accfree[0], 1), (s_accfree[1], 1)], first=first) as i:
                for j in range(2):
                    pool.wait_ge(s_accfree[j], count.due(s_accfree[j]))
                    pool.dma_start(sg_in[:, j, :], sg_scr[which, bass.ds(2 * i + j, 1)].rearrange("o p c -> (o p) c")
                                   ).then_inc(s_sgin[j], 16)

        pool.wait_ge(s_svfree, NS + 1)
        for n in range(8, KD):
            pool.dma_start(y_in[:, n, 0:T], y_scr[H + n]).then_inc(s_yin[1], 16)
        gate_loads(0, 1, 0)
        pool.wait_ge(s_yinfree, 1)
        for n in range(8):
            pool.dma_start(y_in[:, n, 0:T], y_scr[H + n]).then_inc(s_yin[2], 16)
        gate_loads(0, KD // 2 - 1, 1)
        gate_loads(1, KD // 2, 0)
        pool.wait_ge(s_yinfree, 2)
        for n in range(KD):
            pool.dma_start(X[:, n, :], xt_scr[n]).then_inc(s_xin, 16)
        pool.wait_ge(s_xin, 16 * KD)
        for n in range(KD):
            pool.wait_ge(s_mr, count.due(s_mr))
            pool.tensor_tensor(X[:, n, :], X[:, n, :], M[:, n, :], ALU.add).then_inc(s_h, 1)
        pool.wait_ge(s_h, KD)

        for n in range(2):
            pool.dma_start(pp_in[:, n, :], pp_scr[n]).then_inc(s_ppin[n], 16)

        def rows_out(i, j):
            pool.wait_ge(s_onat, count.due(s_onat))
            pool.sem_inc(s_pool_waits, 1)
            dst = y_prompt[0].rearrange("(t p) c -> p t c", p=P)[:, :, bass.ds((2 * i + j) * P, P)]
            store(dst, onat[:, j, :].rearrange("p (t c) -> p t c", t=TB), s_ost, s_ofree[j])
        with count.loop(KD // 2 - 1, [(s_ppread, 2), (s_onat, 2), (s_ost, 2)]) as i:
            for j in range(2):
                pool.wait_ge(s_ppread, count.due(s_ppread))
                pool.sem_inc(s_pool_waits, 1)
                pool.dma_start(pp_in[:, j, :], pp_scr[bass.ds(2 * i + 2 + j, 1)].rearrange("o p c -> (o p) c")
                               ).then_inc(s_ppin[j], 16)
                rows_out(i, j)
        for j in range(2):
            rows_out(KD // 2 - 1, j)
        pool.wait_ge(s_osrow, 1)
        pool.dma_start(y_sample.rearrange("b o (q c) -> (b o) q c", q=4), osr[0:NS, :, 0:T]).then_inc(s_osst, 16)
        pool.wait_ge(s_newrow, 16 * 2 * G)
        pool.wait_ge(s_osst, 16)

    stack.close()


def constants():
    ident = np.eye(P, dtype=np.float32)
    q, x = np.arange(P)[:, None], np.arange(T)[None, :]
    d0 = q + P - x[:, :2 * P]
    d0 = np.where((d0 >= 0) & (d0 <= WIN[0]), d0, BIG)
    d12 = q + T - P - x
    tabs = [d0] + [np.where((d12 >= 0) & (d12 % dil == 0) & (d12 <= win), d12, BIG)
                   for dil, win in zip(DIL[1:], WIN[1:])]
    dist = np.concatenate(tabs, axis=1).astype(np.float32)
    slope = np.tile(-slopes()[None, :], (P, 1)).astype(np.float32)
    lg = log_decay()
    rel = x - q
    decay = np.concatenate([np.where(rel >= 0, np.exp(np.maximum(rel, 0) * lg[h]), 0.0) for h in range(H)], axis=1)
    j = np.arange(TB)[None, :] * P + np.arange(P)[:, None]
    kdec = np.concatenate([np.exp((T - 1 - j) * lg[h]) for h in range(H)], axis=1)
    bias = np.zeros((H, G, NK + 1))
    sl = slopes().reshape(G, H)
    for g in range(G):
        far = (NK - np.arange(NK + 1)) * DIL[g]
        bias[:, g] = -sl[g][:, None] * far[None, :]
    return {"c_ident": ident, "c_dist": dist, "c_slope": slope, "c_decay": decay.astype(np.float32),
            "c_kdec": kdec.astype(np.float32), "c_bias": bias.reshape(H, -1).astype(np.float32)}


_INS = ["x_prompt", "x_sample", "cache_win0", "cache_win1", "cache_win2", "state_ret", "p_prompt", "p_sample",
        "g_pre", "w_in", "g_ret", "w_a_out", "w_r_out", "w_o", "g_post", "w_ple_gate", "w_ple_proj"]
_OUTS = [(1, T, D), (NS, 1, D), (1, 1, 128, 2, H, HD), (1, 1, T, 2, H, HD), (1, 1, T, 2, H, HD),
         (1, 1, H, RK, RK), (1, NS, 128, 2, H, HD), (1, NS, 512, 2, H, HD), (1, NS, 2048, 2, H, HD),
         (1, NS, H, RK, RK)]


def declare(nc, inputs):
    arrays, args = {}, []
    for name, a in [(n, inputs[n]) for n in _INS] + list(constants().items()):
        a = np.ascontiguousarray(a)
        arrays[f"in_{name}"] = a
        args.append(nc.dram_tensor(f"in_{name}", a.shape, mybir.dt.from_np(a.dtype), kind="ExternalInput").ap())
    for i, shape in enumerate(_OUTS):
        args.append(nc.dram_tensor(f"out_{i}", shape, F32, kind="ExternalOutput").ap())
    build(nc, *args)
    return arrays


def kernel(**inputs):
    import concourse.bacc as bacc
    from concourse.bass_utils import run_bass_kernel_spmd

    nc = bacc.Bacc("TRN2", target_bir_lowering=False, num_devices=1)
    arrays = declare(nc, inputs)
    r = run_bass_kernel_spmd(nc, [arrays], core_ids=[0])
    return tuple(r.results[0][f"out_{i}"] for i in range(len(_OUTS)))
```

```python
from contextlib import contextmanager, ExitStack

import numpy as np

import concourse.bass as bass
from concourse import mybir
from concourse.alu_op_type import AluOpType as ALU

F32 = mybir.dt.float32
F32R = mybir.dt.float32r
ACT = mybir.ActivationFunctionType
AX = mybir.AxisListType

P = 128
D = 2048
KD = D // P
T = 512
TB = T // P
NS = 8
TC = T + NS
HC = TC // 2
H = 8
G = 3
HD = 128
DIL = (1, 4, 16)
WIN = (128, 512, 2048)
NK = 128
RK = 256
PLE = 256
EPS = 1e-6
QA, KA, VA, ZA = 0, 3072, 6144, 9216
QR, KR, VR, ZR = 10240, 12288, 14336, 16384
GA, GB = 18432, 20480
N_IN = 22528
ZT = GA // P
NYT = H + 2 * H
ROW = 2 * H * HD
BIG = 1e30


def slopes():
    n = G * H
    return 2.0 ** (-8.0 * (np.arange(n) + 1.0) / n)


def log_decay():
    return np.log1p(-(2.0 ** (-5.0 - np.arange(H))))


def score_width(b):
    w0 = P * min(b + 1, 2)
    return w0, w0 + 2 * P * (b + 1)


class Tally:

    def __init__(self, start=0, unit=1):
        self.base, self.unit, self.local, self.i, self.rate = start, unit, 0, None, 0

    def next(self, skip=0):
        self.local += 1 + skip
        n = self.base + self.local
        return self.unit * n if self.i is None else self.unit * (self.i * self.rate + n)

    def enter(self, i, rate, first):
        self.base, self.local, self.rate = self.base + self.local - first * rate, 0, rate
        self.i = i

    def leave(self, n, first, name):
        assert self.local == self.rate, (name, self.local, self.rate)
        self.base, self.local, self.i = self.base + (n + first) * self.rate, 0, None


def build(nc, x_prompt, x_sample, cache0, cache1, cache2, state, p_prompt, p_sample, g_pre, w_in, g_ret,
          w_a, w_r, w_o, g_post, w_gate, w_proj,
          c_ident, c_dist, c_slope, c_decay, c_kdec, c_bias,
          y_prompt, y_sample, win0p, win1p, win2p, ret_p, win0s, win1s, win2s, ret_s):
    stack = ExitStack()
    caches, winp, wins = (cache0, cache1, cache2), (win0p, win1p, win2p), (win0s, win1s, win2s)
    gamma = [float(np.float32(g)) for g in np.exp(log_decay())]

    def dram(name, shape):
        return nc.dram_tensor(name, shape, F32, kind="Internal").ap()

    xt_scr = dram("xt_scr", [KD, P, TC])
    sg_scr = dram("sg_scr", [2, KD, P, TC])
    y_scr = dram("y_scr", [NYT, P, T])
    pp_scr = dram("pp_scr", [KD, P, TC])
    row_scr = dram("row_scr", [9, 64, HD])
    vrow_scr = dram("vrow_scr", [P, P])

    def sem(name):
        return stack.enter_context(nc.semaphore(name))

    U = stack.enter_context(nc.sbuf_tensor("moving", [P, 2, KD + 2, TC], F32R))
    W = stack.enter_context(nc.sbuf_tensor("weights", [P, 2, 2, KD, P], F32R))
    raw = stack.enter_context(nc.sbuf_tensor("raw_weights", [P, 2, KD, P], F32))
    ident = stack.enter_context(nc.sbuf_tensor("ident", [P, P], F32))
    one = stack.enter_context(nc.sbuf_tensor("one", [P, P], F32))
    mean_rk = stack.enter_context(nc.sbuf_tensor("mean_rk", [P, P], F32))
    mean_d = stack.enter_context(nc.sbuf_tensor("mean_d", [P, P], F32))
    small = stack.enter_context(nc.sbuf_tensor("small", [P, 256], F32))
    zs = stack.enter_context(nc.sbuf_tensor("sampled", [P, ZT * NS], F32))
    POOL_F = (212863 - 107648 - 16384 - 4 * 512 - 1024 - 4608) // 64 * 16 - 16
    pool_f = stack.enter_context(nc.sbuf_tensor("stage_buffers", [P, POOL_F], F32))
    acc = stack.enter_context(nc.psum_tensor("acc", [P, 2, 2, 512], F32))
    aux = stack.enter_context(nc.psum_tensor("aux", [P, 4, 512], F32))

    gpre, gpost, gret = small[:, 0:16], small[:, 16:32], small[:, 32:48]
    nslope, kdec = small[:, 48:72], small[:, 72:104]
    negmax, den, rden = small[:, 104:108], small[:, 108:112], small[:, 112:116]
    selfs, eps = small[:, 116:119], small[:, 120:121]

    rdiag = zs[:, 0:(TB + 1) * P].rearrange("p (t c) -> p t c", t=TB + 1)

    def carve():
        at = [0]

        def take(*shape):
            n = int(np.prod(shape))
            a = pool_f[:, at[0]:at[0] + n]
            at[0] += n
            assert at[0] <= POOL_F, (at[0], POOL_F)
            if len(shape) == 1:
                return a
            names = "abcd"[:len(shape)]
            spec = f"p ({' '.join(names)}) -> p {' '.join(names)}"
            return a.rearrange(spec, **dict(zip(names, shape)))
        return take

    t = carve()
    x_nat, xs_nat = t(TB, D), t(D)
    p_nat, ps_nat = t(TB, PLE), t(PLE)
    xT = t(KD, TC)
    t = carve()
    rstd, utmp, pp_out = t(TC), t(4, TC), t(KD, TC)
    assert KD * TC + 5 * TC <= TB * D + D + TB * PLE + PLE
    t = carve()
    qT, kT, vT, silu_z = t(G, TC), t(G, TC), t(2, TC), t(1, TC)
    k_nat, v_nat = t(G, TB, P), t(G, TB, P)
    sc = [t(score_width(b)[1]) for b in range(TB)]
    PT = t(G, TB, T)
    ya_out = t(T)
    dist = t(256 + 512 + 512)
    t = carve()
    rq, rk, rv, rz = t(2, TC), t(2, TC), t(2, TC), t(2, TC)
    ks, vn = t(TB, RK), t(TB, RK)
    sm = [t(T - P * j) for j in range(TB)]
    rsq, rrs, yt, st = t(2, T), t(T), t(2, T), t(2, RK)
    decay = t(H, T)
    rows = t(9, HD)
    t = carve()
    HH = H // 2
    ysmp = t(NYT, NS)
    sg_out = t(2, TC)
    r_st, r_v = t(2, HH, 2, RK), t(2, HH, RK)
    ysr, ssq, srs, yg = t(2 * H, NS), t(2 * H, NS), t(64), t(2 * H, NS)
    scol, qk, pcol, oself, spv = t(G, H), t(G, H), t(G, H), t(H), t(G, H)
    t = carve()
    t(NYT, NS)
    t(KD, TC)
    s_k, s_q, s_v = t(G, H * HD), t(G, H * HD), t(G, H * HD)
    srow, sbias = t(G, NK + 1), t(G, NK + 1)
    vrow = s_v.rearrange("p g c -> p (g c)")[:, 0:HD]
    row_ms, row_r, row_n = small[:, 160:165], small[:, 168:173], small[:, 176:181]
    pdiag = small[0:H, 128:128 + G * H].rearrange("p (g h) -> p g h", g=G)
    t = carve()
    t(NYT, NS)
    M, X = t(KD, TC), t(KD, TC)
    sg_in, tmp = t(2, TC), t(TC)
    y_in = X
    sqb, sqsum, nrs = sg_in, tmp, sg_in[:, 0, :]
    outT = M[:, 0:2, :]
    outS, sgt, onat = M[:, 2, 0:KD * NS], M[:, 3, :], M[:, 4:6, 0:T]
    etmp, osr, pp_in = M[:, 6, :], M[:, 8:12, :], M[:, 12:14, :]

    def sems(name, n):
        return [sem(f"{name}{i}") for i in range(n)]
    s_begun = sem("program_begun")
    s_pool_waits = sem("pool_waits")
    s_ident = sem("identity_loaded")
    s_const = sem("consts_loaded")
    s_xload = sems("x_loaded", 6)
    s_wload = sems("weights_loaded", 2)
    s_whi = sem("weights_hi")
    s_wready = sem("weights_ready")
    s_unit = sem("unit_done")
    s_accfree = sems("acc_free", 2)
    s_full = sems("aux_full", 4)
    s_free = sems("aux_free", 4)
    s_xt = sem("xT_ready")
    s_sq = sem("squares_ready")
    s_rowsq = sem("row_sums_ready")
    s_diag = sem("rstd_diagonals_ready")
    s_std = sem("std_ready")
    s_u = sem("u_plain_ready")
    s_uhi = sem("moving_hi")
    s_mov = sem("moving_ready")
    s_xtst = sem("xT_stored")
    s_pp = sem("projected_input_ready")
    s_ppst = sem("projected_input_stored")
    s_ppin = sems("projected_input_loaded", 2)
    s_ppread = sem("projected_input_read")
    s_sg = sem("gate_ready")
    s_sgst = sem("gate_stored")
    s_sgfree = sems("gate_buffer_free", 2)
    s_zT = sem("head_tile_ready")
    s_z = sem("silu_z_ready")
    s_knat = sem("k_rows_ready")
    s_vnat = sem("v_rows_ready")
    s_kst = sem("k_rows_stored")
    s_vst = sem("v_rows_stored")
    s_kfree = sems("k_rows_free", 3)
    s_vfree = sems("v_rows_free", 3)
    s_max = sem("max_ready")
    s_exp = sem("exp_ready")
    s_prob = sem("probs_ready")
    s_ya = sem("y_tile_ready")
    s_yast = sem("y_tile_stored")
    s_yafree = sem("y_tile_free")
    s_dist = sem("dist_loaded")
    s_decay = sem("decay_loaded")
    s_ks = sem("scaled_k_ready")
    s_pt = sem("probs_turned")
    s_vn = sem("ret_v_rows_ready")
    s_sm = sem("decayed_scores_ready")
    s_rstd = sem("ret_std_ready")
    s_st = sem("state_ready")
    s_stst = sem("state_stored")
    s_stfree = sem("state_free")
    s_yt = sem("ret_y_ready")
    s_ytst = sem("ret_y_stored")
    s_ytfree = sem("ret_y_free")
    s_rows = sem("sample_rows_ready")
    s_rowst = sem("sample_rows_stored")
    s_newrow = sem("new_cache_rows_stored")
    s_sk = sem("sample_k_and_q_loaded")
    s_skfree = sem("sample_k_and_q_read")
    s_scol = sem("score_columns_ready")
    s_smax = sem("sample_max_ready")
    s_sexp = sem("sample_exp_ready")
    s_sprob = sem("sample_probs_ready")
    s_vprod = sem("weighted_v_ready")
    s_sv = sem("sample_v_loaded")
    s_svfree = sem("sample_v_read")
    s_rst = sems("sample_state_loaded", 2)
    s_rgam = sem("sample_state_scaled")
    s_rhalf = sem("half_states_read")
    s_rnew = sem("sample_state_new")
    s_rnewst = sems("sample_state_stored", 2)
    s_ssq = sem("sample_squares_ready")
    s_sstd = sem("sample_std_ready")
    s_ysmp = sem("sample_y_ready")
    s_sbias = sem("sample_bias_loaded")
    s_yin = [sem(f"y_in_{n}_loaded") for n in ("attention", "ret_8_to_15", "ret_0_to_7")]
    s_yinfree = sem("y_in_read")
    s_sgin = sems("gate_in_loaded", 2)
    s_xin = sem("x_in_loaded")
    s_m = sem("merged_ready")
    s_sqadd = sem("squares_added")
    s_sqsum = sem("square_sums_ready")
    s_mr = sem("normed_y_ready")
    s_h = sem("h_ready")
    s_sgt = sem("ple_gate_ready")
    s_out = sem("out_tile_ready")
    s_onat = sem("out_rows_ready")
    s_ost = sem("out_rows_stored")
    s_ofree = sems("out_rows_free", 2)
    s_os = sem("sample_out_ready")
    s_osrow = sem("sample_out_rows_ready")
    s_osst = sem("sample_out_stored")
    s_copy = sem("cache_rows_copied")

    BY16 = {id(s) for s in [s_const, s_dist, s_decay, s_xtst, s_yast, s_stst, s_ytst, s_rowst, s_xin,
                            s_sbias, s_sgst, s_kst, s_vst, s_ost, s_ppst, *s_ppin, *s_xload, *s_wload, s_sk, s_sv, *s_rst,
                            *s_rnewst, *s_yin, *s_sgin]}

    class Waits:

        def __init__(self, e, ahead=False):
            self.e, self.t, self.ahead, self.starts = e, {}, ahead, {}

        def tally(self, s):
            if id(s) not in self.t:
                self.t[id(s)] = (Tally(self.starts.get(id(s), 0), 16 if id(s) in BY16 else 1), s)
            return self.t[id(s)][0]

        def due(self, s, skip=0):
            v = self.tally(s).next(skip)
            return self.e.to_reg(v) if self.ahead and not isinstance(v, int) else v

        def address(self, v, top):
            return self.e.snap(self.e.to_reg(v), min_val=0, max_val=top)

        def skip(self, s, n=1):
            self.tally(s).local += n

        @contextmanager
        def loop(self, n, rates, first=0):
            for s, _ in rates:
                self.tally(s)
            with self.e.Fori(first, first + n) as i:
                for s, r in rates:
                    self.tally(s).enter(i, r, first)
                yield i
                for s, r in rates:
                    self.tally(s).leave(n, first, s)

    def cols(i, n=P):
        return bass.ds(i, n)

    def halves(a):
        return a.rearrange("p (s c) -> p s c", s=2)

    def w_cols(w, col):
        return w.rearrange("(k p) c -> p k c", p=P)[:, :, bass.ds(col, P)]

    UNITS_ATT, UNITS_RET, UNITS_GATE = 10, 8, 4

    def att_cols(h):
        return [base + g * 1024 + h * P for base in (QA, KA, VA) for g in range(G)] + [ZA + h * P]

    def ret_cols(h):
        return [base + h * RK + j * P for base in (QR, KR, VR, ZR) for j in range(2)]

    def gate_cols(i):
        return [base + i * 2 * P + j * P for j in range(2) for base in (GA, GB)]

    def keep_rows(e, g, b, c):
        rows_kept = WIN[g] - 1
        chunk = {0: 1, 1: 4, 2: 16}[g]
        n = rows_kept * ROW // chunk
        src = caches[g][0].rearrange("b r k h d -> (b r k h d)")
        dst = wins[g][0].rearrange("b r k h d -> (b r k h d)")
        at = b * (WIN[g] * ROW) + c * n
        inner = n // P
        e.dma_start(dst[bass.ds(at, n)].rearrange("(p m n) -> p m n", p=16, n=inner),
                    src[bass.ds(at + ROW, n)].rearrange("(p m n) -> p m n", p=16, n=inner)).then_inc(s_copy, 16)
    N_COPIES = NS * (16 + 4 + 1)

    PT_BATCHES = {0: [(0, 3, 0, 1)], 1: [(0, 2, 0, 2), (2, 3, 0, 2)],
                  2: [(0, 1, 1, 3), (1, 2, 0, 3), (2, 3, 0, 3)],
                  3: [(0, 1, 2, 4), (1, 2, 0, 4), (2, 3, 0, 4)]}
    BATCHES = [(b, *q) for b in range(TB) for q in PT_BATCHES[b]]

    def prob_col(b, g, kb):
        w0, w = score_width(b)
        if g == 0:
            return (kb - max(b - 1, 0)) * P
        return w0 + (g - 1) * P * (b + 1) + kb * P

    block = stack.enter_context(nc.Block())

    @block.sync
    def _(sp):
        count = Waits(sp, ahead=True)
        for tb in range(TB):
            sp.dma_start(x_nat[:, tb, :], x_prompt[0, tb * P:(tb + 1) * P, :]).then_inc(s_xload[tb], 16)
            if tb == 0:
                sp.dma_start(ident[:], c_ident).then_inc(s_ident, 16)
        sp.dma_start(xs_nat[0:NS, :], x_sample[:, 0, :]).then_inc(s_xload[4], 16)
        sp.dma_start(p_nat, p_prompt[0, 0].rearrange("(t p) c -> p t c", p=P)).then_inc(s_xload[5], 16)
        sp.dma_start(ps_nat[0:NS, :], p_sample[0, :, 0, :]).then_inc(s_xload[5], 16)

        def load(slot, w, col, k=KD):
            v, col = count.due(s_wready), count.address(col, w.shape[1] - P)
            sp.wait_ge(s_begun, 1)
            sp.wait_ge(s_wready, v)
            sp.dma_start(raw[:, slot, 0:k, :], w_cols(w, col)).then_inc(s_wload[slot], 16)

        w0 = w_in[0]
        for u in range(2):
            sp.wait_ge(s_wready, count.due(s_wready))
            for k in range(2):
                sp.dma_start(raw[:, u].rearrange("p (n k) c -> p k n c", k=2)[:, k],
                             w_proj[0][k * P:(k + 1) * P, u * 8 * P:(u + 1) * 8 * P].rearrange("p (n c) -> p n c", c=P)
                             ).then_inc(s_wload[u], 16)
        with count.loop(H, [(s_wready, UNITS_ATT)]) as h:
            for j, c in enumerate(att_cols(h)):
                load(j % 2, w0, c)
                keep_rows(sp, 2, h, j)
        with count.loop(H, [(s_wready, UNITS_RET)]) as h:
            for j, c in enumerate(ret_cols(h)):
                load(j % 2, w0, c)
                if j < 6:
                    keep_rows(sp, 2, h, 10 + j)
                else:
                    keep_rows(sp, 1, h, j - 4)
        with count.loop(H, [(s_wready, UNITS_GATE)]) as i:
            for j, c in enumerate(gate_cols(i)):
                load(j % 2, w0, c)
        sp.wait_ge(s_wready, count.due(s_wready))
        sp.dma_start(raw[:, 0, 0:H, :], w_cols(w_a[0], 0)).then_inc(s_wload[0], 16)
        sp.wait_ge(s_wready, count.due(s_wready))
        sp.dma_start(raw[:, 1, 0:H, :], w_cols(w_a[0], P)).then_inc(s_wload[1], 16)
        sp.wait_ge(s_skfree, 1 + NS)
        for n in range(H):
            sp.dma_start(y_in[:, n, 0:T], y_scr[n]).then_inc(s_yin[0], 16)
        with count.loop(KD // 2 - 1, [(s_wready, 2)], first=1) as i:
            for j in range(2):
                load(j, w_a[0], i * 2 * P + j * P, H)
        with count.loop(KD // 2, [(s_wready, 2)]) as i:
            for j in range(2):
                load(j, w_r[0], i * 2 * P + j * P)
                if j == 0:
                    keep_rows(sp, 1, i, 0)
        with count.loop(KD // 2, [(s_wready, 2)]) as i:
            for j in range(2):
                load(j, w_o[0], i * 2 * P + j * P)
                if j == 0:
                    keep_rows(sp, 1, i, 1)
        with count.loop(KD // 2, [(s_wready, 2)]) as i:
            for j in range(2):
                load(j, w_gate[0], i * 2 * P + j * P)
                if j == 0:
                    keep_rows(sp, 0, i, 0)
        sp.wait_ge(s_copy, 16 * N_COPIES)

    @block.tensor
    def _(pe):
        count = Waits(pe)
        count.starts[id(s_wready)] = 2
        halfcols = [(0, HC), (HC, TC)]

        def unit(par, ks=range(KD), hooks=None, tiles_due=None):
            pe.wait_ge(s_wready, count.due(s_wready))
            pe.wait_ge(s_accfree[par], count.due(s_accfree[par]))
            passes = [(0, 0), (0, 1), (1, 0)]
            for k in ks:
                for f in (hooks or {}).get(k, ()):
                    f()
                if tiles_due and k in tiles_due:
                    pe.wait_ge(s_mov, count.due(s_mov, skip=tiles_due[k] - 1))
                for n, (wp, up) in enumerate(passes):
                    for half, (a, b) in enumerate(halfcols):
                        mm = pe.matmul(acc[:, par, half, 0:HC], W[:, par, wp, k, :], U[:, up, k, a:b],
                                       start=(k == ks[0] and n == 0), stop=(k == ks[-1] and n == 2))
            mm.then_inc(s_unit, 1)

        def pair(tiles_due):
            for par in range(2):
                pe.wait_ge(s_wready, count.due(s_wready))
                pe.wait_ge(s_accfree[par], count.due(s_accfree[par]))
            for k in range(KD):
                pe.wait_ge(s_mov, count.due(s_mov, skip=tiles_due[k] - 1))
                for par in range(2):
                    for n, (wp, up) in enumerate([(0, 0), (0, 1), (1, 0)]):
                        for half, (a, b) in enumerate(halfcols):
                            mm = pe.matmul(acc[:, par, half, 0:HC], W[:, par, wp, k, :], U[:, up, k, a:b],
                                           start=(k == 0 and n == 0), stop=(k == KD - 1 and n == 2))
                    if k == KD - 1:
                        mm.then_inc(s_unit, 1)

        pe.wait_ge(s_ident, 16)
        fill = 0
        for tb in range(TB):
            pe.wait_ge(s_xload[tb], count.due(s_xload[tb]))
            for n0 in range(0, KD, 4):
                pe.wait_ge(s_free[fill % 4], count.due(s_free[fill % 4]))
                for n in range(4):
                    mm = pe.transpose(aux[:, fill % 4, n * P:(n + 1) * P],
                                      x_nat[:, tb, (n0 + n) * P:(n0 + n + 1) * P], ident[:])
                mm.then_inc(s_full[fill % 4], 1)
                fill += 1
        pe.wait_ge(s_xload[4], count.due(s_xload[4]))
        pe.wait_ge(s_free[0], count.due(s_free[0]))
        for n in range(KD):
            mm = pe.transpose(aux[:, 0, n * NS:(n + 1) * NS], xs_nat[0:NS, n * P:(n + 1) * P], ident[0:NS, 0:NS])
        mm.then_inc(s_full[0], 1)
        pe.wait_ge(s_xload[5], count.due(s_xload[5], skip=1))
        for j in range(2):
            pe.wait_ge(s_free[1 + j], count.due(s_free[1 + j]))
            for tb in range(TB):
                mm = pe.transpose(aux[:, 1 + j, tb * P:(tb + 1) * P], p_nat[:, tb, j * P:(j + 1) * P], ident[:])
            mm.then_inc(s_full[1 + j], 1)
        pe.wait_ge(s_free[3], count.due(s_free[3]))
        for j in range(2):
            mm = pe.transpose(aux[:, 3, j * NS:(j + 1) * NS], ps_nat[0:NS, j * P:(j + 1) * P], ident[0:NS, 0:NS])
        mm.then_inc(s_full[3], 1)

        pe.wait_ge(s_diag, 1)
        pe.wait_ge(s_free[0], count.due(s_free[0]))
        pe.wait_ge(s_free[1], count.due(s_free[1]))
        for tb in range(TB):
            pe.matmul(aux[:, 0, tb * P:(tb + 1) * P], one[:], rdiag[:, tb, :], start=True, stop=True)
        pe.matmul(aux[:, 1, 0:NS], one[0:NS, :], rdiag[0:NS, TB, 0:NS], start=True, stop=True).then_inc(s_full[0], 1)

        for n in range(KD):
            if n % 8 == 0:
                pe.wait_ge(s_wready, count.due(s_wready))
            pe.wait_ge(s_accfree[n % 2], count.due(s_accfree[n % 2]))
            for k in range(2):
                for m, (wp, up) in enumerate([(0, 0), (0, 1), (1, 0)]):
                    for half, (a, b) in enumerate(halfcols):
                        mm = pe.matmul(acc[:, n % 2, half, 0:HC], W[:, n // 8, wp, 2 * (n % 8) + k, :],
                                       U[:, up, KD + k, a:b], start=(k == 0 and m == 0), stop=(k == 1 and m == 2))
            mm.then_inc(s_unit, 1)
        def head_rows(src, nth_skip, bank, ntb=TB):
            pe.wait_ge(s_zT, count.due(s_zT, nth_skip))
            pe.wait_ge(s_free[bank], count.due(s_free[bank]))
            for tb in range(ntb):
                mm = pe.transpose(aux[:, bank, tb * P:(tb + 1) * P], src[:, tb * P:(tb + 1) * P], ident[:])
            mm.then_inc(s_full[bank], 1)

        def scores(b):
            w0, w = score_width(b)
            wg = P * (b + 1)
            q = slice(b * P, (b + 1) * P)
            for g, (a, n) in enumerate([(max(b - 1, 0) * P, w0), (0, wg), (0, wg)]):
                pe.wait_ge(s_free[g], count.due(s_free[g]))
                pe.matmul(aux[:, g, 0:n], qT[:, g, q], kT[:, g, a:a + n], start=True, stop=True).then_inc(s_full[g], 1)

        def prob_turn(m):
            b, g0, g1, k0, k1 = BATCHES[m]
            if m == 0 or BATCHES[m - 1][0] != b:
                pe.wait_ge(s_prob, count.due(s_prob))
            pe.wait_ge(s_free[m % 3], count.due(s_free[m % 3]))
            at = 0
            for g in range(g0, g1):
                for kb in range(k0, k1):
                    c = prob_col(b, g, kb)
                    mm = pe.transpose(aux[:, m % 3, at:at + P], sc[b][:, c:c + P], ident[:])
                    at += P
            mm.then_inc(s_full[m % 3], 1)

        def values():
            pe.wait_ge(s_vnat, count.due(s_vnat, skip=2))
            pe.wait_ge(s_pt, count.due(s_pt, skip=len(BATCHES) - 1))
            pe.wait_ge(s_free[3], count.due(s_free[3]))
            parts = [(1, kb) for kb in range(TB)] + [(2, kb) for kb in range(TB)] + [(0, kb) for kb in range(TB)]
            for n, (g, kb) in enumerate(parts):
                a, z = kb * P, (min(kb + 2, TB) * P if g == 0 else T)
                mm = pe.matmul(aux[:, 3, a:z], v_nat[:, g, kb, :], PT[:, g, kb, a:z], start=(n == 0),
                               stop=(n == len(parts) - 1))
            mm.then_inc(s_full[3], 1)

        def attention_head(first):
            hooks = {
                4: {8: [lambda: head_rows(kT[:, 0, :], 3, 3)]},
                5: {8: [lambda: head_rows(kT[:, 1, :], 0, 3)]},
                6: {2: [lambda: head_rows(kT[:, 2, :], 0, 3)], 4: [lambda: scores(0)], 8: [lambda: scores(1)],
                    12: [lambda: scores(2)]},
                7: {0: [lambda: scores(3)], 6: [lambda: head_rows(vT[:, 0, :], 0, 3)]},
                8: {2: [lambda: head_rows(vT[:, 1, :], 0, 3)], 6: [lambda: prob_turn(0)], 9: [lambda: prob_turn(1)],
                    12: [lambda: prob_turn(2)]},
                9: {0: [lambda: prob_turn(3)], 2: [lambda: head_rows(vT[:, 0, :], 0, 3)],
                    4: [lambda: prob_turn(4)], 6: [lambda: prob_turn(5)], 8: [lambda: prob_turn(6)],
                    10: [lambda: prob_turn(7)], 12: [lambda: prob_turn(8)], 15: [values]},
            }
            for j in range(UNITS_ATT):
                unit(j % 2, hooks=hooks.get(j), tiles_due={k: 1 for k in range(KD)} if first and j == 0 else None)

        attention_head(True)
        with count.loop(H - 1, [(s_wready, 10), (s_accfree[0], 5), (s_accfree[1], 5), (s_zT, 9), (s_free[0], 7),
                                (s_free[1], 7), (s_free[2], 7), (s_free[3], 7), (s_prob, 4), (s_vnat, 3), (s_pt, 9)],
                        first=1) as h:
            attention_head(False)

        for n in range(9):
            bank = n // 4
            if n % 4 == 0:
                pe.wait_ge(s_free[bank], count.due(s_free[bank]))
            mm = pe.transpose(aux[0:64, bank, (n % 4) * P:(n % 4 + 1) * P], zs[:, n * H * NS:(n + 1) * H * NS], ident[:])
            if n % 4 == 3 or n == 8:
                mm.then_inc(s_full[bank], 1)

        def ret_rows(src, j, nth_skip, bank):
            pe.wait_ge(s_zT, count.due(s_zT, nth_skip))
            pe.wait_ge(s_free[bank], count.due(s_free[bank]))
            for tb in range(TB):
                mm = pe.transpose(aux[:, bank, tb * P:(tb + 1) * P], src[:, j, tb * P:(tb + 1) * P], ident[:])
            mm.then_inc(s_full[bank], 1)

        def ret_scores(jb):
            bank = jb % 2
            pe.wait_ge(s_free[bank], count.due(s_free[bank]))
            for j in range(2):
                mm = pe.matmul(aux[:, bank, 0:T - jb * P], rk[:, j, jb * P:(jb + 1) * P], rq[:, j, jb * P:T],
                               start=(j == 0), stop=(j == 1))
            mm.then_inc(s_full[bank], 1)

        def ret_values(e):
            if e == 0:
                pe.wait_ge(s_sm, count.due(s_sm, skip=3))
                pe.wait_ge(s_vn, count.due(s_vn, skip=1))
            pe.wait_ge(s_free[2 + e], count.due(s_free[2 + e]))
            for jb in range(TB):
                mm = pe.matmul(aux[:, 2 + e, jb * P:T], vn[:, jb, e * P:(e + 1) * P], sm[jb], start=(jb == 0),
                               stop=(jb == TB - 1))
            mm.then_inc(s_full[2 + e], 1)

        def ret_state():
            pe.wait_ge(s_ks, count.due(s_ks, skip=1))
            pe.wait_ge(s_free[0], count.due(s_free[0]))
            for j in range(2):
                for jb in range(TB):
                    mm = pe.matmul(aux[:, 0, j * RK:(j + 1) * RK], ks[:, jb, j * P:(j + 1) * P], vn[:, jb, :],
                                   start=(jb == 0), stop=(jb == TB - 1))
            mm.then_inc(s_full[0], 1)

        def ret_norm():
            pe.wait_ge(s_sq, count.due(s_sq, skip=1))
            pe.wait_ge(s_free[1], count.due(s_free[1]))
            for e in range(2):
                mm = pe.matmul(aux[:, 1, :], mean_rk[:], rsq[:, e, :], start=(e == 0), stop=(e == 1))
            mm.then_inc(s_full[1], 1)

        with count.loop(H, [(s_wready, 8), (s_accfree[0], 4), (s_accfree[1], 4), (s_zT, 6), (s_free[0], 5),
                        (s_free[1], 5), (s_free[2], 1), (s_free[3], 1), (s_sm, 4), (s_vn, 2), (s_ks, 2),
                        (s_sq, 2)]) as h:
            hooks = {
                4: {4: [lambda: ret_rows(rk, 0, 2, 0)], 8: [lambda: ret_rows(rk, 1, 0, 1)]},
                5: {1: [lambda: ret_scores(0)], 5: [lambda: ret_scores(1)], 9: [lambda: ret_scores(2)],
                    13: [lambda: ret_scores(3)]},
                6: {2: [lambda: ret_rows(rv, 0, 0, 0)], 6: [lambda: ret_rows(rv, 1, 0, 1)]},
                7: {1: [lambda: ret_values(0)], 5: [lambda: ret_values(1)], 9: [ret_state], 13: [ret_norm]},
            }
            for j in range(UNITS_RET):
                unit(j % 2, hooks=hooks.get(j))

        def sample_rows():
            pe.wait_ge(s_free[3], count.due(s_free[3]))
            pe.transpose(aux[:, 3, 0:P], zs[:, VR // P * NS:(VR // P + 16) * NS], ident[:]).then_inc(s_full[3], 1)

        def sample_scores():
            pe.wait_ge(s_scol, count.due(s_scol))
            pe.wait_ge(s_free[0], count.due(s_free[0]))
            for g in range(G):
                at = g * (NK + 1)
                pe.transpose(aux[0:H, 0, at:at + NK], scol[:, g, :], ident[:])
                mm = pe.matmul(aux[0:H, 0, at + NK:at + NK + 1], qk[:, g, :], one[:, 0:1], start=True, stop=True)
            mm.then_inc(s_full[0], 1)

        def sample_probs():
            pe.wait_ge(s_sprob, count.due(s_sprob))
            pe.wait_ge(s_free[1], count.due(s_free[1]))
            for g in range(G):
                pe.matmul(aux[:, 1, (G + g) * H:(G + g + 1) * H], one[0:H, :], pdiag[:, g, :], start=True, stop=True)
                mm = pe.transpose(aux[:, 1, g * H:(g + 1) * H], srow[0:H, g, 0:NK], ident[0:H, 0:H])
            mm.then_inc(s_full[1], 1)

        def sample_values(h):
            if h == 0:
                pe.wait_ge(s_vprod, count.due(s_vprod))
                pe.wait_ge(s_free[2], count.due(s_free[2]))
            for a in (h, h + 1):
                mm = pe.matmul(aux[:, 2, a:a + 1], s_v[:, 0, a * HD:(a + 1) * HD], one[:, 0:1], start=True, stop=True)
            if h == H - 2:
                mm.then_inc(s_full[2], 1)

        def sample_states(half, h):
            if h == 0:
                pe.wait_ge(s_rnew, count.due(s_rnew))
                pe.wait_ge(s_free[3], count.due(s_free[3]))
            for e in range(2):
                mm = pe.matmul(aux[:, 3, 2 * h + e:2 * h + e + 1], r_v[:, half, h, e * P:(e + 1) * P],
                               one[:, 0:1], start=True, stop=True)
            if h == HH - 1:
                mm.then_inc(s_full[3], 1)

        values = [lambda h=h: sample_values(h) for h in range(0, H, 2)]
        low, high = ([lambda n=n, half=half: sample_states(half, n) for n in range(HH)] for half in range(2))

        def gates(first, last):
            hooks = {
                0: {9: [sample_rows]} if first else {**{3 + n: [values[n]] for n in range(4)},
                                                     **{9 + n: [high[n]] for n in range(4)}},
                2: {8: [sample_scores]},
                3: {5: [sample_probs], **{7 + n: [low[n]] for n in range(HH)},
                    15: values if last else []},
            }
            for j in range(UNITS_GATE):
                unit(j % 2, hooks=hooks.get(j))

        gates(True, False)
        with count.loop(H - 2, [(s_wready, 4), (s_accfree[0], 2), (s_accfree[1], 2), (s_scol, 1), (s_sprob, 1),
                                (s_vprod, 1), (s_rnew, 2), (s_free[0], 1), (s_free[1], 1), (s_free[2], 1),
                                (s_free[3], 2)], first=1) as i:
            gates(False, False)
        gates(False, True)

        rates = [(s_wready, 2), (s_accfree[0], 1), (s_accfree[1], 1)]

        def sample_norm():
            pe.wait_ge(s_ssq, count.due(s_ssq))
            pe.wait_ge(s_free[2], count.due(s_free[2]))
            for e in range(2):
                mm = pe.matmul(aux[:, 2, 0:64], mean_rk[:], ssq[:, :, :].rearrange("p (h e) b -> p e h b", e=2)[:, e],
                               start=(e == 0), stop=(e == 1))
            mm.then_inc(s_full[2], 1)

        att_ks = list(range(H))
        unit(0, att_ks, tiles_due={k: 1 for k in att_ks})
        unit(1, att_ks)
        unit(0, att_ks, hooks={4 + n: [high[n]] for n in range(HH)})
        unit(1, att_ks)
        unit(0, att_ks, hooks={3: [sample_norm]})
        unit(1, att_ks)
        with count.loop(KD // 2 - 3, rates, first=3) as i:
            for j in range(2):
                unit(j, att_ks)
        ret_ks = list(range(8, KD)) + list(range(8))
        unit(0, ret_ks, tiles_due={8: 8, **{k: 1 for k in range(8)}})
        unit(1, ret_ks)
        with count.loop(KD // 2 - 1, rates, first=1) as i:
            for j in range(2):
                unit(j, ret_ks)
        unit(0, tiles_due={k: 1 for k in range(KD)})
        unit(1)
        with count.loop(KD // 2 - 1, rates, first=1) as i:
            for j in range(2):
                unit(j)
        pe.wait_ge(s_sqsum, 1)
        pe.wait_ge(s_free[0], count.due(s_free[0]))
        pe.wait_ge(s_free[1], count.due(s_free[1]))
        pe.matmul(aux[:, 0, 0:HC], mean_d[:], sqsum[:, 0:HC], start=True, stop=True)
        pe.matmul(aux[:, 1, 0:HC], mean_d[:], sqsum[:, HC:TC], start=True, stop=True).then_inc(s_full[0], 1)

        def out_turn(slot):
            pe.wait_ge(s_out, count.due(s_out))
            pe.wait_ge(s_free[slot], count.due(s_free[slot]))
            for tb in range(TB):
                mm = pe.transpose(aux[:, slot, tb * P:(tb + 1) * P], outT[:, slot, tb * P:(tb + 1) * P], ident[:])
            mm.then_inc(s_full[slot], 1)

        pair([1] * KD)
        unit(0, hooks={4: [lambda: out_turn(0)], 10: [lambda: out_turn(1)]})
        unit(1, hooks={8: [lambda: out_turn(0)]})
        with count.loop(KD // 2 - 2, [*rates, (s_out, 2), (s_free[0], 1), (s_free[1], 1)], first=2) as i:
            for j in range(2):
                unit(j, hooks={8: [lambda: out_turn(1 - j)]})
        out_turn(1)
        pe.wait_ge(s_os, count.due(s_os))
        for n in range(KD):
            if n % 4 == 0:
                pe.wait_ge(s_free[n // 4], count.due(s_free[n // 4]))
            mm = pe.transpose(aux[0:NS, n // 4, (n % 4) * P:(n % 4 + 1) * P], outS[:, n * NS:(n + 1) * NS], ident[:])
            if n % 4 == 3:
                mm.then_inc(s_full[n // 4], 1)

    @block.scalar
    def _(act):
        count = Waits(act)

        def hi(par, k=KD, loads=1):
            act.wait_ge(s_wload[par], count.due(s_wload[par], skip=loads - 1))
            act.activation(W[:, par, 0, 0:k], raw[:, par, 0:k], ACT.Copy).then_inc(s_whi, 1)

        act.sem_inc(s_accfree[0], 1)
        act.sem_inc(s_accfree[1], 1)
        for b in range(4):
            act.sem_inc(s_free[b], 1)

        act.wait_ge(s_begun, 2)
        for tb in range(TB):
            act.wait_ge(s_xload[tb], 16)
            act.drain()
            act.activation(W[:, 1, 1].rearrange("p k c -> p (k c)"), x_nat[:, tb, :], ACT.Square,
                           accum_out=row_ms[:, tb:tb + 1])
            for q in range(4):
                if q % 2 == 0:
                    act.wait_ge(s_full[q], count.due(s_full[q]))
                    act.activation(xT[:, 4 * q:4 * q + 4, tb * P:(tb + 1) * P],
                                   aux[:, q, :].rearrange("p (n c) -> p n c", n=4), ACT.Copy).then_inc(s_free[q], 1)
                else:
                    count.skip(s_full[q])
        act.wait_ge(s_xload[4], 16)
        act.drain()
        act.activation(W[0:NS, 1, 1].rearrange("p k c -> p (k c)"), xs_nat[0:NS], ACT.Square,
                       accum_out=row_ms[0:NS, TB:TB + 1])
        act.drain()
        act.activation(row_r, row_ms, ACT.Sqrt, scale=1.0 / D, bias=eps[:, 0:1])
        act.drain().then_inc(s_rowsq, 1)
        act.wait_ge(s_full[0], count.due(s_full[0]))
        act.activation(xT[:, :, T:TC], aux[:, 0, 0:P].rearrange("p (n c) -> p n c", n=KD), ACT.Copy).then_inc(s_free[0], 1)
        for j in range(2):
            act.wait_ge(s_full[1 + j], count.due(s_full[1 + j]))
            act.activation(U[:, 0, KD + j, 0:T], aux[:, 1 + j, :], ACT.Copy).then_inc(s_uhi, 1)
        act.wait_ge(s_full[3], count.due(s_full[3]))
        act.activation(U[:, 0, KD:KD + 2, T:TC], aux[:, 3, 0:2 * NS].rearrange("p (n c) -> p n c", n=2),
                       ACT.Copy).then_inc(s_uhi, 1)
        act.drain().then_inc(s_xt, 1)
        hi(0, loads=2)

        def std(dst):
            act.wait_ge(s_full[0], count.due(s_full[0]))
            act.activation(dst[:, 0:HC], aux[:, 0, 0:HC], ACT.Sqrt, bias=eps[:, 0:1]).then_inc(s_free[0], 1)
            act.activation(dst[:, HC:TC], aux[:, 1, 0:HC], ACT.Sqrt, bias=eps[:, 0:1]).then_inc(s_free[1], 1)
            act.drain().then_inc(s_std, 1)

        act.wait_ge(s_xt, count.due(s_xt, skip=1))
        act.wait_ge(s_full[0], count.due(s_full[0]))
        act.activation(rstd[:, 0:T], aux[:, 0, :], ACT.Copy).then_inc(s_free[0], 1)
        act.activation(rstd[:, T:TC], aux[:, 1, 0:NS], ACT.Copy).then_inc(s_free[1], 1)
        act.drain().then_inc(s_std, 1)
        for n in range(KD):
            act.wait_ge(s_u, count.due(s_u))
            act.activation(U[:, 0, n, :], utmp[:, n % 4, :], ACT.Copy).then_inc(s_uhi, 1)
            act.wait_ge(s_unit, count.due(s_unit))
            act.activation(halves(pp_out[:, n, :]), acc[:, n % 2, :, 0:HC], ACT.Copy).then_inc(s_accfree[n % 2], 1)
            act.drain().then_inc(s_pp, 1)
            if n == 1:
                hi(1, loads=2)
            if n % 8 == 7:
                hi(n // 8)
        act.wait_ge(s_xtst, 16 * KD)
        act.wait_ge(s_ppst, 16 * 4)

        def head_tile(par, dst, tile, ready, func=ACT.Copy, scale=1.0):
            act.wait_ge(s_unit, count.due(s_unit))
            act.activation(halves(dst), acc[:, par, :, 0:HC], func, scale=scale).then_inc(ready, 1)
            act.activation(zs[:, bass.ds(tile * NS, NS)], acc[:, par, 1, HC - NS:HC], func,
                           scale=scale).then_inc(s_accfree[par], 1)

        def exps(b):
            act.wait_ge(s_max, count.due(s_max))
            act.activation(sc[b], sc[b], ACT.Exp, bias=negmax[:, b:b + 1], accum_out=den[:, b:b + 1]).then_inc(s_exp, 1)

        def prob_copy(m):
            b, g0, g1, k0, k1 = BATCHES[m]
            act.wait_ge(s_full[m % 3], count.due(s_full[m % 3]))
            ng, nk = g1 - g0, k1 - k0
            src = aux[:, m % 3, 0:ng * nk * P].rearrange("p (g k c) -> p g k c", g=ng, k=nk)
            act.activation(PT[:, g0:g1, k0:k1, b * P:(b + 1) * P], src, ACT.Copy).then_inc(s_free[m % 3], 1)
            act.drain().then_inc(s_pt, 1)

        with count.loop(H, [(s_unit, 10), (s_wload[0], 5), (s_wload[1], 5), (s_max, 4), (s_full[0], 7), (s_full[1], 7),
                        (s_full[2], 7), (s_full[3], 7)]) as h:
            for j in range(UNITS_ATT):
                par = j % 2
                if j == 6:
                    for b in range(3):
                        exps(b)
                if j == 7:
                    exps(3)
                    for g in range(G):
                        count.skip(s_full[g], 4)
                if j == 8:
                    for m in range(3):
                        prob_copy(m)
                if j == 9:
                    for m in range(3, 9):
                        prob_copy(m)
                    count.skip(s_full[3], 7)
                g = j % 3
                if j < 3:
                    head_tile(par, qT[:, g, :], QA // P + g * H + h, s_zT, scale=HD ** -0.5)
                elif j < 6:
                    head_tile(par, kT[:, g, :], KA // P + g * H + h, s_zT)
                elif j < 9:
                    head_tile(par, vT[:, g % 2, :], VA // P + g * H + h, s_zT)
                else:
                    head_tile(par, silu_z[:, 0, :], ZA // P + h, s_z, ACT.Silu)
                hi(par)

        for q in range(3):
            count.skip(s_full[q], 1)

        with count.loop(H, [(s_unit, 8), (s_wload[0], 4), (s_wload[1], 4), (s_full[0], 5), (s_full[1], 5),
                        (s_full[2], 1), (s_full[3], 1)]) as h:
            for j in range(UNITS_RET):
                par = j % 2
                if j == 7:
                    for e in range(2):
                        act.wait_ge(s_full[2 + e], count.due(s_full[2 + e]))
                        act.activation(rsq[:, e, :], aux[:, 2 + e, :], ACT.Square).then_inc(s_sq, 1)
                    count.skip(s_full[0], 5)
                    act.wait_ge(s_full[1], count.due(s_full[1], skip=4))
                    act.activation(rrs, aux[:, 1, :], ACT.Sqrt, bias=eps[:, 0:1]).then_inc(s_free[1], 1)
                    act.drain().then_inc(s_rstd, 1)
                dst = (rq, rk, rv, rz)[j // 2][:, par, :]
                tile = (QR, KR, VR, ZR)[j // 2] // P + 2 * h + par
                if j < 6:
                    head_tile(par, dst, tile, s_zT, scale=RK ** -0.5 if j // 2 == 1 else 1.0)
                else:
                    head_tile(par, dst, tile, s_z, ACT.Silu)
                hi(par)

        act.wait_ge(s_stfree, H + 1)
        act.wait_ge(s_ytfree, H + 1)
        count.skip(s_full[3], 1)

        def scaled_states(half):
            act.wait_ge(s_rst[half], count.due(s_rst[half], skip=1))
            for h in range(HH):
                a = act.activation(r_st[:, half, h], r_st[:, half, h], ACT.Copy, scale=gamma[half * HH + h])
            a.then_inc(s_rgam, 1)

        def gates(last):
            for j in range(UNITS_GATE):
                par = j % 2
                if j == 2:
                    scaled_states(0)
                    act.wait_ge(s_smax, count.due(s_smax))
                    act.activation(srow[0:H], srow[0:H], ACT.Exp, bias=negmax[0:H, 0:1],
                                   accum_out=den[0:H, 0:1]).then_inc(s_sexp, 1)
                if j == 3:
                    scaled_states(1)
                act.wait_ge(s_unit, count.due(s_unit))
                act.wait_ge(s_sgfree[par], count.due(s_sgfree[par]))
                act.activation(halves(sg_out[:, par, :]), acc[:, par, :, 0:HC], ACT.Sigmoid).then_inc(s_accfree[par], 1)
                act.drain().then_inc(s_sg, 1)
                if not (last and j == UNITS_GATE - 1):
                    hi(par)

        with count.loop(H - 1, [(s_unit, 4), (s_wload[0], 2), (s_wload[1], 2), (s_sgfree[0], 2), (s_sgfree[1], 2),
                                (s_smax, 1), (s_rst[0], 2), (s_rst[1], 2)]) as i:
            gates(False)
        gates(True)

        def y_tile(n):
            act.activation(U[:, 0, bass.ds(n, 1), 0:T], y_in[:, bass.ds(n, 1), 0:T], ACT.Copy).then_inc(s_uhi, 1)

        def sampled_tiles(first, at, n):
            act.activation(U[:, 0, at:at + n, T:TC], ysmp[:, first:first + n, :], ACT.Copy).then_inc(s_uhi, 1)

        proj_rates = [(s_unit, 2), (s_wload[0], 1), (s_wload[1], 1)]
        act.wait_ge(s_svfree, NS + 1)
        sampled_tiles(0, 0, H)
        act.wait_ge(s_yin[0], 16 * H)
        for n in range(H):
            y_tile(n)
            if n == 3:
                hi(1, H)
        for j in range(2):
            act.wait_ge(s_unit, count.due(s_unit))
            hi(j, H)
        act.wait_ge(s_yin[1], 16 * 8)
        y_tile(8)
        y_tile(9)
        for j in range(2):
            act.wait_ge(s_unit, count.due(s_unit))
            hi(j, H)
        count.skip(s_full[0], H)
        count.skip(s_full[1], H)
        act.wait_ge(s_full[2], count.due(s_full[2], skip=H))
        act.activation(srs, aux[:, 2, 0:64], ACT.Sqrt, bias=eps[:, 0:1]).then_inc(s_free[2], 1)
        count.skip(s_full[3], 2 * H)
        act.drain().then_inc(s_sstd, 1)
        with count.loop(KD // 2 - 3, proj_rates, first=2) as i:
            y_tile(8 + i)
            for j in range(2):
                act.wait_ge(s_unit, count.due(s_unit))
                hi(j, H)
        act.wait_ge(s_ysmp, count.due(s_ysmp))
        sampled_tiles(H + 8, 8, 8)
        y_tile(KD - 1)
        act.wait_ge(s_unit, count.due(s_unit))
        hi(0)
        act.wait_ge(s_unit, count.due(s_unit))
        sampled_tiles(H, 0, 8)
        act.wait_ge(s_yin[2], 16 * 8)
        for n in range(8):
            y_tile(n)
            if n == 3:
                hi(1)
        with count.loop(KD // 2 - 1, proj_rates) as i:
            for j in range(2):
                act.wait_ge(s_unit, count.due(s_unit))
                hi(j)
        act.wait_ge(s_unit, count.due(s_unit))
        hi(0)
        act.wait_ge(s_unit, count.due(s_unit))
        for n in range(KD):
            act.wait_ge(s_m, count.due(s_m))
            act.activation(U[:, 0, n, :], M[:, n, :], ACT.Copy).then_inc(s_uhi, 1)
            if n == 6:
                hi(1)
        mflat = M.rearrange("p n c -> p (n c)")
        with count.loop(KD // 2, [*proj_rates, (s_sqadd, 2)]) as i:
            for j in range(2):
                act.wait_ge(s_unit, count.due(s_unit))
                act.activation(halves(mflat[:, bass.ds((2 * i + j) * TC, TC)]), acc[:, j, :, 0:HC], ACT.Copy)
                act.wait_ge(s_sqadd, count.due(s_sqadd))
                act.activation(halves(sqb[:, j, :]), acc[:, j, :, 0:HC], ACT.Square).then_inc(s_accfree[j], 1)
                act.drain().then_inc(s_sq, 1)
                hi(j)
        act.wait_ge(s_sqsum, 1)
        act.activation(nrs[:, 0:1], eps, ACT.Sqrt)
        act.drain()
        std(nrs)
        for n in range(KD):
            act.wait_ge(s_h, count.due(s_h))
            act.activation(U[:, 0, n, :], X[:, n, :], ACT.Copy).then_inc(s_uhi, 1)

        def ple_out(slot):
            act.wait_ge(s_full[slot], count.due(s_full[slot]))
            act.wait_ge(s_ofree[slot], count.due(s_ofree[slot]))
            act.activation(onat[:, slot, :], aux[:, slot, :], ACT.Copy).then_inc(s_free[slot], 1)
            act.drain().then_inc(s_onat, 1)

        def ple(first, last):
            for j in range(2):
                if not (first and j == 0):
                    ple_out(1 - j)
                act.wait_ge(s_unit, count.due(s_unit))
                act.activation(halves(sgt), acc[:, j, :, 0:HC], ACT.Sigmoid).then_inc(s_accfree[j], 1)
                act.drain().then_inc(s_sgt, 1)
                if not last:
                    hi(j)

        ple(True, False)
        with count.loop(KD // 2 - 2, [*proj_rates, (s_full[0], 1), (s_full[1], 1), (s_ofree[0], 1), (s_ofree[1], 1)],
                        first=1) as i:
            ple(False, False)
        ple(False, True)
        ple_out(1)
        for q in range(4):
            act.wait_ge(s_full[q], count.due(s_full[q]))
            a = act.activation(osr[0:NS, q, 0:T], aux[0:NS, q, :], ACT.Copy)
        a.then_inc(s_osrow, 1)

    @block.vector
    def _(dve):
        count = Waits(dve)

        def lo(par, k=KD):
            dve.wait_ge(s_whi, count.due(s_whi))
            dve.tensor_tensor(W[:, par, 1, 0:k], raw[:, par, 0:k], W[:, par, 0, 0:k].bitcast(F32),
                              ALU.subtract).then_inc(s_wready, 1)

        dve.sem_inc(s_wready, 2)
        dve.sem_inc(s_skfree, 1)
        dve.sem_inc(s_svfree, 1)
        dve.sem_inc(s_rhalf, 2)
        dve.sem_inc(s_sqadd, 2)
        dve.memset(mean_rk[:], 1.0 / RK)
        dve.memset(one[:], 1.0)
        dve.memset(eps, EPS)
        dve.memset(mean_d[:], 1.0 / D)
        dve.memset(row_ms, 1.0)
        dve.wait_ge(s_begun, 1)
        dve.drain().then_inc(s_begun, 1)
        for tb in range(TB):
            for q in range(4):
                if q % 2 == 1:
                    dve.wait_ge(s_full[q], count.due(s_full[q]))
                    dve.tensor_copy(xT[:, 4 * q:4 * q + 4, tb * P:(tb + 1) * P],
                                    aux[:, q, :].rearrange("p (n c) -> p n c", n=4)).then_inc(s_free[q], 1)
                else:
                    count.skip(s_full[q])
        count.skip(s_full[0], 1)
        dve.wait_ge(s_rowsq, 1)
        dve.tensor_scalar(row_ms, row_ms, 1.0 / D, EPS, ALU.mult, ALU.add)
        dve.reciprocal(row_r, row_r)
        dve.drain()
        dve.tensor_tensor(row_n, row_r, row_r, ALU.mult)
        dve.drain()
        dve.tensor_tensor(row_n, row_n, row_ms, ALU.mult)
        dve.drain()
        dve.tensor_scalar(row_n, row_n, -0.5, 1.5, ALU.mult, ALU.add)
        dve.drain()
        dve.tensor_tensor(row_r, row_r, row_n, ALU.mult)
        dve.drain()
        dve.wait_ge(s_ident, 16)
        for tb in range(TB):
            dve.tensor_scalar(rdiag[:, tb, :], ident[:], row_r[:, tb:tb + 1], None, ALU.mult)
        dve.tensor_scalar(rdiag[0:NS, TB, 0:NS], ident[0:NS, 0:NS], row_r[0:NS, TB:TB + 1], None, ALU.mult)
        dve.drain().then_inc(s_diag, 1)
        for j in range(2):
            count.skip(s_full[1 + j], 1)
            dve.wait_ge(s_uhi, count.due(s_uhi))
            dve.tensor_tensor(U[:, 1, KD + j, 0:T], aux[:, 1 + j, :], U[:, 0, KD + j, 0:T].bitcast(F32),
                              ALU.subtract).then_inc(s_free[1 + j], 1)
        count.skip(s_full[3], 1)
        dve.wait_ge(s_uhi, count.due(s_uhi))
        dve.tensor_tensor(U[:, 1, KD:KD + 2, T:TC], aux[:, 3, 0:2 * NS].rearrange("p (n c) -> p n c", n=2),
                          U[:, 0, KD:KD + 2, T:TC].bitcast(F32), ALU.subtract).then_inc(s_free[3], 1)
        dve.drain().then_inc(s_xt, 1)
        lo(0)
        dve.wait_ge(s_std, count.due(s_std))
        count.skip(s_full[0], 1)
        dve.wait_ge(s_const, 5 * 16)
        for m in range(KD + 2):
            if 4 <= m < KD:
                dve.wait_ge(s_mov, count.due(s_mov))
            if m < KD:
                dve.scalar_tensor_tensor(out=utmp[:, m % 4, :], in0=xT[:, m, :], scalar=gpre[:, m:m + 1], in1=rstd,
                                         op0=ALU.mult, op1=ALU.mult).then_inc(s_u, 1)
            n = m - 2
            if n >= 0:
                dve.wait_ge(s_uhi, count.due(s_uhi))
                dve.wait_ge(s_u, count.due(s_u))
                dve.tensor_tensor(U[:, 1, n, :], utmp[:, n % 4, :], U[:, 0, n, :].bitcast(F32),
                                  ALU.subtract).then_inc(s_mov, 1)
                if n == 3:
                    lo(1)
                if n == 9:
                    lo(0)
        lo(1)
        count.skip(s_unit, KD)

        def rows_copy(dst, ready, free):
            dve.wait_ge(s_full[3], count.due(s_full[3]))
            dve.wait_ge(free, count.due(free))
            dve.tensor_copy(dst, aux[:, 3, :].rearrange("p (t c) -> p t c", t=TB)).then_inc(s_free[3], 1)
            dve.drain().then_inc(ready, 1)

        def masked(b, h):
            w0, w = score_width(b)
            wg = P * (b + 1)
            parts = [(0, w0, 256 - w0), (w0, wg, 256 + T - wg), (w0 + wg, wg, 256 + 2 * T - wg)]
            for g, (at, n, tab) in enumerate(parts):
                dve.wait_ge(s_full[g], count.due(s_full[g]))
                dve.scalar_tensor_tensor(out=sc[b][:, at:at + n], in0=dist[:, tab:tab + n],
                                         scalar=nslope[:, bass.ds(h + g * H, 1)], in1=aux[:, g, 0:n],
                                         op0=ALU.mult, op1=ALU.add).then_inc(s_free[g], 1)
            dve.drain()
            dve.reduce_max(negmax[:, b:b + 1], sc[b], AX.X)
            dve.drain()
            dve.tensor_scalar(negmax[:, b:b + 1], negmax[:, b:b + 1], -1.0, None, ALU.mult).then_inc(s_max, 1)

        def normed(b):
            dve.wait_ge(s_exp, count.due(s_exp))
            dve.reciprocal(rden[:, b:b + 1], den[:, b:b + 1])
            dve.drain()
            dve.tensor_scalar(sc[b], sc[b], rden[:, b:b + 1], None, ALU.mult).then_inc(s_prob, 1)

        dve.wait_ge(s_dist, count.due(s_dist))
        with count.loop(H, [(s_whi, 10), (s_full[0], 7), (s_full[1], 7), (s_full[2], 7), (s_full[3], 7), (s_exp, 4),
                        (s_kfree[0], 1), (s_kfree[1], 1), (s_kfree[2], 1), (s_vfree[0], 1), (s_vfree[1], 1), (s_vfree[2], 1),
                        (s_z, 1), (s_yafree, 1)]) as h:
            for j in range(UNITS_ATT):
                if j in (4, 5, 6):
                    rows_copy(k_nat[:, j - 4], s_knat, s_kfree[j - 4])
                if j == 6:
                    masked(0, h)
                    masked(1, h)
                    normed(0)
                    masked(2, h)
                    normed(1)
                if j == 7:
                    masked(3, h)
                    for g in range(G):
                        count.skip(s_full[g], 3)
                    normed(2)
                    rows_copy(v_nat[:, 0], s_vnat, s_vfree[0])
                    normed(3)
                if j == 8:
                    rows_copy(v_nat[:, 1], s_vnat, s_vfree[1])
                if j == 9:
                    rows_copy(v_nat[:, 2], s_vnat, s_vfree[2])
                lo(j % 2)
            dve.wait_ge(s_full[3], count.due(s_full[3]))
            dve.wait_ge(s_z, count.due(s_z))
            dve.wait_ge(s_yafree, count.due(s_yafree))
            dve.tensor_tensor(ya_out, aux[:, 3, :], silu_z[:, 0, 0:T], ALU.mult).then_inc(s_free[3], 1)
            dve.drain().then_inc(s_ya, 1)
        count.skip(s_unit, 10 * H)

        decayf = decay.rearrange("p h c -> p (h c)")

        def new_buffers():
            for g in range(G):
                dve.wait_ge(s_kfree[g], count.due(s_kfree[g]))
                dve.wait_ge(s_vfree[g], count.due(s_vfree[g]))
            dve.wait_ge(s_yafree, count.due(s_yafree))
            dve.wait_ge(s_decay, count.due(s_decay))
            for bank, n in ((0, 4), (1, 4), (2, 1)):
                dve.wait_ge(s_full[bank], count.due(s_full[bank]))
                dve.tensor_copy(rows[0:64, bank * 4:bank * 4 + n, :],
                                aux[0:64, bank, 0:n * P].rearrange("p (n c) -> p n c", n=n)).then_inc(s_free[bank], 1)
            dve.drain().then_inc(s_rows, 1)

        def retention_head(h, first):
            for j in range(UNITS_RET):
                if first and j == 4:
                    new_buffers()
                if j == 4:
                    for d in range(2):
                        dve.wait_ge(s_full[d], count.due(s_full[d]))
                        for tb in range(TB):
                            a = dve.tensor_scalar(ks[:, tb, d * P:(d + 1) * P], aux[:, d, tb * P:(tb + 1) * P],
                                                  kdec[:, bass.ds(h * TB + tb, 1)], None, ALU.mult)
                        a.then_inc(s_free[d], 1)
                        dve.drain().then_inc(s_ks, 1)
                if j == 5:
                    for jb in range(TB):
                        dve.wait_ge(s_full[jb % 2], count.due(s_full[jb % 2]))
                        dve.tensor_tensor(sm[jb], aux[:, jb % 2, 0:T - jb * P], decayf[:, bass.ds(h * T, T - jb * P)],
                                          ALU.mult).then_inc(s_free[jb % 2], 1)
                        dve.drain().then_inc(s_sm, 1)
                if j == 6:
                    for e in range(2):
                        dve.wait_ge(s_full[e], count.due(s_full[e]))
                        dve.tensor_copy(vn[:, :, e * P:(e + 1) * P],
                                        aux[:, e, :].rearrange("p (t c) -> p t c", t=TB)).then_inc(s_free[e], 1)
                        dve.drain().then_inc(s_vn, 1)
                if j == 7:
                    dve.wait_ge(s_full[0], count.due(s_full[0]))
                    dve.wait_ge(s_stfree, count.due(s_stfree))
                    dve.tensor_copy(st, aux[:, 0, :].rearrange("p (j c) -> p j c", j=2)).then_inc(s_free[0], 1)
                    dve.drain().then_inc(s_st, 1)
                lo(j % 2)
            dve.wait_ge(s_full[1], count.due(s_full[1]))
            dve.wait_ge(s_rstd, count.due(s_rstd))
            dve.wait_ge(s_z, count.due(s_z, skip=1))
            dve.wait_ge(s_ytfree, count.due(s_ytfree))
            dve.reciprocal(rrs, rrs)
            dve.drain()
            for e in range(2):
                dve.wait_ge(s_full[2 + e], count.due(s_full[2 + e]))
                dve.scalar_tensor_tensor(out=yt[:, e, :], in0=aux[:, 2 + e, :], scalar=gret[:, bass.ds(2 * h + e, 1)],
                                         in1=rrs, op0=ALU.mult, op1=ALU.mult).then_inc(s_free[2 + e], 1)
            dve.drain()
            for e in range(2):
                dve.tensor_tensor(yt[:, e, :], yt[:, e, :], rz[:, e, 0:T], ALU.mult).then_inc(s_yt, 1)

        retention_head(0, True)
        with count.loop(H - 1, [(s_whi, 8), (s_full[0], 5), (s_full[1], 5), (s_full[2], 1), (s_full[3], 1), (s_z, 2),
                                (s_rstd, 1), (s_stfree, 1), (s_ytfree, 1)], first=1) as h:
            retention_head(h, False)
        count.skip(s_unit, 8 * H)

        dve.wait_ge(s_stfree, count.due(s_stfree))
        dve.wait_ge(s_ytfree, count.due(s_ytfree))
        dve.wait_ge(s_full[3], count.due(s_full[3]))
        dve.tensor_copy(vrow, aux[:, 3, 0:P]).then_inc(s_free[3], 1)
        dve.drain().then_inc(s_rows, 1)
        zg = zs[:].rearrange("p (t b) -> p t b", b=NS)

        def flat(a):
            return a.rearrange("p g c -> p (g c)")

        def token(first, n, i):
            return zg[:, first:first + n, bass.ds(i, 1)]

        def column(a):
            return a.rearrange("p (t o) -> p t o", o=1)

        def sample_keys(i):
            dve.wait_ge(s_sk, count.due(s_sk, skip=G))
            dve.tensor_tensor(s_k, s_k, s_q, ALU.mult)
            dve.tensor_tensor(column(flat(qk)), token(0, G * H, i), token(KA // P, G * H, i), ALU.mult)
            dve.drain()
            dve.tensor_reduce(scol, s_k.rearrange("p g (h d) -> p g h d", h=H), AX.X, ALU.add).then_inc(s_skfree, 1)
            dve.drain().then_inc(s_scol, 1)

        def sample_softmax():
            dve.wait_ge(s_full[0], count.due(s_full[0]))
            dve.tensor_tensor(flat(srow)[0:H], aux[0:H, 0, 0:G * (NK + 1)], flat(sbias)[0:H], ALU.add).then_inc(s_free[0], 1)
            dve.drain()
            dve.reduce_max(negmax[0:H, 0:1], flat(srow)[0:H], AX.X)
            dve.drain()
            dve.tensor_scalar(negmax[0:H, 0:1], negmax[0:H, 0:1], -1.0, None, ALU.mult).then_inc(s_smax, 1)

        def sample_normed():
            dve.wait_ge(s_sexp, count.due(s_sexp))
            dve.reciprocal(rden[0:H, 0:1], den[0:H, 0:1])
            dve.drain()
            dve.tensor_scalar(srow[0:H], srow[0:H], rden[0:H, 0:1], None, ALU.mult)
            dve.drain()
            for g in range(G):
                dve.tensor_scalar(pdiag[:, g, :], ident[0:H, 0:H], srow[0:H, g, NK:NK + 1], None, ALU.mult)
            dve.drain().then_inc(s_sprob, 1)

        def sample_columns(i):
            dve.wait_ge(s_full[1], count.due(s_full[1]))
            dve.tensor_copy(flat(pcol), aux[:, 1, 0:G * H])
            dve.tensor_tensor(column(flat(spv)), column(aux[:, 1, G * H:2 * G * H]), token(VA // P, G * H, i),
                              ALU.mult).then_inc(s_free[1], 1)
            dve.drain()
            dve.wait_ge(s_sv, count.due(s_sv, skip=G - 1))
            heads = s_v.rearrange("p g (h d) -> p (g h) d", h=H)
            dve.tensor_tensor(heads, heads, column(flat(pcol)).broadcast_to([P, G * H, HD]), ALU.mult)
            dve.drain()
            dve.tensor_tensor(s_v[:, 0], s_v[:, 0], s_v[:, 1], ALU.add)
            dve.drain()
            dve.tensor_tensor(s_v[:, 0], s_v[:, 0], s_v[:, 2], ALU.add)
            dve.drain().then_inc(s_vprod, 1)
            dve.tensor_tensor(oself, spv[:, 0, :], spv[:, 1, :], ALU.add)
            dve.drain()
            dve.tensor_tensor(oself, oself, spv[:, 2, :], ALU.add)

        def sample_output(i):
            dve.drain()
            dve.wait_ge(s_full[2], count.due(s_full[2]))
            dve.tensor_tensor(oself, aux[:, 2, 0:H], oself, ALU.add).then_inc(s_free[2], 1)
            dve.drain()
            dve.tensor_tensor(ysmp[:, 0:H, bass.ds(i, 1)], column(oself), token(ZA // P, H, i), ALU.mult).then_inc(s_svfree, 1)

        def sample_states(half, i):
            dve.wait_ge(s_rgam, count.due(s_rgam))
            for h in range(HH):
                for j in range(2):
                    at = (KR // P + 2 * (half * HH + h) + j) * NS
                    dve.scalar_tensor_tensor(out=r_st[:, half, h, j, :], in0=r_v[:, half, h, :],
                                             scalar=zs[:, bass.ds(at + i, 1)],
                                             in1=r_st[:, half, h, j, :], op0=ALU.mult, op1=ALU.add)
            dve.drain()

        def sample_queries(half, i):
            for h in range(HH):
                at = (QR // P + 2 * (half * HH + h)) * NS
                dve.tensor_scalar(r_v[:, half, h, :], r_st[:, half, h, 0, :], zs[:, bass.ds(at + i, 1)], None, ALU.mult)
            dve.drain()
            for h in range(HH):
                at = (QR // P + 2 * (half * HH + h) + 1) * NS
                dve.scalar_tensor_tensor(out=r_v[:, half, h, :], in0=r_st[:, half, h, 1, :],
                                         scalar=zs[:, bass.ds(at + i, 1)], in1=r_v[:, half, h, :],
                                         op0=ALU.mult, op1=ALU.add)
            dve.drain().then_inc(s_rnew, 1)

        def sample_ret_y(half, i):
            dve.wait_ge(s_full[3], count.due(s_full[3]))
            dve.tensor_copy(ysr[:, half * H:(half + 1) * H, bass.ds(i, 1)], column(aux[:, 3, 0:H])).then_inc(s_free[3], 1)
            dve.drain().then_inc(s_rhalf, 1)

        def gates(i, first, last):
            for j in range(UNITS_GATE):
                if j == 1:
                    if not first:
                        sample_output(i - 1)
                        sample_ret_y(1, i - 1)
                    sample_keys(i)
                if j == 2:
                    sample_states(0, i)
                    sample_softmax()
                    sample_queries(0, i)
                    sample_normed()
                if j == 3:
                    sample_columns(i)
                    if last:
                        sample_output(i)
                    else:
                        sample_states(1, i)
                        sample_queries(1, i)
                    sample_ret_y(0, i)
                if not (last and j == UNITS_GATE - 1):
                    lo(j % 2)

        gates(0, True, False)
        with count.loop(H - 2, [(s_whi, 4), (s_sk, G + 1), (s_full[0], 1), (s_full[1], 1), (s_full[2], 1), (s_full[3], 2),
                                (s_sexp, 1), (s_rgam, 2), (s_sv, G)], first=1) as i:
            gates(i, False, False)
        gates(H - 1, False, True)
        dve.drain()
        count.skip(s_unit, 4 * H)

        def y_tile(n):
            dve.wait_ge(s_uhi, count.due(s_uhi))
            dve.tensor_tensor(U[:, 1, bass.ds(n, 1), 0:T], y_in[:, bass.ds(n, 1), 0:T],
                              U[:, 0, bass.ds(n, 1), 0:T].bitcast(F32), ALU.subtract).then_inc(s_mov, 1)

        def sampled_tiles(first, at, n):
            dve.wait_ge(s_uhi, count.due(s_uhi))
            dve.tensor_tensor(U[:, 1, at:at + n, T:TC], ysmp[:, first:first + n, :],
                              U[:, 0, at:at + n, T:TC].bitcast(F32), ALU.subtract)

        mflat = M.rearrange("p n c -> p (n c)")
        proj_rates = [(s_unit, 2), (s_whi, 2), (s_sgin[0], 1), (s_sgin[1], 1)]

        def att_unit(i, j, k):
            dve.wait_ge(s_unit, count.due(s_unit))
            dve.wait_ge(s_sgin[j], count.due(s_sgin[j]))
            dve.tensor_tensor(halves(mflat[:, bass.ds((2 * i + j) * TC, TC)]), acc[:, j, :, 0:HC],
                              halves(sg_in[:, j, :]), ALU.mult).then_inc(s_accfree[j], 1)
            if k:
                lo(j, k)

        sampled_tiles(0, 0, H)
        for n in range(H):
            y_tile(n)
            if n == 3:
                lo(1, H)
        dve.drain().then_inc(s_yinfree, 1)
        att_unit(0, 0, H)
        sample_states(1, H - 1)
        att_unit(0, 1, H)
        sample_queries(1, H - 1)
        y_tile(8)
        y_tile(9)
        att_unit(1, 0, H)
        sample_ret_y(1, H - 1)
        dve.tensor_tensor(ssq, ysr, ysr, ALU.mult).then_inc(s_ssq, 1)
        att_unit(1, 1, H)
        dve.wait_ge(s_full[2], count.due(s_full[2]))
        dve.wait_ge(s_sstd, count.due(s_sstd))
        dve.reciprocal(srs, srs)
        for tile in range(2 * H):
            dve.tensor_scalar(yg[:, tile, :], zg[:, ZR // P + tile, :], gret[:, tile:tile + 1], None, ALU.mult)
        dve.drain()
        dve.tensor_tensor(yg, yg, ysr, ALU.mult)
        dve.drain()
        for e in range(2):
            dve.tensor_tensor(ysmp[:, H:NYT, :].rearrange("p (h e) b -> p e h b", e=2)[:, e],
                              yg.rearrange("p (h e) b -> p e h b", e=2)[:, e],
                              srs.rearrange("p (h b) -> p h b", b=NS), ALU.mult)
        dve.drain().then_inc(s_ysmp, 1)
        with count.loop(KD // 2 - 3, [*proj_rates, (s_uhi, 1)], first=2) as i:
            y_tile(8 + i)
            for j in range(2):
                att_unit(i, j, H)
        sampled_tiles(H + 8, 8, 8)
        y_tile(KD - 1)
        att_unit(KD // 2 - 1, 0, KD)
        att_unit(KD // 2 - 1, 1, 0)
        sampled_tiles(H, 0, 8)
        for n in range(8):
            y_tile(n)
            if n == 3:
                lo(1)
        dve.drain().then_inc(s_yinfree, 1)

        def ret_units(i, last):
            for j in range(2):
                dve.wait_ge(s_unit, count.due(s_unit))
                dve.wait_ge(s_sgin[j], count.due(s_sgin[j]))
                dve.tensor_tensor(halves(tmp), acc[:, j, :, 0:HC], halves(sg_in[:, j, :]),
                                  ALU.mult).then_inc(s_accfree[j], 1)
                dve.drain()
                mt = mflat[:, bass.ds((2 * i + j) * TC, TC)]
                dve.tensor_tensor(mt, mt, tmp, ALU.add).then_inc(s_m, 1)
                if not (last and j == 1):
                    lo(j)
                dve.drain()

        with count.loop(KD // 2 - 1, proj_rates) as i:
            ret_units(i, False)
        ret_units(KD // 2 - 1, True)
        for n in range(KD):
            dve.wait_ge(s_uhi, count.due(s_uhi))
            dve.tensor_tensor(U[:, 1, n, :], M[:, n, :], U[:, 0, n, :].bitcast(F32), ALU.subtract).then_inc(s_mov, 1)
            if n == 6:
                lo(1)
        dve.memset(sqsum, 0.0)
        count.skip(s_sq, 2 * H)

        def add_squares(last):
            for j in range(2):
                dve.drain()
                dve.wait_ge(s_sq, count.due(s_sq))
                dve.tensor_tensor(sqsum, sqsum, sqb[:, j, :], ALU.add).then_inc(s_sqadd, 1)
                if last and j == 1:
                    dve.drain().then_inc(s_sqsum, 1)
                lo(j)

        with count.loop(KD // 2 - 1, [(s_whi, 2), (s_sq, 2)]) as i:
            add_squares(False)
        add_squares(True)
        count.skip(s_unit, KD)
        dve.wait_ge(s_std, count.due(s_std))
        count.skip(s_full[0], 1)
        dve.reciprocal(nrs, nrs)
        dve.drain()
        for n in range(KD + 3):
            if n < KD:
                dve.scalar_tensor_tensor(out=M[:, n, :], in0=M[:, n, :], scalar=gpost[:, n:n + 1], in1=nrs,
                                         op0=ALU.mult, op1=ALU.mult).then_inc(s_mr, 1)
            if n >= 3:
                dve.wait_ge(s_uhi, count.due(s_uhi))
                dve.tensor_tensor(U[:, 1, n - 3, :], X[:, n - 3, :], U[:, 0, n - 3, :].bitcast(F32),
                                  ALU.subtract).then_inc(s_mov, 1)

        xflat = X.rearrange("p n c -> p (n c)")

        def ple(i, last):
            for j in range(2):
                dve.wait_ge(s_sgt, count.due(s_sgt))
                dve.wait_ge(s_ppin[j], count.due(s_ppin[j]))
                dve.tensor_tensor(etmp, sgt, pp_in[:, j, :], ALU.mult).then_inc(s_ppread, 1)
                dve.drain()
                dve.tensor_tensor(outT[:, j, :], etmp, xflat[:, bass.ds((2 * i + j) * TC, TC)], ALU.add).then_inc(s_out, 1)
                dve.drain()
                dve.tensor_copy(outS[:, bass.ds((2 * i + j) * NS, NS)], outT[:, j, T:TC])
                if not last:
                    lo(j)

        with count.loop(KD // 2 - 1, [(s_whi, 2), (s_sgt, 2), (s_ppin[0], 1), (s_ppin[1], 1)]) as i:
            ple(i, False)
        ple(KD // 2 - 1, True)
        dve.drain().then_inc(s_os, 1)

    @block.gpsimd
    def _(pool):
        count = Waits(pool)
        pool.sem_inc(s_begun, 1)
        for q in [*s_sgfree, *s_kfree, *s_vfree, s_yafree, s_stfree, s_ytfree, *s_ofree]:
            pool.sem_inc(q, 1)

        def store(dst, src, stored, free=None):
            pool.dma_start(dst, src).then_inc(stored, 16)
            pool.wait_ge(stored, count.due(stored))
            if free is not None:
                pool.sem_inc(free, 1)
        with nc.allow_non_contiguous_dma("small per-feature vectors"):
            pool.dma_start(small[:, 0:16], g_pre[0].rearrange("(n p) -> p n", p=P)).then_inc(s_const, 16)
            pool.dma_start(small[:, 16:32], g_post[0].rearrange("(n p) -> p n", p=P)).then_inc(s_const, 16)
            pool.dma_start(small[:, 32:48], g_ret[0].rearrange("(n p) -> p n", p=P)).then_inc(s_const, 16)
        pool.dma_start(small[:, 48:72], c_slope).then_inc(s_const, 16)
        pool.dma_start(small[:, 72:104], c_kdec).then_inc(s_const, 16)
        pool.wait_ge(s_xt, count.due(s_xt, skip=1))
        for n in range(KD):
            pool.dma_start(xt_scr[n], xT[:, n, :]).then_inc(s_xtst, 16)
        for n in range(0, KD, 4):
            pool.wait_ge(s_pp, count.due(s_pp, skip=3))
            pool.dma_start(pp_scr[n:n + 4].rearrange("n p c -> p n c"), pp_out[:, n:n + 4, :]).then_inc(s_ppst, 16)
        pool.wait_ge(s_ppst, 16 * 4)
        pool.wait_ge(s_xtst, 16 * KD)
        pool.dma_start(dist, c_dist).then_inc(s_dist, 16)
        with count.loop(H, [(s_knat, 3), (s_vnat, 3), (s_ya, 1), (s_kst, 3), (s_vst, 3), (s_yast, 1)]) as h:
            for kv, (src, ready, stored, free) in enumerate(((k_nat, s_knat, s_kst, s_kfree), (v_nat, s_vnat, s_vst, s_vfree))):
                for g in range(G):
                    pool.wait_ge(ready, count.due(ready))
                    pool.sem_inc(s_pool_waits, 1)
                    keep = min(WIN[g], T)
                    dst = winp[g][0, 0].rearrange("(t p) k h d -> p t k (h d)", p=P)[:, :, kv, bass.ds(h * HD, HD)]
                    store(dst, src[:, g, TB - keep // P:TB, :], stored, free[g])
            pool.wait_ge(s_ya, count.due(s_ya))
            store(y_scr[bass.ds(h, 1)].rearrange("o p c -> (o p) c"), ya_out, s_yast, s_yafree)
        pool.dma_start(decay.rearrange("p h c -> p (h c)"), c_decay).then_inc(s_decay, 16)
        pool.wait_ge(s_rows, 1)
        pool.dma_start(row_scr.rearrange("n p c -> p n c"), rows[0:64]).then_inc(s_rowst, 16)
        with count.loop(H, [(s_st, 1), (s_yt, 2), (s_stst, 1), (s_ytst, 2)]) as h:
            pool.wait_ge(s_st, count.due(s_st))
            store(ret_p[0, 0, bass.ds(h, 1)].rearrange("o (j p) e -> p (o j) e", p=P), st, s_stst, s_stfree)
            for e in range(2):
                pool.wait_ge(s_yt, count.due(s_yt))
                store(y_scr[bass.ds(H + 2 * h + e, 1)].rearrange("o p c -> (o p) c"), yt[:, e, :], s_ytst,
                      s_ytfree if e == 1 else None)

        pool.wait_ge(s_rowst, 16)
        pool.dma_start(sbias[0:H], c_bias.rearrange("p (g c) -> p g c", g=G)).then_inc(s_sbias, 16)

        def cached(i, kv, dst, done):
            for g in range(G):
                src = caches[g][0, bass.ds(i, 1), :, kv].rearrange("b (m o) h d -> m (b o) (h d)", o=DIL[g])[:, 0, :]
                pool.dma_start(dst[:, g, :], src).then_inc(done, 16)

        def gate_store(i, j):
            pool.wait_ge(s_sg, count.due(s_sg))
            pool.sem_inc(s_pool_waits, 1)
            store(sg_scr[j % 2, bass.ds(2 * i + j // 2, 1)].rearrange("o p c -> (o p) c"),
                  sg_out[:, j % 2, :], s_sgst, s_sgfree[j % 2])

        def states_in(i, half):
            pool.wait_ge(s_rhalf, count.due(s_rhalf))
            pool.sem_inc(s_pool_waits, 1)
            pool.dma_start(r_st[:, half].rearrange("p h j e -> p (h j) e"),
                           state[0, bass.ds(i, 1), half * HH:(half + 1) * HH].rearrange("b h (j p) e -> p (b h j) e", p=P)
                           ).then_inc(s_rst[half], 16)
            v_src = vrow_scr.rearrange("(t b) c -> b t c", b=NS)[bass.ds(i, 1), half * H:(half + 1) * H]
            pool.dma_start(r_v[:, half].rearrange("p h (e c) -> p (h e) c", e=2),
                           v_src.broadcast_to([P, H, P])).then_inc(s_rst[half], 16)

        def states_out(i, half):
            pool.wait_ge(s_rnew, count.due(s_rnew))
            pool.sem_inc(s_pool_waits, 1)
            pool.dma_start(ret_s[0, bass.ds(i, 1), half * HH:(half + 1) * HH].rearrange("b h (j p) e -> p (b h j) e", p=P),
                           r_st[:, half].rearrange("p h j e -> p (h j) e")).then_inc(s_rnewst[half], 16)

        def states_stored():
            for q in range(2):
                pool.wait_ge(s_rnewst[q], count.due(s_rnewst[q]))

        def keys_in(i):
            pool.wait_ge(s_skfree, count.due(s_skfree))
            pool.sem_inc(s_pool_waits, 1)
            cached(i, 0, s_k, s_sk)
            q_src = row_scr[0:G].rearrange("g (h b) d -> b (g h) d", b=NS)[bass.ds(i, 1)]
            pool.dma_start(s_q.rearrange("p g (h d) -> p (g h) d", h=H), q_src.broadcast_to([P, G * H, HD])).then_inc(s_sk, 16)

        def gates(i, first, last):
            if first:
                keys_in(0)
            if first:
                pool.wait_ge(s_rows, 2)
                pool.dma_start(vrow_scr, vrow).then_inc(s_rowst, 16)
                pool.wait_ge(s_rowst, 32)
            states_in(i, 0)
            gate_store(i, 0)
            pool.wait_ge(s_svfree, count.due(s_svfree))
            pool.sem_inc(s_pool_waits, 1)
            cached(i, 1, s_v, s_sv)
            states_in(i, 1)
            gate_store(i, 1)
            states_out(i, 0)
            if not last:
                keys_in(i + 1)
            gate_store(i, 2)
            if not last:
                states_out(i, 1)
            gate_store(i, 3)
            if not last:
                states_stored()

        gates(0, True, False)
        with count.loop(H - 2, [(s_skfree, 1), (s_svfree, 1), (s_rhalf, 2), (s_rnew, 2), (s_rnewst[0], 1), (s_rnewst[1], 1),
                                (s_sg, 4), (s_sgst, 4)], first=1) as i:
            gates(i, False, False)
        gates(H - 1, False, True)

        for q in range(2):
            count.starts[id(s_accfree[q])] = KD // 2 + (H * UNITS_GATE + H * UNITS_ATT + H * UNITS_RET) // 2

        def gate_loads(which, n, first):
            with count.loop(n, [(s_accfree[0], 1), (s_accfree[1], 1)], first=first) as i:
                for j in range(2):
                    pool.wait_ge(s_accfree[j], count.due(s_accfree[j]))
                    pool.dma_start(sg_in[:, j, :], sg_scr[which, bass.ds(2 * i + j, 1)].rearrange("o p c -> (o p) c")
                                   ).then_inc(s_sgin[j], 16)

        gate_loads(0, 1, 0)
        pool.wait_ge(s_svfree, NS + 1)
        for n in range(8, KD):
            pool.dma_start(y_in[:, n, 0:T], y_scr[H + n]).then_inc(s_yin[1], 16)
        states_out(H - 1, 1)
        states_stored()
        pool.wait_ge(s_yinfree, 1)
        for n in range(8):
            pool.dma_start(y_in[:, n, 0:T], y_scr[H + n]).then_inc(s_yin[2], 16)
        gate_loads(0, KD // 2 - 1, 1)
        for kv in range(2):
            for g in range(G):
                pool.dma_start(wins[g][0, :, WIN[g] - 1, kv],
                               row_scr[(1 + kv) * G + g].rearrange("(h b) d -> b h d", b=NS)).then_inc(s_newrow, 16)
        gate_loads(1, KD // 2, 0)
        pool.wait_ge(s_yinfree, 2)
        for n in range(KD):
            pool.dma_start(X[:, n, :], xt_scr[n]).then_inc(s_xin, 16)
        pool.wait_ge(s_xin, 16 * KD)
        for n in range(KD):
            pool.wait_ge(s_mr, count.due(s_mr))
            pool.tensor_tensor(X[:, n, :], X[:, n, :], M[:, n, :], ALU.add).then_inc(s_h, 1)
        pool.wait_ge(s_h, KD)

        for n in range(2):
            pool.dma_start(pp_in[:, n, :], pp_scr[n]).then_inc(s_ppin[n], 16)

        def rows_out(i, j):
            pool.wait_ge(s_onat, count.due(s_onat))
            pool.sem_inc(s_pool_waits, 1)
            dst = y_prompt[0].rearrange("(t p) c -> p t c", p=P)[:, :, bass.ds((2 * i + j) * P, P)]
            store(dst, onat[:, j, :].rearrange("p (t c) -> p t c", t=TB), s_ost, s_ofree[j])
        with count.loop(KD // 2 - 1, [(s_ppread, 2), (s_onat, 2), (s_ost, 2)]) as i:
            for j in range(2):
                pool.wait_ge(s_ppread, count.due(s_ppread))
                pool.sem_inc(s_pool_waits, 1)
                pool.dma_start(pp_in[:, j, :], pp_scr[bass.ds(2 * i + 2 + j, 1)].rearrange("o p c -> (o p) c")
                               ).then_inc(s_ppin[j], 16)
                rows_out(i, j)
        for j in range(2):
            rows_out(KD // 2 - 1, j)
        pool.wait_ge(s_osrow, 1)
        pool.dma_start(y_sample.rearrange("b o (q c) -> (b o) q c", q=4), osr[0:NS, :, 0:T]).then_inc(s_osst, 16)
        pool.wait_ge(s_newrow, 16 * 2 * G)
        pool.wait_ge(s_osst, 16)

    stack.close()


def constants():
    ident = np.eye(P, dtype=np.float32)
    q, x = np.arange(P)[:, None], np.arange(T)[None, :]
    d0 = q + P - x[:, :2 * P]
    d0 = np.where((d0 >= 0) & (d0 <= WIN[0]), d0, BIG)
    d12 = q + T - P - x
    tabs = [d0] + [np.where((d12 >= 0) & (d12 % dil == 0) & (d12 <= win), d12, BIG)
                   for dil, win in zip(DIL[1:], WIN[1:])]
    dist = np.concatenate(tabs, axis=1).astype(np.float32)
    slope = np.tile(-slopes()[None, :], (P, 1)).astype(np.float32)
    lg = log_decay()
    rel = x - q
    decay = np.concatenate([np.where(rel >= 0, np.exp(np.maximum(rel, 0) * lg[h]), 0.0) for h in range(H)], axis=1)
    j = np.arange(TB)[None, :] * P + np.arange(P)[:, None]
    kdec = np.concatenate([np.exp((T - 1 - j) * lg[h]) for h in range(H)], axis=1)
    bias = np.zeros((H, G, NK + 1))
    sl = slopes().reshape(G, H)
    for g in range(G):
        far = (NK - np.arange(NK + 1)) * DIL[g]
        bias[:, g] = -sl[g][:, None] * far[None, :]
    return {"c_ident": ident, "c_dist": dist, "c_slope": slope, "c_decay": decay.astype(np.float32),
            "c_kdec": kdec.astype(np.float32), "c_bias": bias.reshape(H, -1).astype(np.float32)}


_INS = ["x_prompt", "x_sample", "cache_win0", "cache_win1", "cache_win2", "state_ret", "p_prompt", "p_sample",
        "g_pre", "w_in", "g_ret", "w_a_out", "w_r_out", "w_o", "g_post", "w_ple_gate", "w_ple_proj"]
_OUTS = [(1, T, D), (NS, 1, D), (1, 1, 128, 2, H, HD), (1, 1, T, 2, H, HD), (1, 1, T, 2, H, HD),
         (1, 1, H, RK, RK), (1, NS, 128, 2, H, HD), (1, NS, 512, 2, H, HD), (1, NS, 2048, 2, H, HD),
         (1, NS, H, RK, RK)]


def declare(nc, inputs):
    arrays, args = {}, []
    for name, a in [(n, inputs[n]) for n in _INS] + list(constants().items()):
        a = np.ascontiguousarray(a)
        arrays[f"in_{name}"] = a
        args.append(nc.dram_tensor(f"in_{name}", a.shape, mybir.dt.from_np(a.dtype), kind="ExternalInput").ap())
    for i, shape in enumerate(_OUTS):
        args.append(nc.dram_tensor(f"out_{i}", shape, F32, kind="ExternalOutput").ap())
    build(nc, *args)
    return arrays


def kernel(**inputs):
    import concourse.bacc as bacc
    from concourse.bass_utils import run_bass_kernel_spmd

    nc = bacc.Bacc("TRN2", target_bir_lowering=False, num_devices=1)
    arrays = declare(nc, inputs)
    r = run_bass_kernel_spmd(nc, [arrays], core_ids=[0])
    return tuple(r.results[0][f"out_{i}"] for i in range(len(_OUTS)))
```
